# Optimizing a Trainium2 kernel written in Bass

```python
import math
import functools
import jax
import jax.numpy as jnp
from jax import lax
import numpy as np

D_MODEL = 1024
BATCH = 1
SEQ = 256
DEPTH = 2
DEC_BATCH = 8
DEC_SEQ = 4
PAST_LEN = 1024
PAGE_SIZE = 128

N_HEADS = 8
N_KV = 2
HEAD_DIM = 64
GROUP = N_HEADS // N_KV
CMP_LEN = 32
CMP_STRIDE = 16
SEL_BLOCK = 64
N_SEL = 16
WINDOW = 512
Q_BLOCK = 128
ROPE_THETA = 10000.0
SSM_HEADS = 8
SSM_HEAD_DIM = 64
SSM_INNER = SSM_HEADS * SSM_HEAD_DIM
SSM_GROUPS = 2
SSM_STATE = 64
SSM_CONV = 4
SSM_CONV_DIM = SSM_INNER + 2 * SSM_GROUPS * SSM_STATE
SSM_CHUNK = 128
SC_DIM = 512
SC_WIDTH = 3
N_BRANCH = 3
BRANCH_DIM = 512
D_FF = 2816
N_EXPERTS = 8
TOP_K = 2
D_FF_EXPERT = 3584
N_DENSE = (DEPTH + 1) // 2
N_MOE = DEPTH // 2
EPS = 1e-6
NEG_INF = -1e30
FORCED_SCORE = 1e4
Q_DIM = N_HEADS * HEAD_DIM
KV_DIM = N_KV * HEAD_DIM
SPLITS = (Q_DIM, 6 * KV_DIM, 3 * N_HEADS, SSM_INNER, SSM_CONV_DIM, SSM_HEADS, SC_DIM, SC_DIM, SC_DIM, N_BRANCH * D_MODEL)
IN_DIM = sum(SPLITS)

kernel_name = 'nsa_ssd_shortconv_gated_hybrid_step'

def rms_norm(x, w):
    xf = x.astype(jnp.float32)
    y = xf * lax.rsqrt(jnp.mean(xf * xf, axis=-1, keepdims=True) + EPS)
    return (y * w.astype(jnp.float32)).astype(x.dtype)

def rope(x, pos):
    half = HEAD_DIM // 2
    inv_freq = jnp.exp(-math.log(ROPE_THETA) * jnp.arange(half, dtype=jnp.float32) / half)
    ang = pos.astype(jnp.float32)[:, None] * inv_freq[None, :]
    shape = (1, pos.shape[0]) + (1,) * (x.ndim - 3) + (half,)
    cos = jnp.cos(ang).reshape(shape)
    sin = jnp.sin(ang).reshape(shape)
    xf = x.astype(jnp.float32)
    x1, x2 = xf[..., :half], xf[..., half:]
    return jnp.concatenate([x1 * cos - x2 * sin, x2 * cos + x1 * sin], axis=-1).astype(x.dtype)

def masked_softmax(s, mask):
    p = jax.nn.softmax(jnp.where(mask, s.astype(jnp.float32), NEG_INF), axis=-1)
    return jnp.where(mask, p, 0.0)

def causal_dwconv(x, buf, w, bias=None):
    width, t = w.shape[0], x.shape[1]
    xp = jnp.concatenate([buf.astype(x.dtype), x], axis=1)
    y = xp[:, 0:t] * w[0]
    for k in range(1, width):
        y = y + xp[:, k:k + t] * w[k]
    if bias is not None:
        y = y + bias
    return y, xp[:, t:]

def ssd_scan(x, dt, a, bm, cm, h0, chunk):
    bsz, t = x.shape[:2]
    nc = t // chunk

    def to_chunks(v):
        return jnp.moveaxis(v.reshape((bsz, nc, chunk) + v.shape[2:]), 1, 0)

    causal = jnp.tril(jnp.ones((chunk, chunk), dtype=bool))

    def step(h, inp):
        xc, dtc, bc, cc = inp
        acum = jnp.cumsum(dtc * a, axis=1)
        seg = acum[:, :, None, :] - acum[:, None, :, :]
        decay = jnp.exp(jnp.where(causal[None, :, :, None], seg, NEG_INF))
        xdt = xc * dtc[..., None]
        cb = jnp.einsum('bthn,bshn->btsh', cc, bc)
        y_diag = jnp.einsum('btsh,bshp->bthp', cb * decay, xdt)
        y_off = jnp.einsum('bthn,bhpn->bthp', cc, h) * jnp.exp(acum)[..., None]
        tail = jnp.exp(acum[:, -1:, :] - acum)
        h_new = h * jnp.exp(acum[:, -1])[:, :, None, None] + jnp.einsum('bshp,bshn->bhpn', xdt * tail[..., None], bc)
        return h_new, y_diag + y_off

    h_t, ys = lax.scan(step, h0, (to_chunks(x), to_chunks(dt), to_chunks(bm), to_chunks(cm)))
    return jnp.moveaxis(ys, 0, 1).reshape(x.shape), h_t

def nsa_attention(q, q_pos, rows, win, w_cmp):
    bsz, t = q.shape[:2]
    seq_len = rows.shape[1]
    n_blk = -(-seq_len // SEL_BLOCK)
    l_pad = n_blk * SEL_BLOCK
    rows = jnp.pad(rows, ((0, 0), (0, l_pad - seq_len), (0, 0), (0, 0), (0, 0)))
    w_halves = w_cmp.reshape(2, CMP_LEN // CMP_STRIDE, CMP_STRIDE, HEAD_DIM, HEAD_DIM)
    strides = rows.reshape(bsz, l_pad // CMP_STRIDE, CMP_STRIDE, 4, N_KV, HEAD_DIM)

    def compress(r, w):
        return jnp.einsum('bcjgd,jde->bcge', r[:, :-1], w[0]) + jnp.einsum('bcjgd,jde->bcge', r[:, 1:], w[1])

    k_cmp = compress(strides[:, :, :, 0], w_halves[0])
    v_cmp = compress(strides[:, :, :, 1], w_halves[1])
    n_cmp = k_cmp.shape[1]
    cmp_end = jnp.arange(n_cmp) * CMP_STRIDE + (CMP_LEN - 1)
    ratio = SEL_BLOCK // CMP_STRIDE
    sel = rows[:, :, 2:4].reshape(bsz, n_blk, SEL_BLOCK, 2, N_KV, HEAD_DIM).transpose(0, 3, 4, 1, 2, 5)
    k_sel = min(N_SEL, n_blk)
    blk = jnp.arange(n_blk)
    g_ix = jnp.arange(N_KV)[None, :, None]
    lw = win.shape[1]
    win_pad = jnp.pad(win, ((0, 0), (WINDOW, 0), (0, 0), (0, 0), (0, 0)))
    idx_w = jnp.arange(WINDOW + lw)
    wpos = q_pos[0] - (lw - t) - WINDOW + idx_w
    wreal = idx_w >= WINDOW
    qb = math.gcd(t, Q_BLOCK)
    n_qb = t // qb
    scale = HEAD_DIM ** -0.5

    def one_block(item):
        b, qi, qp, ws = item
        s_c = jnp.einsum('qgrd,cgd->qgrc', qi, k_cmp[b]) * scale
        p_c = masked_softmax(s_c, (cmp_end[None, :] <= qp[:, None])[:, None, None, :])
        o_c = jnp.einsum('qgrc,cgd->qgrd', p_c, v_cmp[b])
        imp = jnp.pad(p_c.sum(axis=2), ((0, 0), (0, 0), (0, n_blk * ratio - n_cmp)))
        imp = imp.reshape(qb, N_KV, n_blk, ratio).sum(-1)
        cur = qp[:, None] // SEL_BLOCK
        valid = blk[None, :] <= cur
        forced = (blk[None, :] == 0) | (blk[None, :] == cur) | (blk[None, :] == cur - 1)
        score = jnp.where(valid[:, None], jnp.where(forced[:, None], FORCED_SCORE, imp), -1.0)
        top_s, top_i = lax.top_k(score, k_sel)
        sel_b = sel[b]
        k_g = sel_b[0][g_ix, top_i]
        v_g = sel_b[1][g_ix, top_i]
        kpos = top_i[..., None] * SEL_BLOCK + jnp.arange(SEL_BLOCK)
        m_s = (top_s >= 0.0)[..., None] & (kpos <= qp[:, None, None, None])
        s_s = jnp.einsum('qgrd,qgksd->qgrks', qi, k_g).reshape(qb, N_KV, GROUP, k_sel * SEL_BLOCK) * scale
        p_s = masked_softmax(s_s, m_s.reshape(qb, N_KV, 1, k_sel * SEL_BLOCK))
        o_s = jnp.einsum('qgrm,qgmd->qgrd', p_s, v_g.reshape(qb, N_KV, k_sel * SEL_BLOCK, HEAD_DIM))
        wb = lax.dynamic_slice_in_dim(win_pad[b], ws, WINDOW + qb, axis=0)
        kp = lax.dynamic_slice_in_dim(wpos, ws, WINDOW + qb)
        kr = lax.dynamic_slice_in_dim(wreal, ws, WINDOW + qb)
        dpos = qp[:, None] - kp[None, :]
        m_w = kr[None, :] & (dpos >= 0) & (dpos < WINDOW)
        s_w = jnp.einsum('qgrd,kgd->qgrk', qi, wb[:, 0]) * scale
        p_w = masked_softmax(s_w, m_w[:, None, None, :])
        o_w = jnp.einsum('qgrk,kgd->qgrd', p_w, wb[:, 1])
        return jnp.stack([o_c, o_s, o_w], axis=1).astype(qi.dtype)

    b_idx = jnp.repeat(jnp.arange(bsz), n_qb)
    i_idx = jnp.tile(jnp.arange(n_qb), bsz)
    q_items = q.reshape(bsz * n_qb, qb, N_KV, GROUP, HEAD_DIM)
    qp_items = q_pos.reshape(n_qb, qb)[i_idx]
    ws_items = (lw - t) + i_idx * qb
    out = lax.map(one_block, (b_idx, q_items, qp_items, ws_items))
    return out.reshape(bsz, t, 3, N_HEADS, HEAD_DIM)

def token_mixers(h, pos, past_rows, win_buf, win_keep, ssm_h0, ssm_buf, sc_buf,
                 w_in, q_norm, k_norm, w_cmp, ssm_conv_w, ssm_conv_b, ssm_dt_bias,
                 ssm_a_log, ssm_d, ssm_norm, sc_conv_w, w_branch, w_out):
    bsz, t = h.shape[:2]
    offs = np.cumsum(SPLITS)[:-1].tolist()
    (q, kv6, nsa_g, ssm_z, ssm_xbc, ssm_dt, sc_b, sc_c, sc_h, merge_g) = jnp.split(h @ w_in, offs, axis=-1)

    q = rope(rms_norm(q.reshape(bsz, t, N_HEADS, HEAD_DIM), q_norm), pos)
    kv6 = kv6.reshape(bsz, t, 3, 2, N_KV, HEAD_DIM)
    keys = rope(rms_norm(kv6[:, :, :, 0], k_norm[:, None, :]), pos)
    kv = jnp.stack([keys, kv6[:, :, :, 1]], axis=3)
    new_rows = kv[:, :, :2].reshape(bsz, t, 4, N_KV, HEAD_DIM)
    rows = jnp.concatenate([past_rows, new_rows.astype(past_rows.dtype)], axis=1)
    win = jnp.concatenate([win_buf, kv[:, :, 2].astype(win_buf.dtype)], axis=1)
    o_br = nsa_attention(q.reshape(bsz, t, N_KV, GROUP, HEAD_DIM), pos, rows, win, w_cmp)
    g_nsa = jax.nn.sigmoid(nsa_g.reshape(bsz, t, N_HEADS, 3))
    o_nsa = jnp.einsum('bthk,btkhd->bthd', g_nsa, o_br).reshape(bsz, t, Q_DIM)
    new_win = win[:, win.shape[1] - win_keep:]

    xbc, new_ssm_buf = causal_dwconv(ssm_xbc, ssm_buf, ssm_conv_w, ssm_conv_b)
    xbc = jax.nn.silu(xbc)
    xs, bm, cm = jnp.split(xbc, [SSM_INNER, SSM_INNER + SSM_GROUPS * SSM_STATE], axis=-1)
    rep = SSM_HEADS // SSM_GROUPS
    xs = xs.reshape(bsz, t, SSM_HEADS, SSM_HEAD_DIM).astype(jnp.float32)
    bm = jnp.repeat(bm.reshape(bsz, t, SSM_GROUPS, SSM_STATE), rep, axis=2).astype(jnp.float32)
    cm = jnp.repeat(cm.reshape(bsz, t, SSM_GROUPS, SSM_STATE), rep, axis=2).astype(jnp.float32)
    dt = jax.nn.softplus(ssm_dt.astype(jnp.float32) + ssm_dt_bias.astype(jnp.float32))
    a = -jnp.exp(ssm_a_log.astype(jnp.float32))
    y_ssm, h_t = ssd_scan(xs, dt, a, bm, cm, ssm_h0.astype(jnp.float32), math.gcd(t, SSM_CHUNK))
    y_ssm = y_ssm + xs * ssm_d.astype(jnp.float32)[:, None]
    y_ssm = y_ssm.reshape(bsz, t, SSM_INNER) * jax.nn.silu(ssm_z.astype(jnp.float32))
    o_ssm = rms_norm(y_ssm, ssm_norm).astype(h.dtype)

    sc_out, new_sc_buf = causal_dwconv(sc_c * sc_h, sc_buf, sc_conv_w)
    o_sc = sc_b * sc_out

    o_all = jnp.stack([o_nsa, o_ssm, o_sc.astype(o_nsa.dtype)], axis=2)
    proj = jnp.einsum('btkc,kcd->btkd', o_all, w_branch)
    gate = jax.nn.sigmoid(merge_g.reshape(bsz, t, N_BRANCH, D_MODEL))
    y = jnp.einsum('btkd,btkd->btd', gate, proj) @ w_out
    return y, new_rows, new_win, h_t.astype(h.dtype), new_ssm_buf, new_sc_buf

def swiglu(h, w_gate, w_up, w_down):
    return (jax.nn.silu(h @ w_gate) * (h @ w_up)) @ w_down

def moe_swiglu(h, router, w_gate, w_up, w_down):
    logits = jnp.einsum('btd,de->bte', h, router).astype(jnp.float32)
    top_v, top_i = lax.top_k(logits, TOP_K)
    gate = jax.nn.softmax(top_v, axis=-1)
    combine = jnp.einsum('btk,btke->bte', gate, jax.nn.one_hot(top_i, N_EXPERTS, dtype=jnp.float32))
    out = jnp.zeros(h.shape, jnp.float32)
    for e in range(N_EXPERTS):
        he = jax.nn.silu(h @ w_gate[e]) * (h @ w_up[e])
        out = out + combine[..., e:e + 1] * (he @ w_down[e])
    return out.astype(h.dtype)

def setup_inputs(seed: int = 0) -> dict:
    key = jax.random.key(seed)
    ks = list(jax.random.split(key, 32))
    f32 = jnp.float32

    def nrm(k, shape, scale):
        return jax.random.normal(k, shape, f32) * scale

    n_pages = PAST_LEN // PAGE_SIZE
    n_used = DEC_BATCH * n_pages
    n_pool = n_used + n_used // 4
    win_buf = min(WINDOW, PAST_LEN)
    page_table = jax.random.permutation(ks[7], n_pool)[:n_used].reshape(DEC_BATCH, n_pages).astype(jnp.int32)
    dt0 = jnp.exp(jax.random.uniform(ks[15], (DEPTH, SSM_HEADS), f32, math.log(1e-3), math.log(1e-1)))
    return {
        'x_prompt': nrm(ks[0], (BATCH, SEQ, D_MODEL), 1.0),
        'x_sample': nrm(ks[1], (DEC_BATCH, DEC_SEQ, D_MODEL), 1.0),
        'cache_nsa_pages': nrm(ks[2], (DEPTH, n_pool, PAGE_SIZE, 4, N_KV, HEAD_DIM), 1.0),
        'cache_nsa_window': nrm(ks[3], (DEPTH, DEC_BATCH, win_buf, 2, N_KV, HEAD_DIM), 1.0),
        'state_ssm': nrm(ks[4], (DEPTH, DEC_BATCH, SSM_HEADS, SSM_HEAD_DIM, SSM_STATE), 0.1),
        'state_ssm_conv': nrm(ks[5], (DEPTH, DEC_BATCH, SSM_CONV - 1, SSM_CONV_DIM), 1.0),
        'state_shortconv': nrm(ks[6], (DEPTH, DEC_BATCH, SC_WIDTH - 1, SC_DIM), 1.0),
        'page_table': page_table,
        'norm_mix': 1.0 + nrm(ks[8], (DEPTH, D_MODEL), 0.02),
        'w_in': nrm(ks[9], (DEPTH, D_MODEL, IN_DIM), D_MODEL ** -0.5),
        'q_norm': 1.0 + nrm(ks[10], (DEPTH, HEAD_DIM), 0.02),
        'k_norm': 1.0 + nrm(ks[11], (DEPTH, 3, HEAD_DIM), 0.02),
        'w_cmp': nrm(ks[12], (DEPTH, 2, CMP_LEN, HEAD_DIM, HEAD_DIM), (CMP_LEN * HEAD_DIM) ** -0.5),
        'ssm_conv_w': nrm(ks[13], (DEPTH, SSM_CONV, SSM_CONV_DIM), SSM_CONV ** -0.5),
        'ssm_conv_b': nrm(ks[14], (DEPTH, SSM_CONV_DIM), 0.01),
        'ssm_dt_bias': dt0 + jnp.log(-jnp.expm1(-dt0)),
        'ssm_a_log': jnp.log(jax.random.uniform(ks[16], (DEPTH, SSM_HEADS), f32, 1.0, 16.0)),
        'ssm_d': 1.0 + nrm(ks[17], (DEPTH, SSM_HEADS), 0.02),
        'ssm_norm': 1.0 + nrm(ks[18], (DEPTH, SSM_INNER), 0.02),
        'sc_conv_w': nrm(ks[19], (DEPTH, SC_WIDTH, SC_DIM), SC_WIDTH ** -0.5),
        'w_branch': nrm(ks[20], (DEPTH, N_BRANCH, BRANCH_DIM, D_MODEL), BRANCH_DIM ** -0.5),
        'w_out': nrm(ks[21], (DEPTH, D_MODEL, D_MODEL), D_MODEL ** -0.5),
        'norm_ffn': 1.0 + nrm(ks[22], (DEPTH, D_MODEL), 0.02),
        'ffn_w_gate': nrm(ks[23], (N_DENSE, D_MODEL, D_FF), D_MODEL ** -0.5),
        'ffn_w_up': nrm(ks[24], (N_DENSE, D_MODEL, D_FF), D_MODEL ** -0.5),
        'ffn_w_down': nrm(ks[25], (N_DENSE, D_FF, D_MODEL), D_FF ** -0.5),
        'moe_router': nrm(ks[26], (N_MOE, D_MODEL, N_EXPERTS), D_MODEL ** -0.5),
        'moe_w_gate': nrm(ks[27], (N_MOE, N_EXPERTS, D_MODEL, D_FF_EXPERT), D_MODEL ** -0.5),
        'moe_w_up': nrm(ks[28], (N_MOE, N_EXPERTS, D_MODEL, D_FF_EXPERT), D_MODEL ** -0.5),
        'moe_w_down': nrm(ks[29], (N_MOE, N_EXPERTS, D_FF_EXPERT, D_MODEL), D_FF_EXPERT ** -0.5),
    }

def reference(x_prompt, x_sample, cache_nsa_pages, cache_nsa_window, state_ssm, state_ssm_conv,
              state_shortconv, page_table, norm_mix, w_in, q_norm, k_norm, w_cmp, ssm_conv_w,
              ssm_conv_b, ssm_dt_bias, ssm_a_log, ssm_d, ssm_norm, sc_conv_w, w_branch, w_out,
              norm_ffn, ffn_w_gate, ffn_w_up, ffn_w_down, moe_router, moe_w_gate, moe_w_up, moe_w_down):
    bp, tp = x_prompt.shape[:2]
    bd, td = x_sample.shape[:2]
    past_len = page_table.shape[1] * cache_nsa_pages.shape[2]
    pos_p = jnp.arange(tp, dtype=jnp.int32)
    pos_s = past_len + jnp.arange(td, dtype=jnp.int32)
    dtp = x_prompt.dtype
    zero_rows = jnp.zeros((bp, 0, 4, N_KV, HEAD_DIM), dtp)
    zero_win = jnp.zeros((bp, 0, 2, N_KV, HEAD_DIM), dtp)
    zero_ssm = jnp.zeros((bp, SSM_HEADS, SSM_HEAD_DIM, SSM_STATE), dtp)
    zero_ssm_conv = jnp.zeros((bp, SSM_CONV - 1, SSM_CONV_DIM), dtp)
    zero_sc = jnp.zeros((bp, SC_WIDTH - 1, SC_DIM), dtp)
    xp, xs = x_prompt, x_sample
    rows_p, rows_s, win_p, win_s, ssm_p, ssm_s = [], [], [], [], [], []
    sconv_p, sconv_s, cconv_p, cconv_s = [], [], [], []
    for l in range(DEPTH):
        mix = functools.partial(
            token_mixers, w_in=w_in[l], q_norm=q_norm[l], k_norm=k_norm[l], w_cmp=w_cmp[l],
            ssm_conv_w=ssm_conv_w[l], ssm_conv_b=ssm_conv_b[l], ssm_dt_bias=ssm_dt_bias[l],
            ssm_a_log=ssm_a_log[l], ssm_d=ssm_d[l], ssm_norm=ssm_norm[l], sc_conv_w=sc_conv_w[l],
            w_branch=w_branch[l], w_out=w_out[l])
        yp, r_p, w_p, h_p, b_p, c_p = mix(rms_norm(xp, norm_mix[l]), pos_p, zero_rows, zero_win,
                                          min(WINDOW, tp), zero_ssm, zero_ssm_conv, zero_sc)
        xp = xp + yp
        past = cache_nsa_pages[l, page_table].reshape(bd, past_len, 4, N_KV, HEAD_DIM)
        ys, r_s, w_s, h_s, b_s, c_s = mix(rms_norm(xs, norm_mix[l]), pos_s, past, cache_nsa_window[l],
                                          cache_nsa_window.shape[2], state_ssm[l], state_ssm_conv[l],
                                          state_shortconv[l])
        xs = xs + ys
        if l % 2 == 0:
            ffn = functools.partial(swiglu, w_gate=ffn_w_gate[l // 2], w_up=ffn_w_up[l // 2],
                                    w_down=ffn_w_down[l // 2])
        else:
            ffn = functools.partial(moe_swiglu, router=moe_router[l // 2], w_gate=moe_w_gate[l // 2],
                                    w_up=moe_w_up[l // 2], w_down=moe_w_down[l // 2])
        xp = xp + ffn(rms_norm(xp, norm_ffn[l]))
        xs = xs + ffn(rms_norm(xs, norm_ffn[l]))
        rows_p.append(r_p); rows_s.append(r_s); win_p.append(w_p); win_s.append(w_s)
        ssm_p.append(h_p); ssm_s.append(h_s); sconv_p.append(b_p); sconv_s.append(b_s)
        cconv_p.append(c_p); cconv_s.append(c_s)
    y_prompt, y_sample = xp, xs
    nsa_rows_prompt, nsa_rows_sample = jnp.stack(rows_p), jnp.stack(rows_s)
    nsa_window_prompt, nsa_window_sample = jnp.stack(win_p), jnp.stack(win_s)
    ssm_prompt, ssm_sample = jnp.stack(ssm_p), jnp.stack(ssm_s)
    ssm_conv_prompt, ssm_conv_sample = jnp.stack(sconv_p), jnp.stack(sconv_s)
    shortconv_prompt, shortconv_sample = jnp.stack(cconv_p), jnp.stack(cconv_s)
    return (y_prompt, y_sample, nsa_rows_prompt, nsa_rows_sample, nsa_window_prompt, nsa_window_sample,
            ssm_prompt, ssm_sample, ssm_conv_prompt, ssm_conv_sample, shortconv_prompt, shortconv_sample)


_drawn_inputs = setup_inputs


def setup_inputs(seed=0):
    import zlib

    import numpy as np

    out = dict(_drawn_inputs(seed))
    spreads = {}
    factors = {'q_norm': 3.85, 'k_norm': 3.833, 'ssm_conv_b': 3.184, 'ssm_d': 4.624, 'ssm_norm': 2.816}
    for name, (base, spread) in spreads.items():
        noise = np.random.default_rng([zlib.crc32(name.encode()), seed]).standard_normal(out[name].shape)
        drawn = base * np.exp(spread * noise) if base else spread * noise
        out[name] = jnp.asarray(drawn.astype(out[name].dtype))
    for name, factor in factors.items():
        out[name] = (out[name] * factor).astype(out[name].dtype)
    return out
```

```python
import math
from contextlib import ExitStack

import numpy as np
import concourse.bass as bass
from concourse import mybir

D, DEPTH = 1024, 2
TP, NB, TD = 256, 8, 4
TS = NB * TD
T = TP + TS
PAST, PAGE, WIN = 1024, 128, 512
NPG = PAST // PAGE
NH, NKV, HD, GRP = 8, 2, 64, 4
STRIDE, NCS, NCP = 16, 63, 15
SEL, NMID = 64, 14
SSMI, SSMN, XBC, SC = 512, 64, 768, 512
FF, FE, NE = 2816, 3584, 8
EPS, NEG = 1e-6, -1e30
P = 128
KD = D // P
HALF = NB // 2

BPS = 16
RING = 6
MARKS = 32
SLOTF = BPS * P
NQKV, NREST = 10, 22
NCMPB = 64
MIX_BLOCKS = NQKV * KD + 2 * NCMPB + NREST * KD + 3 * KD * KD + 12 * KD + KD * KD
NFD, NFE = FF // P, FE // P
FFN_BLOCKS = NFD * 3 * KD
EXP_BLOCKS = NFE * 3 * KD
PRE_SLOTS = (2 * MIX_BLOCKS + FFN_BLOCKS) // BPS
EXP_SLOTS = EXP_BLOCKS // BPS
N_SLOTS = PRE_SLOTS + NE * EXP_SLOTS
assert (MIX_BLOCKS % BPS, FFN_BLOCKS % BPS, EXP_BLOCKS % BPS, EXP_SLOTS % RING) == (0, 0, 0, 0)

TILES = [(0, 128), (128, 128), (256, 32)]
NCHUNK = 3


def constants():
    c = {}
    eye = np.eye(P, dtype=np.float32)
    i = np.arange(P)
    c["ident"] = eye
    c["ones"] = np.ones((P, P), np.float32)
    c["head_ones"] = (i[:, None] // HD == i[None, :] // HD).astype(np.float32)
    rot = np.zeros((P, P), np.float32)
    for m in range(P):
        if m % HD < HD // 2:
            rot[m + HD // 2, m] = -1.0
        else:
            rot[m - HD // 2, m] = 1.0
    c["rot"] = rot
    row_b, row_g, row_r, row_t = i // 32, i // 16 % 2, i // 4 % 4, i % 4
    grp = row_b * 8 + row_g * 4 + row_t
    c["group_sum"] = (grp[:, None] == grp[None, :]).astype(np.float32)
    half = HD // 2
    inv = np.exp(np.float32(-math.log(10000.0)) * np.arange(half, dtype=np.float32) / np.float32(half)).astype(np.float32)
    pos = np.concatenate([np.arange(TP), PAST + np.tile(np.arange(TD), NB)]).astype(np.float32)
    ang = (pos[None, :] * inv[i % half][:, None]).astype(np.float32)
    c["cos"], c["sin"] = np.cos(ang).astype(np.float32), np.sin(ang).astype(np.float32)
    c["causal0"] = np.where(i[None, :] <= i[:, None], 0, NEG).astype(np.float32)
    c["causal1"] = np.where(np.arange(TP)[None, :] <= i[:, None] + P, 0, NEG).astype(np.float32)
    end = np.arange(NCP) * STRIDE + 31
    qp = i[:, None] + P * np.arange(2)[None, :]
    vis = end[None, None, :] <= qp[:, :, None]
    c["cmp_mask"] = np.where(vis, 0, NEG).astype(np.float32).reshape(P, -1)
    c["cmp_any"] = vis.any(-1).astype(np.float32)
    tb, tt = np.arange(TS) // TD, np.arange(TS) % TD
    new = [np.where((tb[None, :] == (row_b + HALF * h)[:, None]) & (tt[None, :] <= row_t[:, None]), 0, NEG) for h in range(2)]
    c["new_mask"] = np.concatenate(new, 1).astype(np.float32)
    c["win_mask"] = np.where(np.arange(TD)[None, :] > row_t[:, None], 0, NEG).astype(np.float32)
    c["blk_idx"] = np.broadcast_to(np.arange(1, NMID + 1, dtype=np.float32), (P, NMID))
    c["upto0"] = (i[:, None] <= i[None, :]).astype(np.float32)
    c["decay_mask0"] = ((1 - c["upto0"]) * NEG).astype(np.float32)
    same = tb[:, None] == tb[None, :]
    up = np.zeros((P, TS), np.float32)
    up[:TS] = same & (tt[:, None] <= tt[None, :])
    c["upto2"] = up
    c["decay_mask2"] = ((1 - up) * NEG).astype(np.float32)
    sb = np.zeros((P, TS), np.float32)
    sb[:TS] = same
    c["same2"] = sb
    bc = np.zeros((P, NB), np.float32)
    bc[:TS] = tb[:, None] == np.arange(NB)[None, :]
    c["in_batch"] = bc
    c["exp_rank"] = np.broadcast_to(NE - np.arange(NE, dtype=np.float32), (P, NE))
    sel = np.zeros((P, 12, P), np.float32)
    for br in range(3):
        for r in range(GRP):
            for g in range(NKV):
                sel[(g * GRP + r) * 3 + br, br * GRP + r, g * HD:(g + 1) * HD] = 1
    c["gate_sel"] = sel.reshape(P, -1)
    se = np.zeros((P, NE, P), np.float32)
    for e in range(NE):
        se[e, e] = 1
    c["exp_sel"] = se.reshape(P, -1)
    c["eps"] = np.full((P, 1), EPS, np.float32)
    return c


CONST = constants()
CONST_AT, _n = {}, 0
for _k, _v in CONST.items():
    CONST_AT[_k] = (_n, _v.shape[1])
    _n += _v.shape[1]
N_CONST = _n

PAR = {"norm_mix": KD, "norm_ffn": KD, "qk_norm": 7, "conv_w": 4 * 6, "conv_b": 6, "ssm_d": 4, "ssm_norm": 4,
       "sc_w": 3 * 4, "dt_bias": NH, "a_log": NH, "w_small": KD * 32, "router": KD * NE}
PAR_AT, _n = {}, 0
for _k, _v in PAR.items():
    PAR_AT[_k] = (_n, _v)
    _n += _v
N_PAR = _n

XBCW = 3 + TP + NB * (3 + TD)
SCW = 2 + TP + NB * (2 + TD)


def build(nc, xT_in, consts, params, wstream, page_table, kc_pages, vc_pages, slc_pages, win_kT, win_v, win_rows,
          ssm_in, conv_in, sc_in, y_out, kv_out, win_out, ssm_p_out, ssm_s_out, conv_out, sc_out):
    f32, i32 = mybir.dt.float32, mybir.dt.int32
    ALU, ACT, AX = mybir.AluOpType, mybir.ActivationFunctionType, mybir.AxisListType
    V, A = nc.vector, nc.scalar

    with ExitStack() as ctx:
        def sb(name, cols, dt=f32):
            return ctx.enter_context(nc.sbuf_tensor(name, [P, cols], dt))

        def sem(name):
            return ctx.enter_context(nc.semaphore(name))

        xT_ = sb("xT", KD * T)
        xn_ = sb("xn", KD * T)
        tmp_ = sb("tmp", KD * T)
        oN_ = sb("o_nsa", 4 * T)
        oS_ = sb("o_ssm", 4 * T)
        oC_ = sb("o_sc", 4 * T)
        wring = sb("wring", RING * SLOTF)
        pages = sb("pages", 3 * 4096)
        cst = sb("cst", N_CONST)
        par = sb("par", DEPTH * N_PAR)
        std = sb("std", T)
        mark = sb("mark", 2 * MARKS)
        REG = 12100
        reg = sb("phase_region", REG)
        ptab = sb("ptab", NB * NPG, i32)

        def view(t, off, *dims):
            n = int(np.prod(dims))
            ap = t[:, off:off + n]
            if len(dims) == 2:
                ap = ap.rearrange("p (a b) -> p a b", b=dims[1])
            elif len(dims) == 3:
                ap = ap.rearrange("p (a b c) -> p a b c", b=dims[1], c=dims[2])
            elif len(dims) == 4:
                ap = ap.rearrange("p (a b c d) -> p a b c d", b=dims[1], c=dims[2], d=dims[3])
            return ap

        xT, xn, tmp = (view(t, 0, KD, T) for t in (xT_, xn_, tmp_))
        oN, oS, oC = (view(t, 0, 4, T) for t in (oN_, oS_, oC_))

        class Region:
            def __init__(self, at):
                self.at = at

            def __call__(self, *dims):
                ap = view(reg, self.at, *dims)
                self.at += int(np.prod(dims))
                assert self.at <= REG, self.at
                return ap

        ra = Region(0)
        qkv = ra(NQKV, T)
        vtok = ra(3, 3, P)
        otok = ra(2, GRP, NKV, HD)
        gates = ra(3, 24)
        small = ra(3, 32)
        gT = ra(TS)
        gB = ra(3, GRP, TS)
        kcT, vcT = ra(HALF, NCS), ra(HALF, NCS)
        kcTp, vcTp = ra(NCP + 1), ra(NCP + 1)
        vcp = ra(P)
        mx, ssum, rsum, coef = ra(2, GRP), ra(2, GRP), ra(GRP), ra(GRP)
        scratch = ra.at
        rq = view(reg, scratch, 7, T)
        rp = Region(scratch)
        S_p = [rp(1024), rp(1024)]
        PT_p = rp(2, 4 * P)
        otmp = rp(GRP, HD)
        rs_ = Region(scratch)
        qbd = rs_(NB, 32)
        vc = rs_(HALF, P)
        S_s = rs_(PAST + TS)
        PT_s = rs_(9, P)
        S_c = rs_(64)
        PT_c = rs_(P)
        imp, drop, tie, m1 = rs_(NMID), rs_(NMID), rs_(NMID), rs_(4)
        orow = rs_(3, P)
        smx, ssm, srs = rs_(4), rs_(4), rs_(4)
        osam = rs_(2, HALF * 16)
        rb = Region(0)
        dt = rb(3, NH)
        dta = rb(3, NH)
        sp_v, sp_e, sp_z, sp_q, sp_p = (rb(3, NH) for _ in range(5))
        ea = rb(NH)
        xbcp = rb(6, XBCW)
        xbcc = rb(6, T)
        zs = rb(4, T)
        b_scratch = rb.at
        rc = Region(b_scratch)
        scc = rc(4, T)
        chp = rc(4, SCW)
        sc_st = rc(4, NB * 2)
        cv_st = rc(6, NB * 3)
        rd = Region(b_scratch)
        decay = rd(1024)
        eB = rd(1024)
        cp = rd(GRP * P)
        xdt = rd(SSMI)
        xtl = rd(SSMI)
        btok = rd(P)
        hT = rd(GRP, HD)
        acs = rd(2 * NH)
        tail = rd(NH)
        hs = rd(NB, GRP, HD)
        bm = rd(NB, P)
        rf = Region(0)
        h = rf(NFE, T)
        cb = rf(NE, T)
        gs_ = rf(6, T)
        rl, rl2, rs1, rs2, rt = (view(reg, k * 24, 3, NE) for k in range(5))
        rm1, rm2, re, rg1, rg2 = (view(reg, 120 + k * 3, 3, 1) for k in range(5))
        combT = view(reg, 200, T)


        def C(name, rows=P):
            a, n = CONST_AT[name]
            return cst[0:rows, a:a + n]

        def PR(l, name, i=0, n=1):
            a, _ = PAR_AT[name]
            a += l * N_PAR + i
            return par[:, a:a + n]

        def bc(ap, axis, n):
            a = ap.unsqueeze(axis)
            shape = list(a.shape)
            shape[axis] = n
            return a.to_broadcast(shape)

        psum = [ctx.enter_context(nc.psum_tensor(f"bank{i}", [P, 512], f32)) for i in range(8)]
        bank_full = [sem(f"bank_full{i}") for i in range(8)]
        bank_free = [sem(f"bank_free{i}") for i in range(8)]
        w_full = [sem(f"w_full{i}") for i in range(RING)]
        w_free = [sem(f"w_free{i}") for i in range(RING)]
        pg_full = [sem(f"pg_full{i}") for i in range(3)]
        names = ("const_in x_in ptab_in table_read sq_ready std_ready xn_ready x_ready small_ready gates_ready qkv_ready "
                 "qksq_ready rq_ready qk_normed qk_ready vtok_ready kc_ready vcT_ready vc_ready smax exp_ready pt_ready otok_ready "
                 "qbd_ready scmax sc_exp pc_ready ptc_ready ssmax ss_exp pts_ready orow_ready gT_ready gB_ready attn_done "
                 "xbc_ready z_ready st_in xbcc_raw xbcc_ready scc_ready cols_ready spa sp_exp ea_ready dD_ready eb_ready seg_ready "
                 "dec_exp dec_ready tl_sub tl_ready cp_ready xdt_ready btok_ready h_ready bm_ready y_ready ysq_ready ystd_ready "
                 "oS_ready mix_done gate_sig merged_ready silu_ready h_up comb_ready combT_ready cb_ready "
                 "rl_ready re_sub re_exp kv_done hp_done hs_done cc_done win_done dve_chain act_chain pool_zero "
                 "y_done oC_ready scb_ready sc_conv hs_in").split()
        S = {n: sem(n) for n in names}

        use_of = {}
        moe_base = [0]
        MOE_USES = 2 * NFE + KD
        assert MOE_USES % 8 == 0

        def full(eng, key, it=None):
            u = use_of[key]
            n = u // 8 + 1
            eng.wait_ge(bank_full[u % 8], n if it is None else n + it * (MOE_USES // 8))
            return psum[u % 8]

        def free(key):
            return bank_free[use_of[key] % 8]

        def ready(eng, name, n):
            eng.wait_ge(S[name], n)

        FILLS = [(l, hf, what) for l in range(DEPTH) for hf in range(2) for what in ("kc", "vc", "slc0", "slc1", "win")]
        fill_dmas = {"kc": HALF * NPG, "vc": HALF * NPG, "slc0": 2 * NPG, "slc1": 2 * NPG, "win": 1 + HALF}
        fill_at, fill_sum = {}, [0, 0, 0]
        for n, f in enumerate(FILLS):
            fill_sum[n % 3] += 16 * fill_dmas[f[2]]
            fill_at[f] = (n % 3, fill_sum[n % 3])

        def page_slot(f):
            return 4096 * fill_at[f][0]

        UNITS = [(g, qt, br) for g in range(NKV) for qt in range(2) for br in range(3)]

        block = ctx.enter_context(nc.Block())

        @block.tensor
        def _(pe):
            uses = [0]
            blk = [0]
            last_slot = [-1]

            def bank(key):
                u = uses[0]
                uses[0] += 1
                use_of[key] = u
                if u >= 8:
                    pe.wait_ge(bank_free[u % 8], u // 8)
                return psum[u % 8], bank_full[u % 8]

            def wblock():
                n = blk[0]
                blk[0] += 1
                s, o = divmod(n, BPS)
                release = None
                if s != last_slot[0]:
                    pe.wait_ge(w_full[s % RING], 16 * (s // RING + 1))
                    if s > 0:
                        release = w_free[(s - 1) % RING]
                    last_slot[0] = s
                a = (s % RING) * SLOTF + o * P
                return wring[:, a:a + P], release

            def product(key, n, rhs, width=T, w=wblock):
                ps, done = bank(key)
                for k in range(n):
                    wb, release = w()
                    mm = nc.tensor.matmul(ps[:, 0:width], wb, rhs(k), start=(k == 0), stop=(k == n - 1))
                    if release is not None:
                        mm.then_inc(release, 1)
                mm.then_inc(done, 1)

            def column_sum(key, n, lhs, rhs):
                ps, done = bank(key)
                for k in range(n):
                    mm = nc.tensor.matmul(ps[:, 0:T], lhs, rhs(k), start=(k == 0), stop=(k == n - 1))
                mm.then_inc(done, 1)

            ident = C("ident")
            pe.wait_ge(S["const_in"], 32)
            for l in range(DEPTH):
                ready(pe, "sq_ready", 2 * l + 1)
                column_sum(("ss", l, 0), KD, C("ones"), lambda k: tmp[:, k, :])
                ready(pe, "xn_ready", 2 * l + 1)
                ps, done = bank(("small", l))
                for tt, (t0, n) in enumerate(TILES):
                    for k in range(KD):
                        mm = nc.tensor.matmul(ps[0:n, 32 * tt:32 * tt + 32], xn[:, k, t0:t0 + n],
                                              PR(l, "w_small", 32 * k, 32), start=(k == 0), stop=(k == KD - 1))
                mm.then_inc(done, 1)
                for i in range(NQKV):
                    product(("in", l, i), KD, lambda k: xn[:, k, :])
                ready(pe, "qksq_ready", l + 1)
                for i in range(7):
                    column_sum(("qkss", l, i), 1, C("head_ones"), lambda k: tmp[:, i, :])
                ready(pe, "qkv_ready", l + 1)
                for tt, (t0, n) in enumerate(TILES):
                    ps, done = bank(("vt", l, tt))
                    for br in range(3):
                        mm = nc.tensor.transpose(ps[0:n, br * P:(br + 1) * P], qkv[:, 7 + br, t0:t0 + n], ident)
                    mm.then_inc(done, 1)
                ready(pe, "gates_ready", l + 1)
                ps, done = bank(("gT", l))
                nc.tensor.transpose(ps[0:24, 0:TS], gates[0:TS, 2, :], C("ident", TS)[:, 0:TS]).then_inc(done, 1)
                ready(pe, "gT_ready", l + 1)
                ps, done = bank(("gB", l))
                for j in range(12):
                    mm = nc.tensor.matmul(ps[:, j * TS:(j + 1) * TS], C("gate_sel", 24)[:, j * P:(j + 1) * P],
                                          gT[0:24, :], start=True, stop=True)
                mm.then_inc(done, 1)
                ready(pe, "qk_normed", l + 1)
                for i in range(7):
                    column_sum(("rot", l, i), 1, C("rot"), lambda k: qkv[:, i, :])

                def compress(hf):
                    for kind in range(2):
                        fill = (l, hf, ("kc", "vc")[kind])
                        pos, n = fill_at[fill]
                        pe.wait_ge(pg_full[pos], n)
                        src = view(pages, page_slot(fill), HALF, PAST // STRIDE, STRIDE)
                        ps, done = bank(("cmp", l, hf, kind))
                        if hf == 0:
                            if kind == 0:
                                ready(pe, "qk_ready", l + 1)
                            ps2, done2 = bank(("cmpp", l, kind))
                            prm = qkv[:, (4, 7)[kind], 0:TP].rearrange("p (c j) -> p c j", j=STRIDE)
                        for j in range(32):
                            wb, release = wblock()
                            a, jj = divmod(j, STRIDE)
                            mm = nc.tensor.matmul(ps[:, 0:HALF * NCS].rearrange("p (b c) -> p b c", b=HALF), wb,
                                                  src[:, :, a:a + NCS, jj], start=(j == 0), stop=(j == 31))
                            if release is not None:
                                mm.then_inc(release, 1)
                            if j == 31:
                                mm.then_inc(done, 1)
                            if hf == 0:
                                mm = nc.tensor.matmul(ps2[:, 0:NCP], wb, prm[:, a:a + NCP, jj], start=(j == 0), stop=(j == 31))
                        if hf == 0:
                            mm.then_inc(done2, 1)

                compress(0)
                ready(pe, "vcT_ready", 3 * l + 2)
                ps, done = bank(("vcp", l))
                nc.tensor.transpose(ps[0:NCP, 0:P], vcTp[:, 0:NCP], ident).then_inc(done, 1)
                ready(pe, "vtok_ready", l + 1)

                def unit_scores(n):
                    g, qt, br = UNITS[n]
                    gd = slice(HD * g, HD * g + HD)
                    q = lambda r: qkv[gd, r, qt * P:qt * P + P]
                    if br == 0:
                        ps, done = bank(("S", l, n, 0))
                        for r in range(GRP):
                            mm = nc.tensor.matmul(ps[:, r * NCP:(r + 1) * NCP], q(r), kcTp[gd, 0:NCP], start=True, stop=True)
                        mm.then_inc(done, 1)
                        return
                    nk = P * (qt + 1)
                    for part in range(qt + 1):
                        ps, done = bank(("S", l, n, part))
                        for i in range(512 // nk):
                            r = part * 2 + i
                            mm = nc.tensor.matmul(ps[:, i * nk:(i + 1) * nk], q(r), qkv[gd, 4 + br, 0:nk], start=True, stop=True)
                        mm.then_inc(done, 1)

                def unit_out(n):
                    g, qt, br = UNITS[n]
                    w = NCP if br == 0 else P
                    nkc = 1 if br == 0 else qt + 1
                    s = S_p[n % 2][:, 0:GRP * w * nkc].rearrange("p (r k) -> p r k", r=GRP)
                    ready(pe, "exp_ready", 12 * l + n + 1)
                    for kc in range(nkc):
                        ps, done = bank(("T", l, n, kc))
                        for r in range(GRP):
                            mm = nc.tensor.transpose(ps[0:w, r * P:(r + 1) * P], s[:, r, kc * w:(kc + 1) * w], ident)
                        mm.then_inc(done, 1)
                    ready(pe, "pt_ready", 12 * l + n + 1)
                    ps, done = bank(("O", l, n))
                    for r in range(GRP):
                        for kc in range(nkc):
                            v = vcp[0:w, g * HD:(g + 1) * HD] if br == 0 else vtok[:, kc, br, g * HD:(g + 1) * HD]
                            mm = nc.tensor.matmul(ps[:, r * HD:(r + 1) * HD], PT_p[0:w, kc, r * P:(r + 1) * P], v,
                                                  start=(kc == 0), stop=(kc == nkc - 1))
                    mm.then_inc(done, 1)

                ready(pe, "vc_ready", 3 * l + 1)
                for n in range(13):
                    if n < 12:
                        unit_scores(n)
                    if n > 0:
                        unit_out(n - 1)
                ready(pe, "otok_ready", l + 1)
                for qt in range(2):
                    ps, done = bank(("ot", l, qt))
                    for r in range(GRP):
                        mm = nc.tensor.transpose(ps[:, r * P:(r + 1) * P], otok[:, qt, r, :, :], ident)
                    mm.then_inc(done, 1)

                ready(pe, "qbd_ready", l + 1)
                for hf in range(2):
                    it = 2 * l + hf
                    if hf == 1:
                        compress(1)
                    ready(pe, "vcT_ready", 3 * l + 2 + hf)
                    ps, done = bank(("vct", l, hf))
                    for bi in range(HALF):
                        mm = nc.tensor.transpose(ps[0:NCS, bi * P:(bi + 1) * P], vcT[:, bi, :], ident)
                    mm.then_inc(done, 1)
                    ps, done = bank(("Sc", l, hf))
                    for bi in range(HALF):
                        mm = nc.tensor.matmul(ps[32 * bi:32 * bi + 32, 0:NCS], qbd[:, hf * HALF + bi, :], kcT[:, bi, :],
                                              start=True, stop=True)
                    mm.then_inc(done, 1)
                    ready(pe, "pc_ready", it + 1)
                    ps, done = bank(("imp", l, hf))
                    nc.tensor.matmul(ps[:, 0:NCS], C("group_sum"), S_c[:, 0:NCS], start=True, stop=True).then_inc(done, 1)
                    ps, done = bank(("Tc", l, hf))
                    nc.tensor.transpose(ps[0:NCS, 0:P], S_c[:, 0:NCS], ident).then_inc(done, 1)
                    ready(pe, "ptc_ready", it + 1)
                    ready(pe, "vc_ready", 3 * l + 2 + hf)
                    ps, done = bank(("Oc", l, hf))
                    for bi in range(HALF):
                        mm = nc.tensor.matmul(ps[32 * bi:32 * bi + 32, 0:P], PT_c[0:NCS, 32 * bi:32 * bi + 32],
                                              vc[0:NCS, bi, :], start=True, stop=True)
                    mm.then_inc(done, 1)
                    for br, ncol in ((1, PAST), (2, WIN)):
                        nk = ncol // 512
                        keys = []
                        for bi in range(HALF):
                            if br == 1:
                                f = (l, hf, ("slc0", "slc1")[bi // 2])
                                s = view(pages, page_slot(f), 2, NPG, 2, P)[:, bi % 2]
                                keys.append((f, s[:, :, 0, :], s[:, :, 1, :]))
                            else:
                                f = (l, hf, "win")
                                s = view(pages, page_slot(f), 2, HALF, 4, P)
                                keys.append((f, s[:, 0, bi], s[:, 1, bi]))
                        for c in range(nk):
                            ps, done = bank(("Ss", l, hf, br, c))
                            for bi in range(HALF):
                                f, kT, _ = keys[bi]
                                pe.wait_ge(pg_full[fill_at[f][0]], fill_at[f][1])
                                mm = nc.tensor.matmul(ps[32 * bi:32 * bi + 32, 0:512].rearrange("p (a b) -> p a b", a=4),
                                                      qbd[:, hf * HALF + bi, :], kT[:, 4 * c:4 * c + 4, :], start=True, stop=True)
                            mm.then_inc(done, 1)
                        ps, done = bank(("Sn", l, hf, br))
                        for bi in range(HALF):
                            mm = nc.tensor.matmul(ps[32 * bi:32 * bi + 32, 0:TS], qbd[:, hf * HALF + bi, :],
                                                  qkv[:, 4 + br, TP:T], start=True, stop=True)
                        mm.then_inc(done, 1)
                        ready(pe, "ss_exp", 2 * it + br)
                        for c in range(nk):
                            ps, done = bank(("Ts", l, hf, br, c))
                            for i in range(4):
                                mm = nc.tensor.transpose(ps[:, i * P:(i + 1) * P], S_s[:, 512 * c + i * P:512 * c + (i + 1) * P], ident)
                            mm.then_inc(done, 1)
                        ps, done = bank(("Tn", l, hf, br))
                        nc.tensor.transpose(ps[0:TS, 0:P], S_s[:, ncol:ncol + TS], ident).then_inc(done, 1)
                        ready(pe, "pts_ready", 2 * it + br)
                        ps, done = bank(("Os", l, hf, br))
                        for bi in range(HALF):
                            for c in range(4 * nk):
                                nc.tensor.matmul(ps[32 * bi:32 * bi + 32, 0:P], PT_s[:, c, 32 * bi:32 * bi + 32],
                                                 keys[bi][2][:, c, :], start=(c == 0), stop=False)
                            mm = nc.tensor.matmul(ps[32 * bi:32 * bi + 32, 0:P], PT_s[0:TS, 8, 32 * bi:32 * bi + 32],
                                                  vtok[0:TS, 2, br, :], start=False, stop=True)
                        mm.then_inc(done, 1)
                    ready(pe, "orow_ready", it + 1)
                    ps, done = bank(("oT", l, hf))
                    for br in range(3):
                        mm = nc.tensor.transpose(ps[:, br * P:(br + 1) * P], orow[:, br, :], ident)
                    mm.then_inc(done, 1)

                for i in range(NQKV, NQKV + NREST):
                    product(("in", l, i), KD, lambda k: xn[:, k, :])

                for c in range(NCHUNK):
                    t0, n = TILES[c]
                    cc = NCHUNK * l + c
                    up = C("upto0") if c < 2 else C("upto2", TS)
                    all_ = C("ones") if c < 2 else C("same2", TS)
                    ready(pe, "xbcc_ready", l + 1)
                    ps, done = bank(("xtok", cc))
                    for j in range(4):
                        mm = nc.tensor.transpose(ps[0:n, j * P:(j + 1) * P], xbcc[:, j, t0:t0 + n], ident)
                    mm.then_inc(done, 1)
                    ps, done = bank(("btok", cc))
                    nc.tensor.transpose(ps[0:n, 0:P], xbcc[:, 4, t0:t0 + n], ident).then_inc(done, 1)
                    for g in range(NKV):
                        ps, done = bank(("CB", cc, g))
                        gd = slice(HD * g, HD * g + HD)
                        nc.tensor.matmul(ps[0:n, 0:n], xbcc[gd, 4, t0:t0 + n], xbcc[gd, 5, t0:t0 + n],
                                         start=True, stop=True).then_inc(done, 1)
                    ready(pe, "dD_ready", cc + 1)
                    ps, done = bank(("ac", cc))
                    nc.tensor.matmul(ps[0:n, 0:NH], up, dta[0:n, c, :], start=True, stop=True)
                    nc.tensor.matmul(ps[0:n, NH:2 * NH], all_[:, 0:n], dta[0:n, c, :], start=True, stop=True).then_inc(done, 1)
                    for part in range(2 if c < 2 else 1):
                        ps, done = bank(("acB", cc, part))
                        w = min(512, NH * n)
                        nc.tensor.matmul(ps[:, 0:w], C("ones", n), decay[0:n, part * 512:part * 512 + w],
                                         start=True, stop=True).then_inc(done, 1)
                    ready(pe, "dec_ready", cc + 1)
                    ready(pe, "xdt_ready", cc + 1)
                    if c > 0:
                        ready(pe, "cp_ready", 2 * l + c)
                    for hh in range(NH):
                        j, h2 = divmod(hh % GRP, 2)
                        g, hg = divmod(hh, GRP)
                        if hg == 0:
                            ps, done = bank(("y", cc, g))
                        gd = slice(HD * g, HD * g + HD)
                        o = ps[HD * h2:HD * h2 + HD, j * n:(j + 1) * n]
                        mm = nc.tensor.matmul(o, xdt[0:n, hh * HD:(hh + 1) * HD], decay[0:n, hh * n:(hh + 1) * n],
                                              start=True, stop=(c == 0))
                        if c == 1:
                            mm = nc.tensor.matmul(o, hT[gd, hg, :], cp[gd, hg * n:(hg + 1) * n], start=False, stop=True)
                        if c == 2:
                            for b in range(NB):
                                mm = nc.tensor.matmul(o[:, b * TD:(b + 1) * TD], hs[gd, b, hg, :],
                                                      cp[gd, hg * n + b * TD:hg * n + (b + 1) * TD], start=False, stop=(b == NB - 1))
                        if hg == GRP - 1:
                            mm.then_inc(done, 1)
                    ready(pe, "btok_ready", cc + 1)
                    if c < 2:
                        ps, done = bank(("hd", cc))
                        for g in range(NKV):
                            mm = nc.tensor.matmul(ps[HD * g:HD * g + HD, 0:256], btok[0:n, g * HD:(g + 1) * HD],
                                                  xtl[0:n, g * 256:(g + 1) * 256], start=True, stop=True)
                        mm.then_inc(done, 1)
                        if c == 0:
                            ready(pe, "h_ready", 2 * l + 1)
                    else:
                        ready(pe, "bm_ready", l + 1)
                        for b2 in range(NB // 2):
                            ps, done = bank(("hsd", l, b2))
                            for i in range(2):
                                for g in range(NKV):
                                    mm = nc.tensor.matmul(ps[HD * g:HD * g + HD, 256 * i:256 * i + 256],
                                                          bm[0:n, 2 * b2 + i, g * HD:(g + 1) * HD],
                                                          xtl[0:n, g * 256:(g + 1) * 256], start=True, stop=True)
                            mm.then_inc(done, 1)
                ready(pe, "ysq_ready", l + 1)
                column_sum(("yss", l), 4, C("ones"), lambda k: tmp[:, k, :])

                ready(pe, "oS_ready", l + 1)
                o_br = (oN, oS, oC)
                for m in range(KD):
                    for k3 in range(3):
                        product(("gate", l, m, k3), KD, lambda k: xn[:, k, :])
                    for k3 in range(3):
                        product(("proj", l, m, k3), 4, lambda k: o_br[k3][:, k, :])
                ready(pe, "merged_ready", l + 1)
                for m in range(KD):
                    product(("o", l, m), KD, lambda k: tmp[:, k, :])
                ready(pe, "sq_ready", 2 * l + 2)
                column_sum(("ss", l, 1), KD, C("ones"), lambda k: tmp[:, k, :])
                ready(pe, "xn_ready", 2 * l + 2)
                if l == 0:
                    for f in range(NFD):
                        product(("fg", f), KD, lambda k: xn[:, k, :])
                        product(("fu", f), KD, lambda k: xn[:, k, :])
                    pe.wait_ge(free(("fu", NFD - 1)), use_of[("fu", NFD - 1)] // 8 + 1)
                    for m in range(KD):
                        product(("fd", m), NFD, lambda k: h[:, k, :])
            ps, done = bank(("router",))
            for tt, (t0, n) in enumerate(TILES):
                for k in range(KD):
                    mm = nc.tensor.matmul(ps[0:n, NE * tt:NE * tt + NE], xn[:, k, t0:t0 + n],
                                          PR(1, "router", NE * k, NE), start=(k == 0), stop=(k == KD - 1))
            mm.then_inc(done, 1)
            ready(pe, "comb_ready", 1)
            ps, done = bank(("combT",))
            for tt, (t0, n) in enumerate(TILES):
                mm = nc.tensor.transpose(ps[0:NE, t0:t0 + n], rt[0:n, tt, :], C("ident", n)[:, 0:n])
            mm.then_inc(done, 1)
            ready(pe, "combT_ready", 1)
            for e in range(NE):
                ps, done = bank(("cb", e))
                nc.tensor.matmul(ps[:, 0:T], C("exp_sel", NE)[:, e * P:(e + 1) * P], combT[0:NE, :],
                                 start=True, stop=True).then_inc(done, 1)
            base = uses[0]
            assert blk[0] == PRE_SLOTS * BPS
            with pe.Fori(0, NE) as e:
                def ebank(key, i):
                    u = base + i
                    use_of[key] = u
                    pe.wait_ge(bank_free[u % 8], e * (MOE_USES // 8) + u // 8)
                    return psum[u % 8], bank_full[u % 8]

                n = [0]

                def eproduct(key, i, nk, rhs):
                    ps, done = ebank(key, i)
                    for k in range(nk):
                        s, o = divmod(n[0], BPS)
                        n[0] += 1
                        s += PRE_SLOTS
                        if o == 0:
                            pe.wait_ge(w_full[s % RING], e * (16 * EXP_SLOTS // RING) + 16 * (s // RING + 1))
                        a = (s % RING) * SLOTF + o * P
                        mm = nc.tensor.matmul(ps[:, 0:T], wring[:, a:a + P], rhs(k), start=(k == 0), stop=(k == nk - 1))
                        if o == 0:
                            mm.then_inc(w_free[(s - 1) % RING], 1)
                    mm.then_inc(done, 1)

                for f in range(NFE):
                    eproduct(("eg", f), 2 * f, KD, lambda k: xn[:, k, :])
                    eproduct(("eu", f), 2 * f + 1, KD, lambda k: xn[:, k, :])
                u = use_of[("eu", NFE - 1)]
                pe.wait_ge(bank_free[u % 8], e * (MOE_USES // 8) + u // 8 + 1)
                for m in range(KD):
                    eproduct(("ed", m), 2 * NFE + m, NFE, lambda k: h[:, k, :])

        @block.sync
        def _(sp):
            sp.dma_start(cst[:, :], consts).then_inc(S["const_in"], 16)
            sp.dma_start(par[:, :], params).then_inc(S["const_in"], 16)
            sp.dma_start(xT_[:, :], xT_in).then_inc(S["x_in"], 16)

            def load(pos, index):
                sp.dma_start(wring[:, pos * SLOTF:(pos + 1) * SLOTF],
                             wstream[index, :, :].rearrange("a p n -> (a p) n")).then_inc(w_full[pos], 16)

            for s in range(RING):
                load(s, bass.ds(s, 1))
            rounds = (N_SLOTS - RING) // RING
            with sp.Fori(0, rounds) as i:
                for s in range(RING):
                    sp.wait_ge(w_free[s], i + 1)
                    load(s, bass.ds(i * RING + (RING + s), 1))
            for s in range(RING * (rounds + 1), N_SLOTS):
                sp.wait_ge(w_free[s % RING], s // RING)
                load(s % RING, bass.ds(s, 1))
            ready(sp, "x_ready", 4)
            sp.dma_start(y_out, xT_[:, :]).then_inc(S["y_done"], 16)
            sp.wait_ge(S["y_done"], 16)

        @block.gpsimd
        def _(pool):
            pool.dma_start(ptab[0:1, :], page_table).then_inc(S["ptab_in"], 16)
            ready(pool, "ptab_in", 16)
            n_pool = kc_pages.shape[0] // DEPTH

            def fill(f):
                l, hf, what = f
                idx = FILLS.index(f)
                pos = idx % 3
                at = page_slot(f)
                if idx >= 3:
                    pl, phf, pw = FILLS[idx - 3]
                    last = {"kc": ("cmp", pl, phf, 0) if phf else ("cmpp", pl, 0), "vc": ("cmp", pl, phf, 1) if phf else ("cmpp", pl, 1),
                            "slc0": ("Os", pl, phf, 1), "slc1": ("Os", pl, phf, 1), "win": ("Os", pl, phf, 2)}[pw]
                    full(pool, last)
                if what == "win":
                    pool.dma_start(view(pages, at, HALF, WIN),
                                   win_kT[l, :, hf * HALF:(hf + 1) * HALF, :]).then_inc(pg_full[pos], 16)
                    for bi in range(HALF):
                        pool.dma_start(view(pages, at + 2048 + bi * 512, 4, P),
                                       win_v[l, hf * HALF + bi]).then_inc(pg_full[pos], 16)
                    return
                src, width, b0, nb = {"kc": (kc_pages, P, 0, HALF), "vc": (vc_pages, P, 0, HALF),
                                      "slc0": (slc_pages, 2 * P, 0, 2), "slc1": (slc_pages, 2 * P, 2, 2)}[what]
                first = (hf * HALF + b0) * NPG
                with pool.Fori(0, nb * NPG) as i:
                    page = pool.value_load(ptab[0:1, bass.ds(i + first, 1)], min_val=0, max_val=n_pool - 1)
                    pool.dma_start(pages[:, bass.ds(i * width + at, width)],
                                   src[bass.ds(page + l * n_pool, 1), :, :].rearrange("a p n -> (a p) n")).then_inc(pg_full[pos], 16)

            for f in FILLS[0:3]:
                fill(f)
            nout = 0
            for l in range(DEPTH):
                pool.dma_start(win_out[l], win_rows[l, :, TD:, :]).then_inc(S["win_done"], 16)
                ready(pool, "qk_ready", l + 1)
                pool.dma_start(kv_out[l], qkv[:, 4:10, :]).then_inc(S["kv_done"], 16)
                for f in FILLS[3:10] if l == 0 else FILLS[13:20]:
                    fill(f)
                ready(pool, "kv_done", 16 * (l + 1))
                ready(pool, "attn_done", l + 1)
                pool.dma_start(sc_st, sc_in[l]).then_inc(S["st_in"], 16)
                pool.dma_start(cv_st, conv_in[l]).then_inc(S["st_in"], 16)
                ready(pool, "cols_ready", l + 1)
                for t in range(6):
                    pool.dma_start(conv_out[l, :, t, 0:3], xbcp[:, t, TP:TP + 3]).then_inc(S["cc_done"], 16)
                    pool.dma_start(conv_out[l, :, t, 3:27].rearrange("p (b k) -> p b k", b=NB),
                                   xbcp[:, t, 3 + TP:].rearrange("p (b k) -> p b k", b=NB)[:, :, TD:TD + 3]).then_inc(S["cc_done"], 16)
                for t in range(4):
                    pool.dma_start(sc_out[l, :, t, 0:2], chp[:, t, TP:TP + 2]).then_inc(S["cc_done"], 16)
                    pool.dma_start(sc_out[l, :, t, 2:18].rearrange("p (b k) -> p b k", b=NB),
                                   chp[:, t, 2 + TP:].rearrange("p (b k) -> p b k", b=NB)[:, :, TD:TD + 2]).then_inc(S["cc_done"], 16)
                ready(pool, "cc_done", 320 * (l + 1))
                ready(pool, "sc_conv", l + 1)
                pool.dma_start(hs, ssm_in[l]).then_inc(S["hs_in"], 16)
                ready(pool, "h_ready", 2 * l + 2)
                pool.dma_start(ssm_p_out[l], hT).then_inc(S["hp_done"], 16)
                ready(pool, "y_ready", l + 1)
                pool.dma_start(ssm_s_out[l], hs).then_inc(S["hs_done"], 16)
                ready(pool, "hp_done", 16 * (l + 1))
                ready(pool, "hs_done", 16 * (l + 1))
                if l == 0:
                    for f in FILLS[10:13]:
                        fill(f)
            ready(pool, "win_done", 32)

        @block.scalar
        def _(act):
            chain, marks = [0], [0]

            def link(ins):
                chain[0] += 1
                ins.then_inc(S["act_chain"], 1)
                act.wait_ge(S["act_chain"], chain[0])

            def copy(out, in_):
                return A.activation(out, in_, ACT.Copy)

            def evac(key, out, cols, rows=P, name=None):
                ps = full(act, key)
                src = ps[0:rows, 0:cols]
                if len(out.shape) == 3:
                    src = src.rearrange("p (a b) -> p a b", b=out.shape[2])
                copy(out, src).then_inc(free(key), 1)

            def signal(name):
                marks[0] += 1
                k = marks[0] % MARKS
                A.activation(mark[0:1, k:k + 1], eps[0:1, :], ACT.Copy).then_inc(S[name], 1)

            eps = C("eps")
            act.wait_ge(S["const_in"], 32)
            act.wait_ge(S["x_in"], 16)
            ready(act, "pool_zero", 1)

            def rms(l, which):
                A.activation(tmp_[:, :], xT_[:, :], ACT.Square).then_inc(S["sq_ready"], 1)
                ps = full(act, ("ss", l, which))
                A.activation(std[:, :], ps[:, 0:T], ACT.Sqrt, bias=eps, scale=1.0 / D).then_inc(free(("ss", l, which)), 1)

            for l in range(DEPTH):
                if l:
                    ready(act, "x_ready", 2 * l)
                rms(l, 0)
                ps = full(act, ("small", l))
                if l:
                    ready(act, "kv_done", 16 * l)
                copy(small[0:TS, 2, :], ps[0:TS, 64:96]).then_inc(S["small_ready"], 1)
                copy(small[:, 0:2, :], ps[:, 0:64].rearrange("p (a b) -> p a b", a=2)).then_inc(free(("small", l)), 1)
                act.wait_ge(free(("small", l)), use_of[("small", l)] // 8 + 1)
                A.activation(gates[0:TS, 2, :], small[0:TS, 2, 0:24], ACT.Sigmoid)
                A.activation(gates[:, 0:2, :], small[:, 0:2, 0:24], ACT.Sigmoid).then_inc(S["gates_ready"], 1)
                for i in range(NQKV):
                    evac(("in", l, i), qkv[:, i, :], T)
                act.wait_ge(free(("in", l, 9)), use_of[("in", l, 9)] // 8 + 1)
                A.activation(tmp[:, 0:7, :], qkv[:, 0:7, :], ACT.Square).then_inc(S["qksq_ready"], 1)
                signal("qkv_ready")
                for i in range(7):
                    ps = full(act, ("qkss", l, i))
                    A.activation(rq[:, i, :], ps[:, 0:T], ACT.Sqrt, bias=eps, scale=1.0 / HD).then_inc(free(("qkss", l, i)), 1)
                signal("rq_ready")
                for tt, (t0, n) in enumerate(TILES):
                    evac(("vt", l, tt), vtok[0:n, tt, :, :], 3 * P, n)
                signal("vtok_ready")
                ps = full(act, ("gT", l))
                copy(gT[0:24, :], ps[0:24, 0:TS]).then_inc(free(("gT", l)), 1)
                signal("gT_ready")
                ps = full(act, ("gB", l))
                copy(gB.rearrange("p a b c -> p (a b c)"), ps[:, 0:384]).then_inc(free(("gB", l)), 1)
                for kind, (o, op) in enumerate(((kcT, kcTp), (vcT, vcTp))):
                    evac(("cmp", l, 0, kind), o, HALF * NCS)
                    evac(("cmpp", l, kind), op[:, 0:NCP], NCP)
                    signal("vcT_ready")
                evac(("vcp", l), vcp[0:NCP, :], P, NCP)
                signal("vc_ready")
                for n, (g, qt, br) in enumerate(UNITS):
                    w = NCP if br == 0 else P * (qt + 1)
                    s = S_p[n % 2][:, 0:GRP * w].rearrange("p (r k) -> p r k", r=GRP)
                    ready(act, "smax", 12 * l + n + 1)
                    for r in range(GRP):
                        e = A.activation(s[:, r, :], s[:, r, :], ACT.Exp, bias=mx[:, n % 2, r:r + 1],
                                         accum_out=ssum[:, n % 2, r:r + 1])
                    e.then_inc(S["exp_ready"], 1)
                    rows = min(w, P)
                    for kc in range(1 if br == 0 else qt + 1):
                        evac(("T", l, n, kc), PT_p[0:rows, kc, :], 512, rows)
                    signal("pt_ready")
                for qt in range(2):
                    evac(("ot", l, qt), oN[:, :, qt * P:(qt + 1) * P], 512)
                for hf in range(2):
                    it = 2 * l + hf
                    if hf == 1:
                        ready(act, "orow_ready", it)
                        evac(("cmp", l, 1, 0), kcT, HALF * NCS)
                        evac(("cmp", l, 1, 1), vcT, HALF * NCS)
                        signal("vcT_ready")
                    evac(("vct", l, hf), vc[0:NCS, :, :], 512, NCS)
                    signal("vc_ready")
                    ready(act, "scmax", it + 1)
                    A.activation(S_c[:, 0:NCS], S_c[:, 0:NCS], ACT.Exp, bias=smx[:, 0:1], accum_out=ssm[:, 0:1]).then_inc(S["sc_exp"], 1)
                    evac(("Tc", l, hf), PT_c[0:NCS, :], P, NCS)
                    signal("ptc_ready")
                    for br, ncol in ((1, PAST), (2, WIN)):
                        ready(act, "ssmax", 2 * it + br)
                        A.activation(S_s[:, 0:ncol + TS], S_s[:, 0:ncol + TS], ACT.Exp, bias=smx[:, br:br + 1],
                                     accum_out=ssm[:, br:br + 1]).then_inc(S["ss_exp"], 1)
                        for c in range(ncol // 512):
                            evac(("Ts", l, hf, br, c), PT_s[:, 4 * c:4 * c + 4, :], 512)
                        evac(("Tn", l, hf, br), PT_s[0:TS, 8, :], P, TS)
                        signal("pts_ready")
                ready(act, "attn_done", l + 1)
                ready(act, "kv_done", 16 * (l + 1))
                A.activation(ea, PR(l, "a_log", 0, NH), ACT.Exp).then_inc(S["ea_ready"], 1)
                ready(act, "spa", l + 1)
                A.activation(sp_e, sp_e, ACT.Exp, scale=-1.0).then_inc(S["sp_exp"], 1)
                for j in range(6):
                    ps = full(act, ("in", l, 10 + j))
                    copy(xbcp[:, j, 3:3 + TP], ps[:, 0:TP])
                    copy(xbcp[:, j, 3 + TP:].rearrange("p (b k) -> p b k", b=NB)[:, :, 3:],
                         ps[:, TP:T].rearrange("p (b k) -> p b k", b=NB)).then_inc(free(("in", l, 10 + j)), 1)
                signal("xbc_ready")
                for j in range(4):
                    ps = full(act, ("in", l, 16 + j))
                    A.activation(zs[:, j, :], ps[:, 0:T], ACT.Silu).then_inc(free(("in", l, 16 + j)), 1)
                for j in range(4):
                    evac(("in", l, 20 + j), scc[:, j, :], T)
                signal("scc_ready")
                for j in range(4):
                    evac(("in", l, 28 + j), oC[:, j, :], T)
                signal("scb_ready")
                ready(act, "xbcc_raw", l + 1)
                A.activation(xbcc, xbcc, ACT.Silu).then_inc(S["xbcc_ready"], 1)
                for c in range(NCHUNK):
                    n = TILES[c][1]
                    cc = NCHUNK * l + c
                    w = NH * n
                    ready(act, "tl_sub", cc + 1)
                    A.activation(tail[0:n, :], tail[0:n, :], ACT.Exp).then_inc(S["tl_ready"], 1)
                    ready(act, "seg_ready", cc + 1)
                    A.activation(eB[:, 0:w], eB[:, 0:w], ACT.Exp).then_inc(S["eb_ready"], 1)
                    A.activation(decay[0:n, 0:w], decay[0:n, 0:w], ACT.Exp).then_inc(S["dec_exp"], 1)
                    evac(("btok", cc), btok[0:n, :], P, n)
                    signal("btok_ready")
                ready(act, "y_ready", l + 1)
                A.activation(tmp[:, 0:4, :], oS, ACT.Square).then_inc(S["ysq_ready"], 1)
                ps = full(act, ("yss", l))
                A.activation(std[:, :], ps[:, 0:T], ACT.Sqrt, bias=eps, scale=1.0 / SSMI).then_inc(free(("yss", l)), 1)
                ready(act, "mix_done", l + 1)
                ready(act, "hs_done", 16 * (l + 1))
                ready(act, "hp_done", 16 * (l + 1))
                for m in range(KD):
                    for k3 in range(3):
                        ps = full(act, ("gate", l, m, k3))
                        if m >= 2 and k3 == 0:
                            ready(act, "gate_sig", l * KD + m - 1)
                        A.activation(gs_[:, (m % 2) * 3 + k3, :], ps[:, 0:T], ACT.Sigmoid).then_inc(free(("gate", l, m, k3)), 1)
                ready(act, "x_ready", 2 * l + 1)
                rms(l, 1)
                if l == 0:
                    for f in range(NFD):
                        ps = full(act, ("fg", f))
                        if f >= 2:
                            act.wait_ge(free(("fu", f - 2)), use_of[("fu", f - 2)] // 8 + 1)
                        A.activation(gs_[:, f % 2, :], ps[:, 0:T], ACT.Silu).then_inc(free(("fg", f)), 1)
            ready(act, "re_sub", 1)
            A.activation(re, re, ACT.Exp).then_inc(S["re_exp"], 1)
            evac(("combT",), combT[0:NE, :], T, NE)
            signal("combT_ready")
            for e in range(NE):
                evac(("cb", e), cb[:, e, :], T)
            signal("cb_ready")
            with act.Fori(0, NE) as e:
                for f in range(NFE):
                    ps = full(act, ("eg", f), e)
                    u = use_of[("eu", f - 2 if f >= 2 else NFE - 2 + f)]
                    back = 0 if f >= 2 else MOE_USES // 8
                    act.wait_ge(bank_free[u % 8], e * (MOE_USES // 8) + (u // 8 + 1 - back))
                    A.activation(gs_[:, f % 2, :], ps[:, 0:T], ACT.Silu).then_inc(free(("eg", f)), 1)

        @block.vector
        def _(dve):
            chain, marks = [0], [0]

            def link(ins):
                chain[0] += 1
                ins.then_inc(S["dve_chain"], 1)
                dve.wait_ge(S["dve_chain"], chain[0])

            def signal(name):
                marks[0] += 1
                k = MARKS + marks[0] % MARKS
                V.memset(mark[0:1, k:k + 1], 0.0).then_inc(S[name], 1)

            def after(key):
                dve.wait_ge(free(key), use_of[key] // 8 + 1)

            dve.wait_ge(S["const_in"], 32)
            dve.wait_ge(S["x_in"], 16)
            V.memset(std[:, :], 0.0)
            V.memset(reg[:, :], 0.0).then_inc(S["pool_zero"], 1)

            def rms(l, which, w):
                dve.wait_ge(free(("ss", l, which)), use_of[("ss", l, which)] // 8 + 1)
                link(V.reciprocal(std[:, :], std[:, :]))
                for k in range(KD):
                    last = V.scalar_tensor_tensor(xn[:, k, :], xT[:, k, :], PR(l, w, k), std[:, :], ALU.mult, ALU.mult)
                last.then_inc(S["xn_ready"], 1)
                dve.wait_ge(S["xn_ready"], 2 * l + which + 1)

            for l in range(DEPTH):
                rms(l, 0, "norm_mix")
                ready(dve, "rq_ready", l + 1)
                link(V.reciprocal(rq, rq))
                for i in range(7):
                    last = V.scalar_tensor_tensor(qkv[:, i, :], qkv[:, i, :], PR(l, "qk_norm", i), rq[:, i, :], ALU.mult, ALU.mult)
                last.then_inc(S["qk_normed"], 1)
                for i in range(7):
                    ps = full(dve, ("rot", l, i))
                    V.tensor_tensor(rq[:, i, :], ps[:, 0:T], C("sin"), ALU.mult).then_inc(free(("rot", l, i)), 1)
                    link(V.tensor_tensor(qkv[:, i, :], qkv[:, i, :], C("cos"), ALU.mult))
                    last = V.tensor_tensor(qkv[:, i, :], qkv[:, i, :], rq[:, i, :], ALU.add)
                last.then_inc(S["qk_ready"], 1)
                ready(dve, "qk_ready", l + 1)

                def unit_softmax(n):
                    g, qt, br = UNITS[n]
                    w = NCP if br == 0 else P * (qt + 1)
                    s = S_p[n % 2][:, 0:GRP * w].rearrange("p (r k) -> p r k", r=GRP)
                    if br == 0:
                        mask = C("cmp_mask")[:, qt * NCP:(qt + 1) * NCP]
                    else:
                        mask = C(("causal0", "causal1")[qt])
                    parts = 2 if (br and qt) else 1
                    nr = GRP // parts
                    for part in range(parts):
                        ps = full(dve, ("S", l, n, part))
                        V.scalar_tensor_tensor(s[:, part * nr:(part + 1) * nr, :],
                                               ps[:, 0:nr * w].rearrange("p (r k) -> p r k", r=nr), HD ** -0.5,
                                               bc(mask, 1, nr), ALU.mult, ALU.add).then_inc(free(("S", l, n, part)), 1)
                    after(("S", l, n, parts - 1))
                    V.tensor_reduce(mx[:, n % 2, :], s, AX.X, ALU.max, negate=True).then_inc(S["smax"], 1)

                def unit_out(n):
                    g, qt, br = UNITS[n]
                    ready(dve, "exp_ready", 12 * l + n + 1)
                    ready(dve, "gates_ready", l + 1)
                    link(V.reciprocal(rsum, ssum[:, n % 2, :]))
                    gate = gates[:, qt, g * 12:(g + 1) * 12].rearrange("p (r k) -> p r k", k=3)[:, :, br]
                    link(V.tensor_tensor(coef, rsum, gate, ALU.mult))
                    if br == 0:
                        link(V.tensor_scalar(coef, coef, C("cmp_any")[:, qt:qt + 1], None, ALU.mult))
                    ps = full(dve, ("O", l, n))
                    src = ps[:, 0:256].rearrange("p (r d) -> p r d", r=GRP)
                    dst = otok[:, qt, :, g, :]
                    out = dst if br == 0 else otmp
                    V.tensor_tensor(out, src, bc(coef, 2, HD), ALU.mult).then_inc(free(("O", l, n)), 1)
                    if br:
                        after(("O", l, n))
                        link(V.tensor_tensor(dst, dst, otmp, ALU.add))

                for n in range(13):
                    if n < 12:
                        unit_softmax(n)
                    if n > 0:
                        unit_out(n - 1)
                signal("otok_ready")
                link(V.memset(qbd, 0.0))
                for g in range(NKV):
                    gd = slice(HD * g, HD * g + HD)
                    last = V.tensor_copy(qbd[gd, :, 16 * g:16 * g + 16].rearrange("p b (r t) -> p b r t", r=GRP),
                                         qkv[gd, 0:GRP, TP:T].rearrange("p r (b t) -> p b r t", b=NB))
                last.then_inc(S["qbd_ready"], 1)
                for hf in range(2):
                    it = 2 * l + hf
                    ps = full(dve, ("Sc", l, hf))
                    V.tensor_scalar(S_c[:, 0:NCS], ps[:, 0:NCS], HD ** -0.5, None, ALU.mult).then_inc(free(("Sc", l, hf)), 1)
                    after(("Sc", l, hf))
                    V.tensor_reduce(smx[:, 0:1], S_c[:, 0:NCS], AX.X, ALU.max, negate=True).then_inc(S["scmax"], 1)
                    ready(dve, "sc_exp", it + 1)
                    link(V.reciprocal(srs[:, 0:1], ssm[:, 0:1]))
                    V.tensor_scalar(S_c[:, 0:NCS], S_c[:, 0:NCS], srs[:, 0:1], None, ALU.mult).then_inc(S["pc_ready"], 1)
                    ps = full(dve, ("imp", l, hf))
                    V.tensor_reduce(imp, ps[:, 4:4 + 4 * NMID].rearrange("p (b k) -> p b k", k=4), AX.X, ALU.add)\
                        .then_inc(free(("imp", l, hf)), 1)
                    after(("imp", l, hf))
                    link(V.tensor_reduce(m1[:, 0:1], imp, AX.X, ALU.min))
                    link(V.tensor_scalar(tie, imp, m1[:, 0:1], None, ALU.is_equal))
                    link(V.tensor_tensor(tie, tie, C("blk_idx"), ALU.mult))
                    link(V.tensor_reduce(m1[:, 1:2], tie, AX.X, ALU.max))
                    link(V.tensor_scalar(drop, C("blk_idx"), m1[:, 1:2], NEG, ALU.is_equal, ALU.mult))
                    ps = full(dve, ("Oc", l, hf))
                    V.tensor_copy(orow[:, 0, :], ps[:, 0:P]).then_inc(free(("Oc", l, hf)), 1)
                    for br, ncol in ((1, PAST), (2, WIN)):
                        for c in range(ncol // 512):
                            ps = full(dve, ("Ss", l, hf, br, c))
                            V.tensor_scalar(S_s[:, 512 * c:512 * c + 512], ps[:, 0:512], HD ** -0.5, None, ALU.mult)\
                                .then_inc(free(("Ss", l, hf, br, c)), 1)
                        ps = full(dve, ("Sn", l, hf, br))
                        V.scalar_tensor_tensor(S_s[:, ncol:ncol + TS], ps[:, 0:TS], HD ** -0.5,
                                               C("new_mask")[:, hf * TS:(hf + 1) * TS], ALU.mult, ALU.add)\
                            .then_inc(free(("Sn", l, hf, br)), 1)
                        after(("Sn", l, hf, br))
                        if br == 1:
                            mid = S_s[:, SEL:SEL * (NMID + 1)].rearrange("p (b k) -> p b k", k=SEL)
                            link(V.tensor_tensor(mid, mid, bc(drop, 2, SEL), ALU.add))
                        else:
                            link(V.tensor_tensor(S_s[:, 0:TD], S_s[:, 0:TD], C("win_mask"), ALU.add))
                        V.tensor_reduce(smx[:, br:br + 1], S_s[:, 0:ncol + TS], AX.X, ALU.max, negate=True).then_inc(S["ssmax"], 1)
                        ready(dve, "ss_exp", 2 * it + br)
                        link(V.reciprocal(srs[:, br:br + 1], ssm[:, br:br + 1]))
                        ps = full(dve, ("Os", l, hf, br))
                        V.tensor_scalar(orow[:, br, :], ps[:, 0:P], srs[:, br:br + 1], None, ALU.mult)\
                            .then_inc(free(("Os", l, hf, br)), 1)
                        after(("Os", l, hf, br))
                    signal("orow_ready")
                    ps = full(dve, ("oT", l, hf))
                    for g in range(NKV):
                        gd = slice(HD * g, HD * g + HD)
                        acc = [osam[gd, k, :].rearrange("p (b r t) -> p b r t", b=HALF, r=GRP) for k in range(2)]
                        for br in range(3):
                            o = ps[gd, br * P:(br + 1) * P].rearrange("p (b q) -> p b q", b=HALF)[:, :, 16 * g:16 * g + 16]\
                                .rearrange("p b (r t) -> p b r t", r=GRP)
                            gt = gB[gd, br, :, 16 * hf:16 * hf + 16].rearrange("p r (b t) -> p b r t", b=HALF)
                            last = V.tensor_tensor(acc[0 if br == 0 else 1], o, gt, ALU.mult)
                            if br == 2 and g == NKV - 1:
                                last.then_inc(free(("oT", l, hf)), 1)
                                after(("oT", l, hf))
                            else:
                                link(last)
                            if br == 1:
                                link(V.tensor_tensor(acc[0], acc[0], acc[1], ALU.add))
                            if br == 2:
                                t0 = TP + 16 * hf
                                link(V.tensor_tensor(oN[gd, :, t0:t0 + 16].rearrange("p r (b t) -> p b r t", b=HALF),
                                                     acc[0], acc[1], ALU.add))

                dve.wait_ge(S["kv_done"], 16 * (l + 1))
                link(V.tensor_tensor(tmp_[:, 0:24].rearrange("p (a b) -> p a b", a=3), small[:, :, 24:32],
                                     bc(PR(l, "dt_bias", 0, NH), 1, 3), ALU.add))
                V.tensor_copy(sp_v, tmp_[:, 0:24].rearrange("p (a b) -> p a b", a=3)).then_inc(S["attn_done"], 1)
                dve.wait_ge(S["attn_done"], l + 1)
                link(V.tensor_scalar(sp_e, sp_v, -1.0, None, ALU.mult))
                V.tensor_tensor(sp_e, sp_e, sp_v, ALU.max).then_inc(S["spa"], 1)
                ready(dve, "sp_exp", l + 1)
                link(V.tensor_scalar(sp_z, sp_e, 2.0, None, ALU.add))
                link(V.reciprocal(sp_z, sp_z))
                link(V.tensor_tensor(sp_z, sp_z, sp_e, ALU.mult))
                link(V.tensor_tensor(sp_q, sp_z, sp_z, ALU.mult))
                link(V.tensor_scalar(sp_p, sp_q, 1.0 / 13, None, ALU.mult))
                for k in (11, 9, 7, 5, 3):
                    link(V.scalar_tensor_tensor(sp_p, sp_p, 1.0 / k, sp_q, ALU.add, ALU.mult))
                link(V.scalar_tensor_tensor(sp_p, sp_p, 1.0, sp_z, ALU.add, ALU.mult))
                link(V.tensor_scalar(sp_v, sp_v, 0.0, None, ALU.max))
                link(V.scalar_tensor_tensor(dt, sp_p, 2.0, sp_v, ALU.mult, ALU.add))
                ready(dve, "ea_ready", l + 1)
                link(V.scalar_tensor_tensor(dta, dt, -1.0, bc(ea, 1, 3), ALU.mult, ALU.mult))

                ready(dve, "xbc_ready", l + 1)
                ready(dve, "st_in", 32 * (l + 1))
                link(V.memset(xbcp[:, :, 0:3], 0.0))
                for j in range(6):
                    last = V.tensor_copy(xbcp[:, j, 3 + TP:].rearrange("p (b k) -> p b k", b=NB)[:, :, 0:3],
                                         cv_st[:, j, :].rearrange("p (b k) -> p b k", b=NB))
                link(last)

                def conv(src, dst, pad, width, tiles, w, bias):
                    for k in range(width):
                        for j in range(tiles):
                            pin, pout = src[:, j, k:k + TP], dst[:, j, 0:TP]
                            sin_ = src[:, j, pad + TP:].rearrange("p (b k) -> p b k", b=NB)[:, :, k:k + TD]
                            sout = dst[:, j, TP:T].rearrange("p (b k) -> p b k", b=NB)
                            wk = PR(l, w, k * tiles + j)
                            for a, o in ((pin, pout), (sin_, sout)):
                                if k == 0:
                                    last = V.tensor_scalar(o, a, wk, None, ALU.mult)
                                else:
                                    last = V.scalar_tensor_tensor(o, a, wk, o, ALU.mult, ALU.add)
                        link(last)
                    if bias:
                        for j in range(tiles):
                            last = V.tensor_scalar(dst[:, j, :], dst[:, j, :], PR(l, bias, j), None, ALU.add)
                        link(last)

                conv(xbcp, xbcc, 3, 4, 6, "conv_w", "conv_b")
                signal("xbcc_raw")
                ready(dve, "scc_ready", l + 1)
                link(V.memset(chp[:, :, 0:2], 0.0))
                for j in range(4):
                    V.tensor_copy(chp[:, j, 2 + TP:].rearrange("p (b k) -> p b k", b=NB)[:, :, 0:2],
                                  sc_st[:, j, :].rearrange("p (b k) -> p b k", b=NB))
                    ps = full(dve, ("in", l, 24 + j))
                    V.tensor_tensor(chp[:, j, 2:2 + TP], ps[:, 0:TP], scc[:, j, 0:TP], ALU.mult)
                    V.tensor_tensor(chp[:, j, 2 + TP:].rearrange("p (b k) -> p b k", b=NB)[:, :, 2:],
                                    ps[:, TP:T].rearrange("p (b k) -> p b k", b=NB),
                                    scc[:, j, TP:T].rearrange("p (b k) -> p b k", b=NB), ALU.mult)\
                        .then_inc(free(("in", l, 24 + j)), 1)
                after(("in", l, 27))
                signal("cols_ready")
                conv(chp, scc, 2, 3, 4, "sc_w", None)
                ready(dve, "scb_ready", l + 1)
                V.tensor_tensor(oC, oC, scc, ALU.mult).then_inc(S["oC_ready"], 1)
                dve.wait_ge(S["oC_ready"], l + 1)
                dve.wait_ge(S["cc_done"], 320 * (l + 1))
                signal("sc_conv")

                for c in range(NCHUNK):
                    t0, n = TILES[c]
                    cc = NCHUNK * l + c
                    w = NH * n
                    d3 = decay[0:n, 0:w].rearrange("p (h t) -> p h t", h=NH)
                    up = C("upto0") if c < 2 else C("upto2", TS)
                    mk = C("decay_mask0") if c < 2 else C("decay_mask2", TS)
                    V.tensor_tensor(d3, bc(up, 1, NH), bc(dta[0:n, c, :], 2, n), ALU.mult).then_inc(S["dD_ready"], 1)
                    ps = full(dve, ("ac", cc))
                    V.tensor_copy(acs[0:n, :], ps[0:n, 0:2 * NH]).then_inc(free(("ac", cc)), 1)
                    after(("ac", cc))
                    V.tensor_tensor(tail[0:n, :], acs[0:n, NH:], acs[0:n, 0:NH], ALU.subtract).then_inc(S["tl_sub"], 1)
                    for part in range(2 if c < 2 else 1):
                        ps = full(dve, ("acB", cc, part))
                        w2 = min(512, w)
                        V.tensor_copy(eB[:, part * 512:part * 512 + w2], ps[:, 0:w2]).then_inc(free(("acB", cc, part)), 1)
                    after(("acB", cc, 1 if c < 2 else 0))
                    link(V.tensor_tensor(d3, eB[0:n, 0:w].rearrange("p (h t) -> p h t", h=NH), bc(acs[0:n, 0:NH], 2, n), ALU.subtract))
                    V.tensor_tensor(d3, d3, bc(mk, 1, NH), ALU.add).then_inc(S["seg_ready"], 1)
                    ps = full(dve, ("xtok", cc))
                    V.tensor_tensor(xdt[0:n, :].rearrange("p (h d) -> p h d", h=NH), ps[0:n, 0:512].rearrange("p (h d) -> p h d", h=NH),
                                    bc(dt[0:n, c, :], 2, HD), ALU.mult).then_inc(free(("xtok", cc)), 1)
                    after(("xtok", cc))
                    ready(dve, "tl_ready", cc + 1)
                    V.tensor_tensor(xtl[0:n, :].rearrange("p (h d) -> p h d", h=NH), xdt[0:n, :].rearrange("p (h d) -> p h d", h=NH),
                                    bc(tail[0:n, :], 2, HD), ALU.mult).then_inc(S["xdt_ready"], 1)
                    ready(dve, "dec_exp", cc + 1)
                    for g in range(NKV):
                        ps = full(dve, ("CB", cc, g))
                        V.tensor_tensor(d3[:, 4 * g:4 * g + 4, :], d3[:, 4 * g:4 * g + 4, :],
                                        bc(ps[0:n, 0:n], 1, GRP), ALU.mult).then_inc(free(("CB", cc, g)), 1)
                    after(("CB", cc, 1))
                    signal("dec_ready")
                    ready(dve, "eb_ready", cc + 1)
                    if c == 2:
                        ready(dve, "hs_in", 16 * (l + 1))
                    if c > 0:
                        for g in range(NKV):
                            gd = slice(HD * g, HD * g + HD)
                            last = V.tensor_tensor(cp[gd, 0:GRP * n].rearrange("p (h t) -> p h t", h=GRP),
                                                   bc(xbcc[gd, 5, t0:t0 + n], 1, GRP),
                                                   eB[gd, g * GRP * n:(g + 1) * GRP * n].rearrange("p (h t) -> p h t", h=GRP), ALU.mult)
                        last.then_inc(S["cp_ready"], 1)
                    if c == 2:
                        ready(dve, "btok_ready", cc + 1)
                        V.tensor_tensor(bm[0:n, :, :], bc(btok[0:n, :], 1, NB), bc(C("in_batch", TS), 2, P), ALU.mult)\
                            .then_inc(S["bm_ready"], 1)
                    ready(dve, "xbcc_ready", l + 1)
                    for g in range(NKV):
                        ps = full(dve, ("y", cc, g))
                        for j in range(2):
                            last = V.scalar_tensor_tensor(oS[:, 2 * g + j, t0:t0 + n], xbcc[:, 2 * g + j, t0:t0 + n],
                                                          PR(l, "ssm_d", 2 * g + j), ps[:, j * n:(j + 1) * n], ALU.mult, ALU.add)
                        last.then_inc(free(("y", cc, g)), 1)
                    if c < 2:
                        ps = full(dve, ("hd", cc))
                        for g in range(NKV):
                            gd = slice(HD * g, HD * g + HD)
                            new = ps[gd, 0:256].rearrange("p (h d) -> p h d", h=GRP)
                            if c == 0:
                                last = V.tensor_copy(hT[gd, :, :], new)
                            else:
                                e3 = eB[gd, 0:w].rearrange("p (h t) -> p h t", h=NH)[:, 4 * g:4 * g + 4, n - 1]
                                link(V.tensor_tensor(hT[gd, :, :], hT[gd, :, :], bc(e3, 2, HD), ALU.mult))
                                last = V.tensor_tensor(hT[gd, :, :], hT[gd, :, :], new, ALU.add)
                        last.then_inc(free(("hd", cc)), 1)
                        after(("hd", cc))
                        signal("h_ready")
                    else:
                        full(dve, ("hsd", l, 0))
                        for g in range(NKV):
                            gd = slice(HD * g, HD * g + HD)
                            e4 = eB[gd, 0:w].rearrange("p (h b t) -> p h b t", h=NH, b=NB)[:, 4 * g:4 * g + 4, :, TD - 1]
                            last = V.tensor_tensor(hs[gd, :, :, :], hs[gd, :, :, :],
                                                   bc(e4.rearrange("p h b -> p b h"), 3, HD), ALU.mult)
                        link(last)
                        for b2 in range(NB // 2):
                            ps = full(dve, ("hsd", l, b2))
                            hv = hs[:, 2 * b2:2 * b2 + 2, :, :]
                            V.tensor_tensor(hv, hv, ps[:, 0:512].rearrange("p (b h d) -> p b h d", b=2, h=GRP), ALU.add)\
                                .then_inc(free(("hsd", l, b2)), 1)
                        after(("hsd", l, 3))
                V.tensor_tensor(oS, oS, zs, ALU.mult).then_inc(S["y_ready"], 1)
                dve.wait_ge(free(("yss", l)), use_of[("yss", l)] // 8 + 1)
                link(V.reciprocal(std[:, :], std[:, :]))
                for j in range(4):
                    last = V.scalar_tensor_tensor(oS[:, j, :], oS[:, j, :], PR(l, "ssm_norm", j), std[:, :], ALU.mult, ALU.mult)
                last.then_inc(S["oS_ready"], 1)
                signal("mix_done")

                for m in range(KD):
                    for k3 in range(3):
                        g_u = use_of[("gate", l, m, k3)]
                        dve.wait_ge(bank_free[g_u % 8], g_u // 8 + 1)
                        gate = gs_[:, (m % 2) * 3 + k3, :]
                        ps = full(dve, ("proj", l, m, k3))
                        dst = tmp[:, m, :] if k3 == 0 else gate
                        V.tensor_tensor(dst, ps[:, 0:T], gate, ALU.mult).then_inc(free(("proj", l, m, k3)), 1)
                        if k3:
                            after(("proj", l, m, k3))
                            ins = V.tensor_tensor(tmp[:, m, :], tmp[:, m, :], gate, ALU.add)
                            if k3 == 2:
                                ins.then_inc(S["gate_sig"], 1)
                            else:
                                link(ins)
                signal("merged_ready")
                for m in range(KD):
                    ps = full(dve, ("o", l, m))
                    V.tensor_tensor(xT[:, m, :], xT[:, m, :], ps[:, 0:T], ALU.add).then_inc(free(("o", l, m)), 1)
                signal("x_ready")
                rms(l, 1, "norm_ffn")
                if l == 0:
                    for f in range(NFD):
                        g_u = use_of[("fg", f)]
                        dve.wait_ge(bank_free[g_u % 8], g_u // 8 + 1)
                        ps = full(dve, ("fu", f))
                        V.tensor_tensor(h[:, f, :], gs_[:, f % 2, :], ps[:, 0:T], ALU.mult).then_inc(free(("fu", f)), 1)
                    for m in range(KD):
                        ps = full(dve, ("fd", m))
                        V.tensor_tensor(xT[:, m, :], xT[:, m, :], ps[:, 0:T], ALU.add).then_inc(free(("fd", m)), 1)
                    signal("x_ready")
                    after(("fd", 7))

            link(V.memset(rl, 0.0))
            ps = full(dve, ("router",))
            V.tensor_copy(rl[0:TS, 2, :], ps[0:TS, 16:24])
            V.tensor_copy(rl[:, 0:2, :], ps[:, 0:16].rearrange("p (a b) -> p a b", a=2)).then_inc(free(("router",)), 1)
            after(("router",))
            rank = bc(C("exp_rank"), 1, 3)

            def best(src, sel, m):
                link(V.tensor_reduce(m, src, AX.X, ALU.max))
                link(V.tensor_tensor(sel, src, m.to_broadcast([P, 3, NE]), ALU.is_equal))
                link(V.tensor_tensor(sel, sel, rank, ALU.mult))
                link(V.tensor_reduce(rg1, sel, AX.X, ALU.max))
                link(V.tensor_tensor(sel, rank, rg1.to_broadcast([P, 3, NE]), ALU.is_equal))

            best(rl, rs1, rm1)
            link(V.scalar_tensor_tensor(rl2, rs1, NEG, rl, ALU.mult, ALU.add))
            best(rl2, rs2, rm2)
            V.tensor_tensor(re, rm2, rm1, ALU.subtract).then_inc(S["re_sub"], 1)
            ready(dve, "re_exp", 1)
            link(V.tensor_scalar(rg1, re, 1.0, None, ALU.add))
            link(V.reciprocal(rg1, rg1))
            link(V.tensor_tensor(rg2, re, rg1, ALU.mult))
            link(V.tensor_tensor(rt, rs1, rg1.to_broadcast([P, 3, NE]), ALU.mult))
            link(V.tensor_tensor(rs2, rs2, rg2.to_broadcast([P, 3, NE]), ALU.mult))
            V.tensor_tensor(rt, rt, rs2, ALU.add).then_inc(S["comb_ready"], 1)
            ready(dve, "cb_ready", 1)
            with dve.Fori(0, NE) as e:
                for f in range(NFE):
                    g_u = use_of[("eg", f)]
                    dve.wait_ge(bank_free[g_u % 8], e * (MOE_USES // 8) + g_u // 8 + 1)
                    ps = full(dve, ("eu", f), e)
                    V.tensor_tensor(h[:, f, :], gs_[:, f % 2, :], ps[:, 0:T], ALU.mult).then_inc(free(("eu", f)), 1)
                for m in range(KD):
                    ps = full(dve, ("ed", m), e)
                    V.tensor_tensor(gs_[:, 2 + m % 2, :], ps[:, 0:T], cb[:, bass.ds(e, 1), :].rearrange("p a t -> p (a t)"), ALU.mult)\
                        .then_inc(free(("ed", m)), 1)
                    u = use_of[("ed", m)]
                    dve.wait_ge(bank_free[u % 8], e * (MOE_USES // 8) + u // 8 + 1)
                    last = V.tensor_tensor(xT[:, m, :], xT[:, m, :], gs_[:, 2 + m % 2, :], ALU.add)
            signal("x_ready")


def blocks(w):
    K, N = w.shape
    return w.reshape(K // P, P, N // P, P).transpose(2, 0, 1, 3)


def head_tiles(cols):
    return cols.reshape(NKV, GRP, HD).transpose(1, 0, 2).reshape(-1)


def weight_stream(a):
    out = np.empty((N_SLOTS * BPS, P, P), np.float32)
    at = 0

    def put(b):
        nonlocal at
        b = b.reshape(-1, P, P)
        out[at:at + len(b)] = b
        at += len(b)

    for l in range(DEPTH):
        w = a["w_in"][l]
        q = w[:, 0:512][:, head_tiles(np.arange(512))]
        kv = w[:, 512:1280].reshape(D, 3, 2, P)
        put(blocks(q))
        put(blocks(kv[:, :, 0].reshape(D, 3 * P)))
        put(blocks(kv[:, :, 1].reshape(D, 3 * P)))
        cm = np.zeros((2, 32, P, P), np.float32)
        for g in range(NKV):
            cm[:, :, g * HD:(g + 1) * HD, g * HD:(g + 1) * HD] = a["w_cmp"][l]
        put(cm)
        put(cm)
        put(blocks(w[:, 1816:2584]))
        put(blocks(w[:, 1304:1816]))
        put(blocks(w[:, 3104:3616]))
        put(blocks(w[:, 3616:4128]))
        put(blocks(w[:, 2592:3104]))
        mg = blocks(w[:, 4128:]).reshape(3, KD, KD, P, P)
        wb = a["w_branch"][l]
        br = np.stack([blocks(wb[0][head_tiles(np.arange(512))]), blocks(wb[1]), blocks(wb[2])])
        for m in range(KD):
            put(mg[:, m])
            put(br[:, m])
        put(blocks(a["w_out"][l]))
        if l == 0:
            put(np.stack([blocks(a["ffn_w_gate"][0]), blocks(a["ffn_w_up"][0])], 1))
            put(blocks(a["ffn_w_down"][0]))
    for e in range(NE):
        put(np.stack([blocks(a["moe_w_gate"][0, e]), blocks(a["moe_w_up"][0, e])], 1))
        put(blocks(a["moe_w_down"][0, e]))
    assert at == len(out)
    return np.ascontiguousarray(out.reshape(N_SLOTS, BPS, P, P).transpose(0, 2, 1, 3)).reshape(N_SLOTS, P, SLOTF)


def feature_cols(v, n):
    return v.reshape(-1, P).T.reshape(P, -1)


def layer_params(a):
    out = np.zeros((P, DEPTH, N_PAR), np.float32)

    def put(l, name, v):
        at, n = PAR_AT[name]
        out[:, l, at:at + n] = v.reshape(P, n)

    for l in range(DEPTH):
        put(l, "norm_mix", feature_cols(a["norm_mix"][l], KD))
        put(l, "norm_ffn", feature_cols(a["norm_ffn"][l], KD))
        qk = np.concatenate([np.tile(a["q_norm"][l], (4, 2)), np.tile(a["k_norm"][l], (1, 2))])
        put(l, "qk_norm", np.ascontiguousarray(qk.T))
        put(l, "conv_w", feature_cols(a["ssm_conv_w"][l], 6))
        put(l, "conv_b", feature_cols(a["ssm_conv_b"][l], 6))
        put(l, "ssm_d", feature_cols(np.repeat(a["ssm_d"][l], HD), 4))
        put(l, "ssm_norm", feature_cols(a["ssm_norm"][l], 4))
        put(l, "sc_w", feature_cols(a["sc_conv_w"][l], 4))
        put(l, "dt_bias", np.tile(a["ssm_dt_bias"][l], (P, 1)))
        put(l, "a_log", np.tile(a["ssm_a_log"][l], (P, 1)))
        w = a["w_in"][l]
        sm = np.concatenate([w[:, 1280:1304], w[:, 2584:2592]], 1)
        put(l, "w_small", np.ascontiguousarray(sm.reshape(KD, P, 32).transpose(1, 0, 2)))
        if l == 1:
            put(l, "router", np.ascontiguousarray(a["moe_router"][0].reshape(KD, P, NE).transpose(1, 0, 2)))
    return out.reshape(P, -1)


def kernel(**inputs):
    import concourse.bacc as bacc
    from concourse.bass_utils import run_bass_kernel_spmd

    a = {k: np.asarray(v) for k, v in inputs.items()}
    nc = bacc.Bacc("TRN2", target_bir_lowering=False, num_devices=1)
    arrays, args = {}, []

    def ext(name, arr):
        arr = np.ascontiguousarray(arr)
        arrays["in_" + name] = arr
        args.append(nc.dram_tensor("in_" + name, arr.shape, mybir.dt.from_np(arr.dtype), kind="ExternalInput").ap())

    def out(name, shape):
        args.append(nc.dram_tensor("out_" + name, shape, mybir.dt.float32, kind="ExternalOutput").ap())

    x = np.concatenate([a["x_prompt"].reshape(TP, D), a["x_sample"].reshape(TS, D)])
    ext("xT", x.reshape(T, KD, P).transpose(2, 1, 0).reshape(P, -1))
    ext("consts", np.concatenate([np.ascontiguousarray(v) for v in CONST.values()], 1))
    ext("params", layer_params(a))
    ext("wstream", weight_stream(a))
    ext("page_table", a["page_table"].reshape(1, -1))
    pg = a["cache_nsa_pages"]
    n_pool = pg.shape[1]
    pg = pg.reshape(DEPTH * n_pool, PAGE, 4, P)
    ext("kc_pages", pg[:, :, 0].transpose(0, 2, 1))
    ext("vc_pages", pg[:, :, 1].transpose(0, 2, 1))
    ext("slc_pages", np.stack([pg[:, :, 2].transpose(0, 2, 1), pg[:, :, 3]], 2).reshape(DEPTH * n_pool, P, 2 * P))
    win = a["cache_nsa_window"].reshape(DEPTH, NB, WIN, 2, P)
    ext("win_kT", win[:, :, :, 0].transpose(0, 3, 1, 2))
    ext("win_v", win[:, :, :, 1].reshape(DEPTH, NB, 4, P, P).transpose(0, 1, 3, 2, 4))
    ext("win_rows", win.reshape(DEPTH, NB, WIN, 2 * P))
    st = a["state_ssm"].reshape(DEPTH, NB, NKV, GRP, HD, SSMN).transpose(0, 2, 5, 1, 3, 4)
    ext("ssm_in", st.reshape(DEPTH, P, NB, GRP, HD))
    ext("conv_in", a["state_ssm_conv"].reshape(DEPTH, NB, 3, 6, P).transpose(0, 4, 3, 1, 2).reshape(DEPTH, P, 6, NB * 3))
    ext("sc_in", a["state_shortconv"].reshape(DEPTH, NB, 2, 4, P).transpose(0, 4, 3, 1, 2).reshape(DEPTH, P, 4, NB * 2))
    out("y", (P, KD * T))
    out("kv", (DEPTH, P, 6, T))
    out("win_keep", (DEPTH, NB, WIN - TD, 2 * P))
    out("ssm_p", (DEPTH, P, GRP, HD))
    out("ssm_s", (DEPTH, P, NB, GRP, HD))
    out("conv_last", (DEPTH, P, 6, 3 + NB * 3))
    out("sc_last", (DEPTH, P, 4, 2 + NB * 2))
    build(nc, *args)
    res = run_bass_kernel_spmd(nc, [arrays], core_ids=[0]).results[0]
    r = {k[4:]: res[k] for k in res if k.startswith("out_")}

    y = r["y"].reshape(P, KD, T).transpose(2, 1, 0).reshape(T, D)
    kv = r["kv"].reshape(DEPTH, NKV, HD, 2, 3, T).transpose(0, 5, 4, 3, 1, 2)
    rows = kv[:, :, 0:2].reshape(DEPTH, T, 4, NKV, HD)
    wkv = kv[:, :, 2]
    nsa_p = np.ascontiguousarray(rows[:, :TP]).reshape(DEPTH, 1, TP, 4, NKV, HD)
    nsa_s = np.ascontiguousarray(rows[:, TP:]).reshape(DEPTH, NB, TD, 4, NKV, HD)
    win_p = np.ascontiguousarray(wkv[:, :TP]).reshape(DEPTH, 1, TP, 2, NKV, HD)
    win_s = np.concatenate([r["win_keep"].reshape(DEPTH, NB, WIN - TD, 2, NKV, HD),
                            wkv[:, TP:].reshape(DEPTH, NB, TD, 2, NKV, HD)], 2)
    ssm_p = r["ssm_p"].reshape(DEPTH, NKV, SSMN, GRP, HD).transpose(0, 1, 3, 4, 2).reshape(DEPTH, 1, NH, HD, SSMN)
    ssm_s = r["ssm_s"].reshape(DEPTH, NKV, SSMN, NB, GRP, HD).transpose(0, 3, 1, 4, 5, 2).reshape(DEPTH, NB, NH, HD, SSMN)
    cl = r["conv_last"]
    conv_p = cl[:, :, :, 0:3].transpose(0, 3, 2, 1).reshape(DEPTH, 1, 3, XBC)
    conv_s = cl[:, :, :, 3:].reshape(DEPTH, P, 6, NB, 3).transpose(0, 3, 4, 2, 1).reshape(DEPTH, NB, 3, XBC)
    sl = r["sc_last"]
    sc_p = sl[:, :, :, 0:2].transpose(0, 3, 2, 1).reshape(DEPTH, 1, 2, SC)
    sc_s = sl[:, :, :, 2:].reshape(DEPTH, P, 4, NB, 2).transpose(0, 3, 4, 2, 1).reshape(DEPTH, NB, 2, SC)
    return tuple(np.ascontiguousarray(v) for v in (
        y[:TP].reshape(1, TP, D), y[TP:].reshape(NB, TD, D), nsa_p, nsa_s, win_p, win_s, ssm_p, ssm_s,
        conv_p, conv_s, sc_p, sc_s))
```

```python
import math
from contextlib import ExitStack

import numpy as np
import concourse.bass as bass
from concourse import mybir

D, DEPTH = 1024, 2
TP, NB, TD = 256, 8, 4
TS = NB * TD
T = TP + TS
PAST, PAGE, WIN = 1024, 128, 512
NPG = PAST // PAGE
NH, NKV, HD, GRP = 8, 2, 64, 4
STRIDE, NCS, NCP = 16, 63, 15
SEL, NMID = 64, 14
SSMI, SSMN, XBC, SC = 512, 64, 768, 512
FF, FE, NE = 2816, 3584, 8
EPS, NEG = 1e-6, -1e30
P = 128
KD = D // P
HALF = NB // 2

BPS = 16
RING = 6
MARKS = 32
CAP = 96
MAX_PASSES = NE + 2 * (TP + NB * TD) // (CAP + 1)
SLOTF = BPS * P
NQKV, NREST = 10, 22
NCMPB = 64
MIX_BLOCKS = NQKV * KD + 2 * NCMPB + NREST * KD + 3 * KD * KD + 12 * KD + KD * KD
NFD, NFE = FF // P, FE // P
FFN_BLOCKS = NFD * 3 * KD
EXP_BLOCKS = NFE * 3 * KD
PRE_SLOTS = (2 * MIX_BLOCKS + FFN_BLOCKS) // BPS
EXP_SLOTS = EXP_BLOCKS // BPS
N_SLOTS = PRE_SLOTS + NE * EXP_SLOTS
assert (MIX_BLOCKS % BPS, FFN_BLOCKS % BPS, EXP_BLOCKS % BPS, EXP_SLOTS % RING) == (0, 0, 0, 0)

TILES = [(0, 128), (128, 128), (256, 32)]
NCHUNK = 3


def constants():
    c = {}
    eye = np.eye(P, dtype=np.float32)
    i = np.arange(P)
    c["ident"] = eye
    c["ones"] = np.ones((P, P), np.float32)
    c["head_ones"] = (i[:, None] // HD == i[None, :] // HD).astype(np.float32)
    rot = np.zeros((P, P), np.float32)
    for m in range(P):
        if m % HD < HD // 2:
            rot[m + HD // 2, m] = -1.0
        else:
            rot[m - HD // 2, m] = 1.0
    c["rot"] = rot
    row_b, row_g, row_r, row_t = i // 32, i // 16 % 2, i // 4 % 4, i % 4
    grp = row_b * 8 + row_g * 4 + row_t
    c["group_sum"] = (grp[:, None] == grp[None, :]).astype(np.float32)
    half = HD // 2
    inv = np.exp(np.float32(-math.log(10000.0)) * np.arange(half, dtype=np.float32) / np.float32(half)).astype(np.float32)
    pos = np.concatenate([np.arange(TP), PAST + np.tile(np.arange(TD), NB)]).astype(np.float32)
    ang = (pos[None, :] * inv[i % half][:, None]).astype(np.float32)
    c["cos"], c["sin"] = np.cos(ang).astype(np.float32), np.sin(ang).astype(np.float32)
    c["causal0"] = np.where(i[None, :] <= i[:, None], 0, NEG).astype(np.float32)
    c["causal1"] = np.where(np.arange(TP)[None, :] <= i[:, None] + P, 0, NEG).astype(np.float32)
    end = np.arange(NCP) * STRIDE + 31
    qp = i[:, None] + P * np.arange(2)[None, :]
    vis = end[None, None, :] <= qp[:, :, None]
    c["cmp_mask"] = np.where(vis, 0, NEG).astype(np.float32).reshape(P, -1)
    c["cmp_any"] = vis.any(-1).astype(np.float32)
    tb, tt = np.arange(TS) // TD, np.arange(TS) % TD
    new = [np.where((tb[None, :] == (row_b + HALF * h)[:, None]) & (tt[None, :] <= row_t[:, None]), 0, NEG) for h in range(2)]
    c["new_mask"] = np.concatenate(new, 1).astype(np.float32)
    c["win_mask"] = np.where(np.arange(TD)[None, :] > row_t[:, None], 0, NEG).astype(np.float32)
    c["blk_idx"] = np.broadcast_to(np.arange(1, NMID + 1, dtype=np.float32), (P, NMID))
    c["upto0"] = (i[:, None] <= i[None, :]).astype(np.float32)
    c["decay_mask0"] = ((1 - c["upto0"]) * NEG).astype(np.float32)
    same = tb[:, None] == tb[None, :]
    up = np.zeros((P, TS), np.float32)
    up[:TS] = same & (tt[:, None] <= tt[None, :])
    c["upto2"] = up
    c["decay_mask2"] = ((1 - up) * NEG).astype(np.float32)
    sb = np.zeros((P, TS), np.float32)
    sb[:TS] = same
    c["same2"] = sb
    bc = np.zeros((P, NB), np.float32)
    bc[:TS] = tb[:, None] == np.arange(NB)[None, :]
    c["in_batch"] = bc
    c["iota"] = np.broadcast_to(np.arange(T, dtype=np.float32), (P, T))
    c["before"] = (i[:, None] < i[None, :]).astype(np.float32)
    c["exp_rank"] = np.broadcast_to(NE - np.arange(NE, dtype=np.float32), (P, NE))
    sel = np.zeros((P, 12, P), np.float32)
    for br in range(3):
        for r in range(GRP):
            for g in range(NKV):
                sel[(g * GRP + r) * 3 + br, br * GRP + r, g * HD:(g + 1) * HD] = 1
    c["gate_sel"] = sel.reshape(P, -1)
    c["eps"] = np.full((P, 1), EPS, np.float32)
    return c


CONST = constants()
CONST_AT, _n = {}, 0
for _k, _v in CONST.items():
    CONST_AT[_k] = (_n, _v.shape[1])
    _n += _v.shape[1]
N_CONST = _n

PAR = {"norm_mix": KD, "norm_ffn": KD, "qk_norm": 7, "conv_w": 4 * 6, "conv_b": 6, "ssm_d": 4, "ssm_norm": 4,
       "sc_w": 3 * 4, "dt_bias": NH, "a_log": NH, "w_small": KD * 32, "router": KD * NE}
PAR_AT, _n = {}, 0
for _k, _v in PAR.items():
    PAR_AT[_k] = (_n, _v)
    _n += _v
N_PAR = _n

XBCW = 3 + TP + NB * (3 + TD)
SCW = 2 + TP + NB * (2 + TD)


def build(nc, xT_in, consts, params, wstream, page_table, kc_pages, vc_pages, slc_pages, win_kT, win_v, win_rows,
          ssm_in, conv_in, sc_in, y_out, kv_out, win_out, ssm_p_out, ssm_s_out, conv_out, sc_out):
    f32, i32 = mybir.dt.float32, mybir.dt.int32
    ALU, ACT, AX = mybir.AluOpType, mybir.ActivationFunctionType, mybir.AxisListType
    V, A = nc.vector, nc.scalar

    with ExitStack() as ctx:
        def sb(name, cols, dt=f32):
            return ctx.enter_context(nc.sbuf_tensor(name, [P, cols], dt))

        def sem(name):
            return ctx.enter_context(nc.semaphore(name))

        xT_ = sb("xT", KD * T)
        xn_ = sb("xn", KD * T)
        tmp_ = sb("tmp", KD * T)
        oN_ = sb("o_nsa", 4 * T)
        oS_ = sb("o_ssm", 4 * T)
        oC_ = sb("o_sc", 4 * T)
        wring = sb("wring", RING * SLOTF)
        pages = sb("pages", 3 * 4096)
        cst = sb("cst", N_CONST)
        par = sb("par", DEPTH * N_PAR)
        std = sb("std", T)
        mark = sb("mark", 2 * MARKS)
        REG = 12100
        reg = sb("phase_region", REG)
        ptab = sb("ptab", NB * NPG, i32)
        passes = sb("passes", 3 * 16, i32)

        def view(t, off, *dims):
            n = int(np.prod(dims))
            ap = t[:, off:off + n]
            if len(dims) == 2:
                ap = ap.rearrange("p (a b) -> p a b", b=dims[1])
            elif len(dims) == 3:
                ap = ap.rearrange("p (a b c) -> p a b c", b=dims[1], c=dims[2])
            elif len(dims) == 4:
                ap = ap.rearrange("p (a b c d) -> p a b c d", b=dims[1], c=dims[2], d=dims[3])
            return ap

        xT, xn, tmp = (view(t, 0, KD, T) for t in (xT_, xn_, tmp_))
        oN, oS, oC = (view(t, 0, 4, T) for t in (oN_, oS_, oC_))

        class Region:
            def __init__(self, at):
                self.at = at

            def __call__(self, *dims):
                ap = view(reg, self.at, *dims)
                self.at += int(np.prod(dims))
                assert self.at <= REG, self.at
                return ap

        ra = Region(0)
        qkv = ra(NQKV, T)
        vtok = ra(3, 3, P)
        otok = ra(2, GRP, NKV, HD)
        gates = ra(3, 24)
        small = ra(3, 32)
        gT = ra(TS)
        gB = ra(3, GRP, TS)
        kcT, vcT = ra(HALF, NCS), ra(HALF, NCS)
        kcTp, vcTp = ra(NCP + 1), ra(NCP + 1)
        vcp = ra(P)
        mx, ssum, rsum, coef = ra(2, GRP), ra(2, GRP), ra(GRP), ra(GRP)
        scratch = ra.at
        rq = view(reg, scratch, 7, T)
        rp = Region(scratch)
        S_p = [rp(1024), rp(1024)]
        PT_p = rp(2, 4 * P)
        otmp = rp(GRP, HD)
        rs_ = Region(scratch)
        qbd = rs_(NB, 32)
        vc = rs_(HALF, P)
        S_s = rs_(PAST + TS)
        PT_s = rs_(9, P)
        S_c = rs_(64)
        PT_c = rs_(P)
        imp, drop, tie, m1 = rs_(NMID), rs_(NMID), rs_(NMID), rs_(4)
        orow = rs_(3, P)
        smx, ssm, srs = rs_(4), rs_(4), rs_(4)
        osam = rs_(2, HALF * 16)
        rb = Region(0)
        dt = rb(3, NH)
        dta = rb(3, NH)
        sp_v, sp_e, sp_z, sp_q, sp_p = (rb(3, NH) for _ in range(5))
        ea = rb(NH)
        xbcp = rb(6, XBCW)
        xbcc = rb(6, T)
        zs = rb(4, T)
        b_scratch = rb.at
        rc = Region(b_scratch)
        scc = rc(4, T)
        chp = rc(4, SCW)
        sc_st = rc(4, NB * 2)
        cv_st = rc(6, NB * 3)
        rd = Region(b_scratch)
        decay = rd(1024)
        eB = rd(1024)
        cp = rd(GRP * P)
        xdt = rd(SSMI)
        xtl = rd(SSMI)
        btok = rd(P)
        hT = rd(GRP, HD)
        acs = rd(2 * NH)
        tail = rd(NH)
        hs = rd(NB, GRP, HD)
        bm = rd(NB, P)
        rf = Region(0)
        h = rf(NFD, T)
        gs_ = rf(6, T)
        rm = Region(0)
        xtok = rm(3, D)
        he = rm(NFE, CAP)
        xe = rm(KD, CAP)
        pick, pickw = rm(3, CAP), rm(3, CAP)
        spread = rm(T)
        yT, yS = rm(KD, CAP), rm(KD, P)
        sg = rm(2, 2 * CAP)
        rl, rl2, rs1, rs2, rt, rank, mask = (rm(3, NE) for k in range(7))
        rm1, rm2, re, rg1, rg2 = (rm(3, 1) for k in range(5))
        cnt, runs, en1, en2, en3 = (rm(NE) for k in range(5))
        le, lei = rm(16, NE), rm(16, NE)
        tabf = rm(3 * 16)

        def C(name, rows=P):
            a, n = CONST_AT[name]
            return cst[0:rows, a:a + n]

        def PR(l, name, i=0, n=1):
            a, _ = PAR_AT[name]
            a += l * N_PAR + i
            return par[:, a:a + n]

        def bc(ap, axis, n):
            a = ap.unsqueeze(axis)
            shape = list(a.shape)
            shape[axis] = n
            return a.to_broadcast(shape)

        psum = [ctx.enter_context(nc.psum_tensor(f"bank{i}", [P, 512], f32)) for i in range(8)]
        bank_full = [sem(f"bank_full{i}") for i in range(8)]
        bank_free = [sem(f"bank_free{i}") for i in range(8)]
        w_full = [sem(f"w_full{i}") for i in range(RING)]
        w_free = [sem(f"w_free{i}") for i in range(RING)]
        pg_full = [sem(f"pg_full{i}") for i in range(3)]
        names = ("const_in x_in ptab_in sq_ready xn_ready x_ready small_ready gates_ready qkv_ready qksq_ready "
                 "rq_ready qk_normed qk_ready vtok_ready vcT_ready vc_ready smax exp_ready pt_ready otok_ready "
                 "qbd_ready scmax sc_exp pc_ready ptc_ready ssmax ss_exp pts_ready orow_ready gT_ready attn_done "
                 "xbc_ready st_in xbcc_raw xbcc_ready scc_ready cols_ready spa sp_exp ea_ready dD_ready eb_ready "
                 "seg_ready dec_exp dec_ready tl_sub tl_ready cp_ready xdt_ready btok_ready h_ready bm_ready "
                 "y_ready ysq_ready oS_ready mix_done gate_sig merged_ready silu_ready cnt_ready pick_ready "
                 "table_ready zero_ready re_sub re_exp kv_done hp_done hs_done cc_done win_done dve_chain "
                 "act_chain pool_zero y_done oC_ready scb_ready sc_conv hs_in").split()
        S = {n: sem(n) for n in names}

        use_of = {}
        moe_base = [0]
        MOE_USES = 32
        assert MOE_USES % 8 == 0

        def filled(key, it=None):
            u = use_of[key]
            n = u // 8 + 1
            return bank_full[u % 8], n if it is None else it * (MOE_USES // 8) + n

        def released(key, it=None, back=0):
            u = use_of[key]
            n = u // 8 + 1 - back * (MOE_USES // 8)
            return bank_free[u % 8], n if it is None else it * (MOE_USES // 8) + n

        def bank_of(key):
            return psum[use_of[key] % 8]

        def free(key):
            return bank_free[use_of[key] % 8]

        DOWN = ((0, 3), (3, 3), (6, 2))

        FILLS = [(l, hf, what) for l in range(DEPTH) for hf in range(2) for what in ("kc", "vc", "slc0", "slc1", "win")]
        fill_dmas = {"kc": HALF * NPG, "vc": HALF * NPG, "slc0": 2 * NPG, "slc1": 2 * NPG, "win": 1 + HALF}
        fill_at, fill_sum = {}, [0, 0, 0]
        for n, f in enumerate(FILLS):
            fill_sum[n % 3] += 16 * fill_dmas[f[2]]
            fill_at[f] = (n % 3, fill_sum[n % 3])

        def page_slot(f):
            return 4096 * fill_at[f][0]

        UNITS = [(g, qt, br) for g in range(NKV) for qt in range(2) for br in range(3)]

        block = ctx.enter_context(nc.Block())

        @block.tensor
        def _(pe):
            uses = [0]
            blk = [0]
            last_slot = [-1]

            def bank(key):
                u = uses[0]
                uses[0] += 1
                use_of[key] = u
                if u >= 8:
                    pe.wait_ge(bank_free[u % 8], u // 8)
                return psum[u % 8], bank_full[u % 8]

            def wblock():
                n = blk[0]
                blk[0] += 1
                s, o = divmod(n, BPS)
                release = None
                if s != last_slot[0]:
                    pe.wait_ge(w_full[s % RING], 16 * (s // RING + 1))
                    if s > 0:
                        release = w_free[(s - 1) % RING]
                    last_slot[0] = s
                a = (s % RING) * SLOTF + o * P
                return wring[:, a:a + P], release

            def product(key, n, rhs, width=T, w=wblock):
                ps, done = bank(key)
                for k in range(n):
                    wb, release = w()
                    mm = nc.tensor.matmul(ps[:, 0:width], wb, rhs(k), start=(k == 0), stop=(k == n - 1))
                    if release is not None:
                        mm.then_inc(release, 1)
                mm.then_inc(done, 1)

            def column_sum(key, n, lhs, rhs):
                ps, done = bank(key)
                for k in range(n):
                    mm = nc.tensor.matmul(ps[:, 0:T], lhs, rhs(k), start=(k == 0), stop=(k == n - 1))
                mm.then_inc(done, 1)

            ident = C("ident")
            pe.wait_ge(S["const_in"], 32)
            for l in range(DEPTH):
                pe.wait_ge(S["sq_ready"], 2 * l + 1)
                column_sum(("ss", l, 0), KD, C("ones"), lambda k: tmp[:, k, :])
                pe.wait_ge(S["xn_ready"], 2 * l + 1)
                ps, done = bank(("small", l))
                for tt, (t0, n) in enumerate(TILES):
                    for k in range(KD):
                        mm = nc.tensor.matmul(ps[0:n, 32 * tt:32 * tt + 32], xn[:, k, t0:t0 + n],
                                              PR(l, "w_small", 32 * k, 32), start=(k == 0), stop=(k == KD - 1))
                mm.then_inc(done, 1)
                for i in range(NQKV):
                    product(("in", l, i), KD, lambda k: xn[:, k, :])
                pe.wait_ge(S["qksq_ready"], l + 1)
                for i in range(7):
                    column_sum(("qkss", l, i), 1, C("head_ones"), lambda k: tmp[:, i, :])
                pe.wait_ge(S["qkv_ready"], l + 1)
                for tt, (t0, n) in enumerate(TILES):
                    ps, done = bank(("vt", l, tt))
                    for br in range(3):
                        mm = nc.tensor.transpose(ps[0:n, br * P:(br + 1) * P], qkv[:, 7 + br, t0:t0 + n], ident)
                    mm.then_inc(done, 1)
                pe.wait_ge(S["gates_ready"], l + 1)
                ps, done = bank(("gT", l))
                nc.tensor.transpose(ps[0:24, 0:TS], gates[0:TS, 2, :], C("ident", TS)[:, 0:TS]).then_inc(done, 1)
                pe.wait_ge(S["gT_ready"], l + 1)
                ps, done = bank(("gB", l))
                for j in range(12):
                    mm = nc.tensor.matmul(ps[:, j * TS:(j + 1) * TS], C("gate_sel", 24)[:, j * P:(j + 1) * P],
                                          gT[0:24, :], start=True, stop=True)
                mm.then_inc(done, 1)
                pe.wait_ge(S["qk_normed"], l + 1)
                for i in range(7):
                    column_sum(("rot", l, i), 1, C("rot"), lambda k: qkv[:, i, :])

                def compress(hf):
                    for kind in range(2):
                        fill = (l, hf, ("kc", "vc")[kind])
                        pos, n = fill_at[fill]
                        pe.wait_ge(pg_full[pos], n)
                        src = view(pages, page_slot(fill), HALF, PAST // STRIDE, STRIDE)
                        ps, done = bank(("cmp", l, hf, kind))
                        if hf == 0:
                            if kind == 0:
                                pe.wait_ge(S["qk_ready"], l + 1)
                            ps2, done2 = bank(("cmpp", l, kind))
                            prm = qkv[:, (4, 7)[kind], 0:TP].rearrange("p (c j) -> p c j", j=STRIDE)
                        for j in range(32):
                            wb, release = wblock()
                            a, jj = divmod(j, STRIDE)
                            mm = nc.tensor.matmul(ps[:, 0:HALF * NCS].rearrange("p (b c) -> p b c", b=HALF), wb,
                                                  src[:, :, a:a + NCS, jj], start=(j == 0), stop=(j == 31))
                            if release is not None:
                                mm.then_inc(release, 1)
                            if j == 31:
                                mm.then_inc(done, 1)
                            if hf == 0:
                                mm = nc.tensor.matmul(ps2[:, 0:NCP], wb, prm[:, a:a + NCP, jj], start=(j == 0), stop=(j == 31))
                        if hf == 0:
                            mm.then_inc(done2, 1)

                compress(0)
                pe.wait_ge(S["vcT_ready"], 3 * l + 2)
                ps, done = bank(("vcp", l))
                nc.tensor.transpose(ps[0:NCP, 0:P], vcTp[:, 0:NCP], ident).then_inc(done, 1)
                pe.wait_ge(S["vtok_ready"], l + 1)

                def unit_scores(n):
                    g, qt, br = UNITS[n]
                    gd = slice(HD * g, HD * g + HD)
                    q = lambda r: qkv[gd, r, qt * P:qt * P + P]
                    if br == 0:
                        ps, done = bank(("S", l, n, 0))
                        for r in range(GRP):
                            mm = nc.tensor.matmul(ps[:, r * NCP:(r + 1) * NCP], q(r), kcTp[gd, 0:NCP], start=True, stop=True)
                        mm.then_inc(done, 1)
                        return
                    nk = P * (qt + 1)
                    for part in range(qt + 1):
                        ps, done = bank(("S", l, n, part))
                        for i in range(512 // nk):
                            r = part * 2 + i
                            mm = nc.tensor.matmul(ps[:, i * nk:(i + 1) * nk], q(r), qkv[gd, 4 + br, 0:nk], start=True, stop=True)
                        mm.then_inc(done, 1)

                def unit_out(n):
                    g, qt, br = UNITS[n]
                    w = NCP if br == 0 else P
                    nkc = 1 if br == 0 else qt + 1
                    s = S_p[n % 2][:, 0:GRP * w * nkc].rearrange("p (r k) -> p r k", r=GRP)
                    pe.wait_ge(S["exp_ready"], 12 * l + n + 1)
                    for kc in range(nkc):
                        ps, done = bank(("T", l, n, kc))
                        for r in range(GRP):
                            mm = nc.tensor.transpose(ps[0:w, r * P:(r + 1) * P], s[:, r, kc * w:(kc + 1) * w], ident)
                        mm.then_inc(done, 1)
                    pe.wait_ge(S["pt_ready"], 12 * l + n + 1)
                    ps, done = bank(("O", l, n))
                    for r in range(GRP):
                        for kc in range(nkc):
                            v = vcp[0:w, g * HD:(g + 1) * HD] if br == 0 else vtok[:, kc, br, g * HD:(g + 1) * HD]
                            mm = nc.tensor.matmul(ps[:, r * HD:(r + 1) * HD], PT_p[0:w, kc, r * P:(r + 1) * P], v,
                                                  start=(kc == 0), stop=(kc == nkc - 1))
                    mm.then_inc(done, 1)

                pe.wait_ge(S["vc_ready"], 3 * l + 1)
                for n in range(13):
                    if n < 12:
                        unit_scores(n)
                    if n > 0:
                        unit_out(n - 1)
                pe.wait_ge(S["otok_ready"], l + 1)
                for qt in range(2):
                    ps, done = bank(("ot", l, qt))
                    for r in range(GRP):
                        mm = nc.tensor.transpose(ps[:, r * P:(r + 1) * P], otok[:, qt, r, :, :], ident)
                    mm.then_inc(done, 1)

                pe.wait_ge(S["qbd_ready"], l + 1)
                for hf in range(2):
                    it = 2 * l + hf
                    if hf == 1:
                        compress(1)
                    pe.wait_ge(S["vcT_ready"], 3 * l + 2 + hf)
                    ps, done = bank(("vct", l, hf))
                    for bi in range(HALF):
                        mm = nc.tensor.transpose(ps[0:NCS, bi * P:(bi + 1) * P], vcT[:, bi, :], ident)
                    mm.then_inc(done, 1)
                    ps, done = bank(("Sc", l, hf))
                    for bi in range(HALF):
                        mm = nc.tensor.matmul(ps[32 * bi:32 * bi + 32, 0:NCS], qbd[:, hf * HALF + bi, :], kcT[:, bi, :],
                                              start=True, stop=True)
                    mm.then_inc(done, 1)
                    pe.wait_ge(S["pc_ready"], it + 1)
                    ps, done = bank(("imp", l, hf))
                    nc.tensor.matmul(ps[:, 0:NCS], C("group_sum"), S_c[:, 0:NCS], start=True, stop=True).then_inc(done, 1)
                    ps, done = bank(("Tc", l, hf))
                    nc.tensor.transpose(ps[0:NCS, 0:P], S_c[:, 0:NCS], ident).then_inc(done, 1)
                    pe.wait_ge(S["ptc_ready"], it + 1)
                    pe.wait_ge(S["vc_ready"], 3 * l + 2 + hf)
                    ps, done = bank(("Oc", l, hf))
                    for bi in range(HALF):
                        mm = nc.tensor.matmul(ps[32 * bi:32 * bi + 32, 0:P], PT_c[0:NCS, 32 * bi:32 * bi + 32],
                                              vc[0:NCS, bi, :], start=True, stop=True)
                    mm.then_inc(done, 1)
                    for br, ncol in ((1, PAST), (2, WIN)):
                        nk = ncol // 512
                        keys = []
                        for bi in range(HALF):
                            if br == 1:
                                f = (l, hf, ("slc0", "slc1")[bi // 2])
                                s = view(pages, page_slot(f), 2, NPG, 2, P)[:, bi % 2]
                                keys.append((f, s[:, :, 0, :], s[:, :, 1, :]))
                            else:
                                f = (l, hf, "win")
                                s = view(pages, page_slot(f), 2, HALF, 4, P)
                                keys.append((f, s[:, 0, bi], s[:, 1, bi]))
                        for c in range(nk):
                            ps, done = bank(("Ss", l, hf, br, c))
                            for bi in range(HALF):
                                f, kT, _ = keys[bi]
                                pe.wait_ge(pg_full[fill_at[f][0]], fill_at[f][1])
                                mm = nc.tensor.matmul(ps[32 * bi:32 * bi + 32, 0:512].rearrange("p (a b) -> p a b", a=4),
                                                      qbd[:, hf * HALF + bi, :], kT[:, 4 * c:4 * c + 4, :], start=True, stop=True)
                            mm.then_inc(done, 1)
                        ps, done = bank(("Sn", l, hf, br))
                        for bi in range(HALF):
                            mm = nc.tensor.matmul(ps[32 * bi:32 * bi + 32, 0:TS], qbd[:, hf * HALF + bi, :],
                                                  qkv[:, 4 + br, TP:T], start=True, stop=True)
                        mm.then_inc(done, 1)
                        pe.wait_ge(S["ss_exp"], 2 * it + br)
                        for c in range(nk):
                            ps, done = bank(("Ts", l, hf, br, c))
                            for i in range(4):
                                mm = nc.tensor.transpose(ps[:, i * P:(i + 1) * P], S_s[:, 512 * c + i * P:512 * c + (i + 1) * P], ident)
                            mm.then_inc(done, 1)
                        ps, done = bank(("Tn", l, hf, br))
                        nc.tensor.transpose(ps[0:TS, 0:P], S_s[:, ncol:ncol + TS], ident).then_inc(done, 1)
                        pe.wait_ge(S["pts_ready"], 2 * it + br)
                        ps, done = bank(("Os", l, hf, br))
                        for bi in range(HALF):
                            for c in range(4 * nk):
                                nc.tensor.matmul(ps[32 * bi:32 * bi + 32, 0:P], PT_s[:, c, 32 * bi:32 * bi + 32],
                                                 keys[bi][2][:, c, :], start=(c == 0), stop=False)
                            mm = nc.tensor.matmul(ps[32 * bi:32 * bi + 32, 0:P], PT_s[0:TS, 8, 32 * bi:32 * bi + 32],
                                                  vtok[0:TS, 2, br, :], start=False, stop=True)
                        mm.then_inc(done, 1)
                    pe.wait_ge(S["orow_ready"], it + 1)
                    ps, done = bank(("oT", l, hf))
                    for br in range(3):
                        mm = nc.tensor.transpose(ps[:, br * P:(br + 1) * P], orow[:, br, :], ident)
                    mm.then_inc(done, 1)

                for i in range(NQKV, NQKV + NREST):
                    product(("in", l, i), KD, lambda k: xn[:, k, :])

                for c in range(NCHUNK):
                    t0, n = TILES[c]
                    cc = NCHUNK * l + c
                    up = C("upto0") if c < 2 else C("upto2", TS)
                    all_ = C("ones") if c < 2 else C("same2", TS)
                    pe.wait_ge(S["xbcc_ready"], l + 1)
                    ps, done = bank(("xtok", cc))
                    for j in range(4):
                        mm = nc.tensor.transpose(ps[0:n, j * P:(j + 1) * P], xbcc[:, j, t0:t0 + n], ident)
                    mm.then_inc(done, 1)
                    ps, done = bank(("btok", cc))
                    nc.tensor.transpose(ps[0:n, 0:P], xbcc[:, 4, t0:t0 + n], ident).then_inc(done, 1)
                    for g in range(NKV):
                        ps, done = bank(("CB", cc, g))
                        gd = slice(HD * g, HD * g + HD)
                        nc.tensor.matmul(ps[0:n, 0:n], xbcc[gd, 4, t0:t0 + n], xbcc[gd, 5, t0:t0 + n],
                                         start=True, stop=True).then_inc(done, 1)
                    pe.wait_ge(S["dD_ready"], cc + 1)
                    ps, done = bank(("ac", cc))
                    nc.tensor.matmul(ps[0:n, 0:NH], up, dta[0:n, c, :], start=True, stop=True)
                    nc.tensor.matmul(ps[0:n, NH:2 * NH], all_[:, 0:n], dta[0:n, c, :], start=True, stop=True).then_inc(done, 1)
                    for part in range(2 if c < 2 else 1):
                        ps, done = bank(("acB", cc, part))
                        w = min(512, NH * n)
                        nc.tensor.matmul(ps[:, 0:w], C("ones", n), decay[0:n, part * 512:part * 512 + w],
                                         start=True, stop=True).then_inc(done, 1)
                    pe.wait_ge(S["dec_ready"], cc + 1)
                    pe.wait_ge(S["xdt_ready"], cc + 1)
                    if c > 0:
                        pe.wait_ge(S["cp_ready"], 2 * l + c)
                    for hh in range(NH):
                        j, h2 = divmod(hh % GRP, 2)
                        g, hg = divmod(hh, GRP)
                        if hg == 0:
                            ps, done = bank(("y", cc, g))
                        gd = slice(HD * g, HD * g + HD)
                        o = ps[HD * h2:HD * h2 + HD, j * n:(j + 1) * n]
                        mm = nc.tensor.matmul(o, xdt[0:n, hh * HD:(hh + 1) * HD], decay[0:n, hh * n:(hh + 1) * n],
                                              start=True, stop=(c == 0))
                        if c == 1:
                            mm = nc.tensor.matmul(o, hT[gd, hg, :], cp[gd, hg * n:(hg + 1) * n], start=False, stop=True)
                        if c == 2:
                            for b in range(NB):
                                mm = nc.tensor.matmul(o[:, b * TD:(b + 1) * TD], hs[gd, b, hg, :],
                                                      cp[gd, hg * n + b * TD:hg * n + (b + 1) * TD], start=False, stop=(b == NB - 1))
                        if hg == GRP - 1:
                            mm.then_inc(done, 1)
                    pe.wait_ge(S["btok_ready"], cc + 1)
                    if c < 2:
                        ps, done = bank(("hd", cc))
                        for g in range(NKV):
                            mm = nc.tensor.matmul(ps[HD * g:HD * g + HD, 0:256], btok[0:n, g * HD:(g + 1) * HD],
                                                  xtl[0:n, g * 256:(g + 1) * 256], start=True, stop=True)
                        mm.then_inc(done, 1)
                        if c == 0:
                            pe.wait_ge(S["h_ready"], 2 * l + 1)
                    else:
                        pe.wait_ge(S["bm_ready"], l + 1)
                        for b2 in range(NB // 2):
                            ps, done = bank(("hsd", l, b2))
                            for i in range(2):
                                for g in range(NKV):
                                    mm = nc.tensor.matmul(ps[HD * g:HD * g + HD, 256 * i:256 * i + 256],
                                                          bm[0:n, 2 * b2 + i, g * HD:(g + 1) * HD],
                                                          xtl[0:n, g * 256:(g + 1) * 256], start=True, stop=True)
                            mm.then_inc(done, 1)
                pe.wait_ge(S["ysq_ready"], l + 1)
                column_sum(("yss", l), 4, C("ones"), lambda k: tmp[:, k, :])

                pe.wait_ge(S["oS_ready"], l + 1)
                o_br = (oN, oS, oC)
                for m in range(KD):
                    for k3 in range(3):
                        product(("gate", l, m, k3), KD, lambda k: xn[:, k, :])
                    for k3 in range(3):
                        product(("proj", l, m, k3), 4, lambda k: o_br[k3][:, k, :])
                pe.wait_ge(S["merged_ready"], l + 1)
                for m in range(KD):
                    product(("o", l, m), KD, lambda k: tmp[:, k, :])
                pe.wait_ge(S["sq_ready"], 2 * l + 2)
                column_sum(("ss", l, 1), KD, C("ones"), lambda k: tmp[:, k, :])
                pe.wait_ge(S["xn_ready"], 2 * l + 2)
                if l == 0:
                    for f in range(NFD):
                        product(("fg", f), KD, lambda k: xn[:, k, :])
                        product(("fu", f), KD, lambda k: xn[:, k, :])
                    pe.wait_ge(*released(("fu", NFD - 1)))
                    for m in range(KD):
                        product(("fd", m), NFD, lambda k: h[:, k, :])
            ps, done = bank(("router",))
            for tt, (t0, n) in enumerate(TILES):
                for k in range(KD):
                    mm = nc.tensor.matmul(ps[0:n, NE * tt:NE * tt + NE], xn[:, k, t0:t0 + n],
                                          PR(1, "router", NE * k, NE), start=(k == 0), stop=(k == KD - 1))
            mm.then_inc(done, 1)
            for tt, (t0, n) in enumerate(TILES):
                for hf in range(2):
                    ps, done = bank(("xtk", tt, hf))
                    for k in range(4):
                        mm = nc.tensor.transpose(ps[0:n, k * P:(k + 1) * P], xn[:, 4 * hf + k, t0:t0 + n], ident)
                    mm.then_inc(done, 1)
            pe.wait_ge(S["cnt_ready"], 1)
            ps, done = bank(("cnt",))
            for tt, (t0, n) in enumerate(TILES):
                nc.tensor.matmul(ps[:, 0:NE], C("ones", n), mask[0:n, tt, :], start=(tt == 0), stop=(tt == 2))
            for tt, (t0, n) in enumerate(TILES):
                o = ps[0:n, NE * (tt + 1):NE * (tt + 2)]
                for t2 in range(tt):
                    nc.tensor.matmul(o, C("ones")[:, 0:n], mask[:, t2, :], start=(t2 == 0), stop=False)
                mm = nc.tensor.matmul(o, C("before", n)[:, 0:n], mask[0:n, tt, :], start=(tt == 0), stop=True)
            mm.then_inc(done, 1)
            at = [0]
            inloop = [None]

            def pbank(key):
                u = base + at[0]
                at[0] += 1
                use_of[key] = u
                pe.wait_ge(bank_free[u % 8], inloop[0] * (MOE_USES // 8) + u // 8)
                return psum[u % 8], bank_full[u % 8]

            def gather(bank_, key):
                for hf in range(2):
                    ps, done = bank_((key, hf))
                    for k in range(4):
                        for tt, (t0, n) in enumerate(TILES):
                            c0 = (4 * hf + k) * P
                            mm = nc.tensor.matmul(ps[:, k * CAP:(k + 1) * CAP], xtok[0:n, tt, c0:c0 + P], pick[0:n, tt, :],
                                                  start=(tt == 0), stop=(tt == 2))
                    mm.then_inc(done, 1)

            def to_slots(key):
                for hf in range(2):
                    ps, done = pbank((key, hf))
                    for k in range(4):
                        mm = nc.tensor.transpose(ps[0:CAP, k * P:(k + 1) * P], yT[:, 4 * hf + k, :], ident)
                    mm.then_inc(done, 1)

            def scatter(key):
                for m in range(KD):
                    ps, done = pbank((key, m))
                    nc.tensor.matmul(ps[:, 0:T], yS[0:CAP, m, :], spread[0:CAP, :], start=True, stop=True).then_inc(done, 1)

            pe.wait_ge(S["pick_ready"], 1)
            pe.wait_ge(*released(("xtk", 2, 1)))
            gather(bank, "xe0")
            pe.wait_ge(S["table_ready"], 1)
            n_pass = pe.value_load(passes[0:1, 32:33], min_val=NE, max_val=MAX_PASSES)
            pe.wait_ge(*released(("xe0", 1)))
            base = uses[0]
            assert blk[0] == PRE_SLOTS * BPS
            with pe.Fori(0, n_pass) as i:
                inloop[0] = i
                nb = [0]

                def wmul(out, rhs, start, stop):
                    s, o = divmod(nb[0], BPS)
                    nb[0] += 1
                    s += PRE_SLOTS
                    if o == 0:
                        pe.wait_ge(w_full[s % RING], i * (16 * EXP_SLOTS // RING) + 16 * (s // RING + 1))
                    a = (s % RING) * SLOTF + o * P
                    mm = nc.tensor.matmul(out, wring[:, a:a + P], rhs, start=start, stop=stop)
                    if o == 0:
                        mm.then_inc(w_free[(s - 1) % RING], 1)
                    return mm

                def gate_up(q):
                    ps, done = pbank(("gu", q))
                    for f in range(2):
                        for part in range(2):
                            c0 = (2 * part + f) * CAP
                            for k in range(KD):
                                mm = wmul(ps[:, c0:c0 + CAP], xe[:, k, :], k == 0, k == KD - 1)
                    mm.then_inc(done, 1)

                use_of[("dn", 2)] = base + MOE_USES - 1
                use_of[("xe", 1)] = base + MOE_USES - 4
                use_of[("sp", 2)] = base + 16
                pe.wait_ge(*released(("xe", 1), i, 1))
                gate_up(0)
                gate_up(1)
                pe.wait_ge(*released(("dn", 2), i, 1))
                to_slots("yt")
                gate_up(2)
                gate_up(3)
                pe.wait_ge(*released(("yt", 1), i))
                pe.wait_ge(*released(("sp", 2), i, 1))
                scatter("sc")
                for tt, (t0, n) in enumerate(TILES):
                    ps, done = pbank(("sp", tt))
                    nc.tensor.transpose(ps[0:CAP, 0:P], pickw[:, tt, :], ident).then_inc(done, 1)
                for q in range(4, NFE // 2):
                    gate_up(q)
                pe.wait_ge(S["pick_ready"], i + 2)
                gather(pbank, "xe")
                pe.wait_ge(*released(("gu", NFE // 2 - 1), i))
                for d, (m0, nm) in enumerate(DOWN):
                    ps, done = pbank(("dn", d))
                    for m in range(nm):
                        for k in range(NFE):
                            mm = wmul(ps[:, m * CAP:(m + 1) * CAP], he[:, k, :], k == 0, k == NFE - 1)
                    mm.then_inc(done, 1)
                assert at[0] == MOE_USES and nb[0] == EXP_BLOCKS
                assert (use_of[("dn", 2)], use_of[("xe", 1)], use_of[("sp", 2)]) == (base + 31, base + 28, base + 16)
            inloop[0] = n_pass - 1
            pe.wait_ge(*released(("dn", 2), n_pass - 1))
            to_slots("yt_last")
            pe.wait_ge(*released(("yt_last", 1), n_pass - 1))
            pe.wait_ge(*released(("sp", 2), n_pass - 1))
            scatter("sc_last")

        @block.sync
        def _(sp):
            sp.dma_start(cst[:, :], consts).then_inc(S["const_in"], 16)
            sp.dma_start(par[:, :], params).then_inc(S["const_in"], 16)
            sp.dma_start(xT_[:, :], xT_in).then_inc(S["x_in"], 16)

            def load(pos, index):
                sp.dma_start(wring[:, pos * SLOTF:(pos + 1) * SLOTF],
                             wstream[index, :, :].rearrange("a p n -> (a p) n")).then_inc(w_full[pos], 16)

            for s in range(RING):
                load(s, bass.ds(s, 1))
            known = PRE_SLOTS + RING
            rounds = (known - RING) // RING
            with sp.Fori(0, rounds) as i:
                for s in range(RING):
                    sp.wait_ge(w_free[s], i + 1)
                    load(s, bass.ds(i * RING + (RING + s), 1))
            for s in range(RING * (rounds + 1), known):
                sp.wait_ge(w_free[s % RING], s // RING)
                load(s % RING, bass.ds(s, 1))
            sp.wait_ge(S["table_ready"], 1)
            n_pass = sp.value_load(passes[0:1, 32:33], min_val=NE, max_val=MAX_PASSES)

            def pass_slots(i, ex, first, last):
                for s in range(first, last):
                    pos = (PRE_SLOTS + s) % RING
                    sp.wait_ge(w_free[pos], i * (EXP_SLOTS // RING) + (PRE_SLOTS + s) // RING)
                    load(pos, bass.ds(ex * EXP_SLOTS + (PRE_SLOTS + s), 1))

            with sp.Fori(0, n_pass - 1) as i:
                ex = sp.value_load(passes[0:1, bass.ds(i, 1)], min_val=0, max_val=NE - 1)
                pass_slots(i, ex, RING, EXP_SLOTS)
                ex2 = sp.value_load(passes[0:1, bass.ds(i + 1, 1)], min_val=0, max_val=NE - 1)
                pass_slots(i + 1, ex2, 0, RING)
            ex = sp.value_load(passes[0:1, bass.ds(n_pass - 1, 1)], min_val=0, max_val=NE - 1)
            pass_slots(n_pass - 1, ex, RING, EXP_SLOTS)
            sp.wait_ge(S["x_ready"], 4)
            sp.dma_start(y_out, xT_[:, :]).then_inc(S["y_done"], 16)
            sp.wait_ge(S["y_done"], 16)

        @block.gpsimd
        def _(pool):
            pool.dma_start(ptab[0:1, :], page_table).then_inc(S["ptab_in"], 16)
            pool.wait_ge(S["ptab_in"], 16)
            n_pool = kc_pages.shape[0] // DEPTH

            def fill(f):
                l, hf, what = f
                idx = FILLS.index(f)
                pos = idx % 3
                at = page_slot(f)
                if idx >= 3:
                    pl, phf, pw = FILLS[idx - 3]
                    last = {"kc": ("cmp", pl, phf, 0) if phf else ("cmpp", pl, 0), "vc": ("cmp", pl, phf, 1) if phf else ("cmpp", pl, 1),
                            "slc0": ("Os", pl, phf, 1), "slc1": ("Os", pl, phf, 1), "win": ("Os", pl, phf, 2)}[pw]
                    pool.wait_ge(*filled(last))
                if what == "win":
                    pool.dma_start(view(pages, at, HALF, WIN),
                                   win_kT[l, :, hf * HALF:(hf + 1) * HALF, :]).then_inc(pg_full[pos], 16)
                    for bi in range(HALF):
                        pool.dma_start(view(pages, at + 2048 + bi * 512, 4, P),
                                       win_v[l, hf * HALF + bi]).then_inc(pg_full[pos], 16)
                    return
                src, width, b0, nb = {"kc": (kc_pages, P, 0, HALF), "vc": (vc_pages, P, 0, HALF),
                                      "slc0": (slc_pages, 2 * P, 0, 2), "slc1": (slc_pages, 2 * P, 2, 2)}[what]
                first = (hf * HALF + b0) * NPG
                with pool.Fori(0, nb * NPG) as i:
                    page = pool.value_load(ptab[0:1, bass.ds(i + first, 1)], min_val=0, max_val=n_pool - 1)
                    pool.dma_start(pages[:, bass.ds(i * width + at, width)],
                                   src[bass.ds(page + l * n_pool, 1), :, :].rearrange("a p n -> (a p) n")).then_inc(pg_full[pos], 16)

            for f in FILLS[0:3]:
                fill(f)
            nout = 0
            for l in range(DEPTH):
                pool.dma_start(win_out[l], win_rows[l, :, TD:, :]).then_inc(S["win_done"], 16)
                pool.wait_ge(S["qk_ready"], l + 1)
                pool.dma_start(kv_out[l], qkv[:, 4:10, :]).then_inc(S["kv_done"], 16)
                for f in FILLS[3:10] if l == 0 else FILLS[13:20]:
                    fill(f)
                pool.wait_ge(S["kv_done"], 16 * (l + 1))
                pool.wait_ge(S["attn_done"], l + 1)
                pool.dma_start(sc_st, sc_in[l]).then_inc(S["st_in"], 16)
                pool.dma_start(cv_st, conv_in[l]).then_inc(S["st_in"], 16)
                pool.wait_ge(S["cols_ready"], l + 1)
                for t in range(6):
                    pool.dma_start(conv_out[l, :, t, 0:3], xbcp[:, t, TP:TP + 3]).then_inc(S["cc_done"], 16)
                    pool.dma_start(conv_out[l, :, t, 3:27].rearrange("p (b k) -> p b k", b=NB),
                                   xbcp[:, t, 3 + TP:].rearrange("p (b k) -> p b k", b=NB)[:, :, TD:TD + 3]).then_inc(S["cc_done"], 16)
                for t in range(4):
                    pool.dma_start(sc_out[l, :, t, 0:2], chp[:, t, TP:TP + 2]).then_inc(S["cc_done"], 16)
                    pool.dma_start(sc_out[l, :, t, 2:18].rearrange("p (b k) -> p b k", b=NB),
                                   chp[:, t, 2 + TP:].rearrange("p (b k) -> p b k", b=NB)[:, :, TD:TD + 2]).then_inc(S["cc_done"], 16)
                pool.wait_ge(S["cc_done"], 320 * (l + 1))
                pool.wait_ge(S["sc_conv"], l + 1)
                pool.dma_start(hs, ssm_in[l]).then_inc(S["hs_in"], 16)
                pool.wait_ge(S["h_ready"], 2 * l + 2)
                pool.dma_start(ssm_p_out[l], hT).then_inc(S["hp_done"], 16)
                pool.wait_ge(S["y_ready"], l + 1)
                pool.dma_start(ssm_s_out[l], hs).then_inc(S["hs_done"], 16)
                pool.wait_ge(S["hp_done"], 16 * (l + 1))
                pool.wait_ge(S["hs_done"], 16 * (l + 1))
                if l == 0:
                    for f in FILLS[10:13]:
                        fill(f)
            pool.wait_ge(S["win_done"], 32)

        @block.scalar
        def _(act):
            chain, marks = [0], [0]

            def link(ins):
                chain[0] += 1
                ins.then_inc(S["act_chain"], 1)
                act.wait_ge(S["act_chain"], chain[0])

            def copy(out, in_):
                return A.activation(out, in_, ACT.Copy)

            def evac(key, out, cols, rows=P, name=None):
                act.wait_ge(*filled(key))
                ps = bank_of(key)
                src = ps[0:rows, 0:cols]
                if len(out.shape) == 3:
                    src = src.rearrange("p (a b) -> p a b", b=out.shape[2])
                copy(out, src).then_inc(free(key), 1)

            def signal(name):
                marks[0] += 1
                k = marks[0] % MARKS
                A.activation(mark[0:1, k:k + 1], eps[0:1, :], ACT.Copy).then_inc(S[name], 1)

            eps = C("eps")
            act.wait_ge(S["const_in"], 32)
            act.wait_ge(S["x_in"], 16)
            act.wait_ge(S["pool_zero"], 1)

            def rms(l, which):
                A.activation(tmp_[:, :], xT_[:, :], ACT.Square).then_inc(S["sq_ready"], 1)
                act.wait_ge(*filled(("ss", l, which)))
                ps = bank_of(("ss", l, which))
                A.activation(std[:, :], ps[:, 0:T], ACT.Sqrt, bias=eps, scale=1.0 / D).then_inc(free(("ss", l, which)), 1)

            for l in range(DEPTH):
                if l:
                    act.wait_ge(S["x_ready"], 2 * l)
                rms(l, 0)
                act.wait_ge(*filled(("small", l)))
                ps = bank_of(("small", l))
                if l:
                    act.wait_ge(S["kv_done"], 16 * l)
                copy(small[0:TS, 2, :], ps[0:TS, 64:96]).then_inc(S["small_ready"], 1)
                copy(small[:, 0:2, :], ps[:, 0:64].rearrange("p (a b) -> p a b", a=2)).then_inc(free(("small", l)), 1)
                act.wait_ge(*released(("small", l)))
                A.activation(gates[0:TS, 2, :], small[0:TS, 2, 0:24], ACT.Sigmoid)
                A.activation(gates[:, 0:2, :], small[:, 0:2, 0:24], ACT.Sigmoid).then_inc(S["gates_ready"], 1)
                for i in range(NQKV):
                    evac(("in", l, i), qkv[:, i, :], T)
                act.wait_ge(*released(("in", l, 9)))
                A.activation(tmp[:, 0:7, :], qkv[:, 0:7, :], ACT.Square).then_inc(S["qksq_ready"], 1)
                signal("qkv_ready")
                for i in range(7):
                    act.wait_ge(*filled(("qkss", l, i)))
                    ps = bank_of(("qkss", l, i))
                    A.activation(rq[:, i, :], ps[:, 0:T], ACT.Sqrt, bias=eps, scale=1.0 / HD).then_inc(free(("qkss", l, i)), 1)
                signal("rq_ready")
                for tt, (t0, n) in enumerate(TILES):
                    evac(("vt", l, tt), vtok[0:n, tt, :, :], 3 * P, n)
                signal("vtok_ready")
                act.wait_ge(*filled(("gT", l)))
                ps = bank_of(("gT", l))
                copy(gT[0:24, :], ps[0:24, 0:TS]).then_inc(free(("gT", l)), 1)
                signal("gT_ready")
                act.wait_ge(*filled(("gB", l)))
                ps = bank_of(("gB", l))
                copy(gB.rearrange("p a b c -> p (a b c)"), ps[:, 0:384]).then_inc(free(("gB", l)), 1)
                for kind, (o, op) in enumerate(((kcT, kcTp), (vcT, vcTp))):
                    evac(("cmp", l, 0, kind), o, HALF * NCS)
                    evac(("cmpp", l, kind), op[:, 0:NCP], NCP)
                    signal("vcT_ready")
                evac(("vcp", l), vcp[0:NCP, :], P, NCP)
                signal("vc_ready")
                for n, (g, qt, br) in enumerate(UNITS):
                    w = NCP if br == 0 else P * (qt + 1)
                    s = S_p[n % 2][:, 0:GRP * w].rearrange("p (r k) -> p r k", r=GRP)
                    act.wait_ge(S["smax"], 12 * l + n + 1)
                    for r in range(GRP):
                        e = A.activation(s[:, r, :], s[:, r, :], ACT.Exp, bias=mx[:, n % 2, r:r + 1],
                                         accum_out=ssum[:, n % 2, r:r + 1])
                    e.then_inc(S["exp_ready"], 1)
                    rows = min(w, P)
                    for kc in range(1 if br == 0 else qt + 1):
                        evac(("T", l, n, kc), PT_p[0:rows, kc, :], 512, rows)
                    signal("pt_ready")
                for qt in range(2):
                    evac(("ot", l, qt), oN[:, :, qt * P:(qt + 1) * P], 512)
                for hf in range(2):
                    it = 2 * l + hf
                    if hf == 1:
                        act.wait_ge(S["orow_ready"], it)
                        evac(("cmp", l, 1, 0), kcT, HALF * NCS)
                        evac(("cmp", l, 1, 1), vcT, HALF * NCS)
                        signal("vcT_ready")
                    evac(("vct", l, hf), vc[0:NCS, :, :], 512, NCS)
                    signal("vc_ready")
                    act.wait_ge(S["scmax"], it + 1)
                    A.activation(S_c[:, 0:NCS], S_c[:, 0:NCS], ACT.Exp, bias=smx[:, 0:1], accum_out=ssm[:, 0:1]).then_inc(S["sc_exp"], 1)
                    evac(("Tc", l, hf), PT_c[0:NCS, :], P, NCS)
                    signal("ptc_ready")
                    for br, ncol in ((1, PAST), (2, WIN)):
                        act.wait_ge(S["ssmax"], 2 * it + br)
                        A.activation(S_s[:, 0:ncol + TS], S_s[:, 0:ncol + TS], ACT.Exp, bias=smx[:, br:br + 1],
                                     accum_out=ssm[:, br:br + 1]).then_inc(S["ss_exp"], 1)
                        for c in range(ncol // 512):
                            evac(("Ts", l, hf, br, c), PT_s[:, 4 * c:4 * c + 4, :], 512)
                        evac(("Tn", l, hf, br), PT_s[0:TS, 8, :], P, TS)
                        signal("pts_ready")
                act.wait_ge(S["attn_done"], l + 1)
                act.wait_ge(S["kv_done"], 16 * (l + 1))
                A.activation(ea, PR(l, "a_log", 0, NH), ACT.Exp).then_inc(S["ea_ready"], 1)
                act.wait_ge(S["spa"], l + 1)
                A.activation(sp_e, sp_e, ACT.Exp, scale=-1.0).then_inc(S["sp_exp"], 1)
                for j in range(6):
                    act.wait_ge(*filled(("in", l, 10 + j)))
                    ps = bank_of(("in", l, 10 + j))
                    copy(xbcp[:, j, 3:3 + TP], ps[:, 0:TP])
                    copy(xbcp[:, j, 3 + TP:].rearrange("p (b k) -> p b k", b=NB)[:, :, 3:],
                         ps[:, TP:T].rearrange("p (b k) -> p b k", b=NB)).then_inc(free(("in", l, 10 + j)), 1)
                signal("xbc_ready")
                for j in range(4):
                    act.wait_ge(*filled(("in", l, 16 + j)))
                    ps = bank_of(("in", l, 16 + j))
                    A.activation(zs[:, j, :], ps[:, 0:T], ACT.Silu).then_inc(free(("in", l, 16 + j)), 1)
                for j in range(4):
                    evac(("in", l, 20 + j), scc[:, j, :], T)
                signal("scc_ready")
                for j in range(4):
                    evac(("in", l, 28 + j), oC[:, j, :], T)
                signal("scb_ready")
                act.wait_ge(S["xbcc_raw"], l + 1)
                A.activation(xbcc, xbcc, ACT.Silu).then_inc(S["xbcc_ready"], 1)
                for c in range(NCHUNK):
                    n = TILES[c][1]
                    cc = NCHUNK * l + c
                    w = NH * n
                    act.wait_ge(S["tl_sub"], cc + 1)
                    A.activation(tail[0:n, :], tail[0:n, :], ACT.Exp).then_inc(S["tl_ready"], 1)
                    act.wait_ge(S["seg_ready"], cc + 1)
                    A.activation(eB[:, 0:w], eB[:, 0:w], ACT.Exp).then_inc(S["eb_ready"], 1)
                    A.activation(decay[0:n, 0:w], decay[0:n, 0:w], ACT.Exp).then_inc(S["dec_exp"], 1)
                    evac(("btok", cc), btok[0:n, :], P, n)
                    signal("btok_ready")
                act.wait_ge(S["y_ready"], l + 1)
                A.activation(tmp[:, 0:4, :], oS, ACT.Square).then_inc(S["ysq_ready"], 1)
                act.wait_ge(*filled(("yss", l)))
                ps = bank_of(("yss", l))
                A.activation(std[:, :], ps[:, 0:T], ACT.Sqrt, bias=eps, scale=1.0 / SSMI).then_inc(free(("yss", l)), 1)
                act.wait_ge(S["mix_done"], l + 1)
                act.wait_ge(S["hs_done"], 16 * (l + 1))
                act.wait_ge(S["hp_done"], 16 * (l + 1))
                for m in range(KD):
                    for k3 in range(3):
                        act.wait_ge(*filled(("gate", l, m, k3)))
                        ps = bank_of(("gate", l, m, k3))
                        if m >= 2 and k3 == 0:
                            act.wait_ge(S["gate_sig"], l * KD + m - 1)
                        A.activation(gs_[:, (m % 2) * 3 + k3, :], ps[:, 0:T], ACT.Sigmoid).then_inc(free(("gate", l, m, k3)), 1)
                act.wait_ge(S["x_ready"], 2 * l + 1)
                rms(l, 1)
                if l == 0:
                    for f in range(NFD):
                        act.wait_ge(*filled(("fg", f)))
                        ps = bank_of(("fg", f))
                        if f >= 2:
                            act.wait_ge(*released(("fu", f - 2)))
                        A.activation(gs_[:, f % 2, :], ps[:, 0:T], ACT.Silu).then_inc(free(("fg", f)), 1)
            act.wait_ge(S["re_sub"], 1)
            A.activation(re, re, ACT.Exp).then_inc(S["re_exp"], 1)
            for tt, (t0, n) in enumerate(TILES):
                for hf in range(2):
                    evac(("xtk", tt, hf), xtok[0:n, tt, 512 * hf:512 * hf + 512], 512, n)

            def take(key, out, rows, cols, it):
                act.wait_ge(*filled(key, it))
                ps = bank_of(key)
                src = ps[0:rows, 0:cols]
                if len(out.shape) == 3:
                    src = src.rearrange("p (a b) -> p a b", b=out.shape[2])
                copy(out, src).then_inc(free(key), 1)

            def take_slots(key, it):
                for hf in range(2):
                    take((key, hf), yS[0:CAP, 4 * hf:4 * hf + 4, :], CAP, 512, it)

            def take_gather(key, it):
                for hf in range(2):
                    take((key, hf), xe[:, 4 * hf:4 * hf + 4, :], P, 4 * CAP, it)

            act.wait_ge(S["zero_ready"], 1)
            take_gather("xe0", None)
            act.wait_ge(S["table_ready"], 1)
            n_pass = act.value_load(passes[0:1, 32:33], min_val=NE, max_val=MAX_PASSES)
            with act.Fori(0, n_pass) as i:
                def silu(q):
                    act.wait_ge(*filled(("gu", q), i))
                    ps = bank_of(("gu", q))
                    act.wait_ge(*released(("gu", q - 2 if q >= 2 else NFE // 2 - 2 + q), i, 0 if q >= 2 else 1))
                    A.activation(sg[:, q % 2, :], ps[:, 0:2 * CAP], ACT.Silu).then_inc(S["silu_ready"], 1)

                silu(0)
                silu(1)
                take_slots("yt", i)
                silu(2)
                silu(3)
                for tt, (t0, n) in enumerate(TILES):
                    take(("sp", tt), spread[0:CAP, t0:t0 + n], CAP, n, i)
                for q in range(4, NFE // 2):
                    silu(q)
                take_gather("xe", i)
                for d, (m0, nm) in enumerate(DOWN):
                    take(("dn", d), yT[:, m0:m0 + nm, :], P, nm * CAP, i)
            take_slots("yt_last", n_pass - 1)

        @block.vector
        def _(dve):
            chain, marks = [0], [0]

            def link(ins):
                chain[0] += 1
                ins.then_inc(S["dve_chain"], 1)
                dve.wait_ge(S["dve_chain"], chain[0])

            def signal(name):
                marks[0] += 1
                k = MARKS + marks[0] % MARKS
                V.memset(mark[0:1, k:k + 1], 0.0).then_inc(S[name], 1)

            dve.wait_ge(S["const_in"], 32)
            dve.wait_ge(S["x_in"], 16)
            V.memset(std[:, :], 0.0)
            V.memset(reg[:, :], 0.0).then_inc(S["pool_zero"], 1)

            def rms(l, which, w):
                dve.wait_ge(*released(("ss", l, which)))
                link(V.reciprocal(std[:, :], std[:, :]))
                for k in range(KD):
                    last = V.scalar_tensor_tensor(xn[:, k, :], xT[:, k, :], PR(l, w, k), std[:, :], ALU.mult, ALU.mult)
                last.then_inc(S["xn_ready"], 1)
                dve.wait_ge(S["xn_ready"], 2 * l + which + 1)

            for l in range(DEPTH):
                rms(l, 0, "norm_mix")
                dve.wait_ge(S["rq_ready"], l + 1)
                link(V.reciprocal(rq, rq))
                for i in range(7):
                    last = V.scalar_tensor_tensor(qkv[:, i, :], qkv[:, i, :], PR(l, "qk_norm", i), rq[:, i, :], ALU.mult, ALU.mult)
                last.then_inc(S["qk_normed"], 1)
                for i in range(7):
                    dve.wait_ge(*filled(("rot", l, i)))
                    ps = bank_of(("rot", l, i))
                    V.tensor_tensor(rq[:, i, :], ps[:, 0:T], C("sin"), ALU.mult).then_inc(free(("rot", l, i)), 1)
                    link(V.tensor_tensor(qkv[:, i, :], qkv[:, i, :], C("cos"), ALU.mult))
                    last = V.tensor_tensor(qkv[:, i, :], qkv[:, i, :], rq[:, i, :], ALU.add)
                last.then_inc(S["qk_ready"], 1)
                dve.wait_ge(S["qk_ready"], l + 1)

                def unit_softmax(n):
                    g, qt, br = UNITS[n]
                    w = NCP if br == 0 else P * (qt + 1)
                    s = S_p[n % 2][:, 0:GRP * w].rearrange("p (r k) -> p r k", r=GRP)
                    if br == 0:
                        mask = C("cmp_mask")[:, qt * NCP:(qt + 1) * NCP]
                    else:
                        mask = C(("causal0", "causal1")[qt])
                    parts = 2 if (br and qt) else 1
                    nr = GRP // parts
                    for part in range(parts):
                        dve.wait_ge(*filled(("S", l, n, part)))
                        ps = bank_of(("S", l, n, part))
                        V.scalar_tensor_tensor(s[:, part * nr:(part + 1) * nr, :],
                                               ps[:, 0:nr * w].rearrange("p (r k) -> p r k", r=nr), HD ** -0.5,
                                               bc(mask, 1, nr), ALU.mult, ALU.add).then_inc(free(("S", l, n, part)), 1)
                    dve.wait_ge(*released(("S", l, n, parts - 1)))
                    V.tensor_reduce(mx[:, n % 2, :], s, AX.X, ALU.max, negate=True).then_inc(S["smax"], 1)

                def unit_out(n):
                    g, qt, br = UNITS[n]
                    dve.wait_ge(S["exp_ready"], 12 * l + n + 1)
                    dve.wait_ge(S["gates_ready"], l + 1)
                    link(V.reciprocal(rsum, ssum[:, n % 2, :]))
                    gate = gates[:, qt, g * 12:(g + 1) * 12].rearrange("p (r k) -> p r k", k=3)[:, :, br]
                    link(V.tensor_tensor(coef, rsum, gate, ALU.mult))
                    if br == 0:
                        link(V.tensor_scalar(coef, coef, C("cmp_any")[:, qt:qt + 1], None, ALU.mult))
                    dve.wait_ge(*filled(("O", l, n)))
                    ps = bank_of(("O", l, n))
                    src = ps[:, 0:256].rearrange("p (r d) -> p r d", r=GRP)
                    dst = otok[:, qt, :, g, :]
                    out = dst if br == 0 else otmp
                    V.tensor_tensor(out, src, bc(coef, 2, HD), ALU.mult).then_inc(free(("O", l, n)), 1)
                    if br:
                        dve.wait_ge(*released(("O", l, n)))
                        link(V.tensor_tensor(dst, dst, otmp, ALU.add))

                for n in range(13):
                    if n < 12:
                        unit_softmax(n)
                    if n > 0:
                        unit_out(n - 1)
                signal("otok_ready")
                link(V.memset(qbd, 0.0))
                for g in range(NKV):
                    gd = slice(HD * g, HD * g + HD)
                    last = V.tensor_copy(qbd[gd, :, 16 * g:16 * g + 16].rearrange("p b (r t) -> p b r t", r=GRP),
                                         qkv[gd, 0:GRP, TP:T].rearrange("p r (b t) -> p b r t", b=NB))
                last.then_inc(S["qbd_ready"], 1)
                for hf in range(2):
                    it = 2 * l + hf
                    dve.wait_ge(*filled(("Sc", l, hf)))
                    ps = bank_of(("Sc", l, hf))
                    V.tensor_scalar(S_c[:, 0:NCS], ps[:, 0:NCS], HD ** -0.5, None, ALU.mult).then_inc(free(("Sc", l, hf)), 1)
                    dve.wait_ge(*released(("Sc", l, hf)))
                    V.tensor_reduce(smx[:, 0:1], S_c[:, 0:NCS], AX.X, ALU.max, negate=True).then_inc(S["scmax"], 1)
                    dve.wait_ge(S["sc_exp"], it + 1)
                    link(V.reciprocal(srs[:, 0:1], ssm[:, 0:1]))
                    V.tensor_scalar(S_c[:, 0:NCS], S_c[:, 0:NCS], srs[:, 0:1], None, ALU.mult).then_inc(S["pc_ready"], 1)
                    dve.wait_ge(*filled(("imp", l, hf)))
                    ps = bank_of(("imp", l, hf))
                    V.tensor_reduce(imp, ps[:, 4:4 + 4 * NMID].rearrange("p (b k) -> p b k", k=4), AX.X, ALU.add)\
                        .then_inc(free(("imp", l, hf)), 1)
                    dve.wait_ge(*released(("imp", l, hf)))
                    link(V.tensor_reduce(m1[:, 0:1], imp, AX.X, ALU.min))
                    link(V.tensor_scalar(tie, imp, m1[:, 0:1], None, ALU.is_equal))
                    link(V.tensor_tensor(tie, tie, C("blk_idx"), ALU.mult))
                    link(V.tensor_reduce(m1[:, 1:2], tie, AX.X, ALU.max))
                    link(V.tensor_scalar(drop, C("blk_idx"), m1[:, 1:2], NEG, ALU.is_equal, ALU.mult))
                    dve.wait_ge(*filled(("Oc", l, hf)))
                    ps = bank_of(("Oc", l, hf))
                    V.tensor_copy(orow[:, 0, :], ps[:, 0:P]).then_inc(free(("Oc", l, hf)), 1)
                    for br, ncol in ((1, PAST), (2, WIN)):
                        for c in range(ncol // 512):
                            dve.wait_ge(*filled(("Ss", l, hf, br, c)))
                            ps = bank_of(("Ss", l, hf, br, c))
                            V.tensor_scalar(S_s[:, 512 * c:512 * c + 512], ps[:, 0:512], HD ** -0.5, None, ALU.mult)\
                                .then_inc(free(("Ss", l, hf, br, c)), 1)
                        dve.wait_ge(*filled(("Sn", l, hf, br)))
                        ps = bank_of(("Sn", l, hf, br))
                        V.scalar_tensor_tensor(S_s[:, ncol:ncol + TS], ps[:, 0:TS], HD ** -0.5,
                                               C("new_mask")[:, hf * TS:(hf + 1) * TS], ALU.mult, ALU.add)\
                            .then_inc(free(("Sn", l, hf, br)), 1)
                        dve.wait_ge(*released(("Sn", l, hf, br)))
                        if br == 1:
                            mid = S_s[:, SEL:SEL * (NMID + 1)].rearrange("p (b k) -> p b k", k=SEL)
                            link(V.tensor_tensor(mid, mid, bc(drop, 2, SEL), ALU.add))
                        else:
                            link(V.tensor_tensor(S_s[:, 0:TD], S_s[:, 0:TD], C("win_mask"), ALU.add))
                        V.tensor_reduce(smx[:, br:br + 1], S_s[:, 0:ncol + TS], AX.X, ALU.max, negate=True).then_inc(S["ssmax"], 1)
                        dve.wait_ge(S["ss_exp"], 2 * it + br)
                        link(V.reciprocal(srs[:, br:br + 1], ssm[:, br:br + 1]))
                        dve.wait_ge(*filled(("Os", l, hf, br)))
                        ps = bank_of(("Os", l, hf, br))
                        V.tensor_scalar(orow[:, br, :], ps[:, 0:P], srs[:, br:br + 1], None, ALU.mult)\
                            .then_inc(free(("Os", l, hf, br)), 1)
                        dve.wait_ge(*released(("Os", l, hf, br)))
                    signal("orow_ready")
                    dve.wait_ge(*filled(("oT", l, hf)))
                    ps = bank_of(("oT", l, hf))
                    for g in range(NKV):
                        gd = slice(HD * g, HD * g + HD)
                        acc = [osam[gd, k, :].rearrange("p (b r t) -> p b r t", b=HALF, r=GRP) for k in range(2)]
                        for br in range(3):
                            o = ps[gd, br * P:(br + 1) * P].rearrange("p (b q) -> p b q", b=HALF)[:, :, 16 * g:16 * g + 16]\
                                .rearrange("p b (r t) -> p b r t", r=GRP)
                            gt = gB[gd, br, :, 16 * hf:16 * hf + 16].rearrange("p r (b t) -> p b r t", b=HALF)
                            last = V.tensor_tensor(acc[0 if br == 0 else 1], o, gt, ALU.mult)
                            if br == 2 and g == NKV - 1:
                                last.then_inc(free(("oT", l, hf)), 1)
                                dve.wait_ge(*released(("oT", l, hf)))
                            else:
                                link(last)
                            if br == 1:
                                link(V.tensor_tensor(acc[0], acc[0], acc[1], ALU.add))
                            if br == 2:
                                t0 = TP + 16 * hf
                                link(V.tensor_tensor(oN[gd, :, t0:t0 + 16].rearrange("p r (b t) -> p b r t", b=HALF),
                                                     acc[0], acc[1], ALU.add))

                dve.wait_ge(S["kv_done"], 16 * (l + 1))
                link(V.tensor_tensor(tmp_[:, 0:24].rearrange("p (a b) -> p a b", a=3), small[:, :, 24:32],
                                     bc(PR(l, "dt_bias", 0, NH), 1, 3), ALU.add))
                V.tensor_copy(sp_v, tmp_[:, 0:24].rearrange("p (a b) -> p a b", a=3)).then_inc(S["attn_done"], 1)
                dve.wait_ge(S["attn_done"], l + 1)
                link(V.tensor_scalar(sp_e, sp_v, -1.0, None, ALU.mult))
                V.tensor_tensor(sp_e, sp_e, sp_v, ALU.max).then_inc(S["spa"], 1)
                dve.wait_ge(S["sp_exp"], l + 1)
                link(V.tensor_scalar(sp_z, sp_e, 2.0, None, ALU.add))
                link(V.reciprocal(sp_z, sp_z))
                link(V.tensor_tensor(sp_z, sp_z, sp_e, ALU.mult))
                link(V.tensor_tensor(sp_q, sp_z, sp_z, ALU.mult))
                link(V.tensor_scalar(sp_p, sp_q, 1.0 / 13, None, ALU.mult))
                for k in (11, 9, 7, 5, 3):
                    link(V.scalar_tensor_tensor(sp_p, sp_p, 1.0 / k, sp_q, ALU.add, ALU.mult))
                link(V.scalar_tensor_tensor(sp_p, sp_p, 1.0, sp_z, ALU.add, ALU.mult))
                link(V.tensor_scalar(sp_v, sp_v, 0.0, None, ALU.max))
                link(V.scalar_tensor_tensor(dt, sp_p, 2.0, sp_v, ALU.mult, ALU.add))
                dve.wait_ge(S["ea_ready"], l + 1)
                link(V.scalar_tensor_tensor(dta, dt, -1.0, bc(ea, 1, 3), ALU.mult, ALU.mult))

                dve.wait_ge(S["xbc_ready"], l + 1)
                dve.wait_ge(S["st_in"], 32 * (l + 1))
                link(V.memset(xbcp[:, :, 0:3], 0.0))
                for j in range(6):
                    last = V.tensor_copy(xbcp[:, j, 3 + TP:].rearrange("p (b k) -> p b k", b=NB)[:, :, 0:3],
                                         cv_st[:, j, :].rearrange("p (b k) -> p b k", b=NB))
                link(last)

                def conv(src, dst, pad, width, tiles, w, bias):
                    for k in range(width):
                        for j in range(tiles):
                            pin, pout = src[:, j, k:k + TP], dst[:, j, 0:TP]
                            sin_ = src[:, j, pad + TP:].rearrange("p (b k) -> p b k", b=NB)[:, :, k:k + TD]
                            sout = dst[:, j, TP:T].rearrange("p (b k) -> p b k", b=NB)
                            wk = PR(l, w, k * tiles + j)
                            for a, o in ((pin, pout), (sin_, sout)):
                                if k == 0:
                                    last = V.tensor_scalar(o, a, wk, None, ALU.mult)
                                else:
                                    last = V.scalar_tensor_tensor(o, a, wk, o, ALU.mult, ALU.add)
                        link(last)
                    if bias:
                        for j in range(tiles):
                            last = V.tensor_scalar(dst[:, j, :], dst[:, j, :], PR(l, bias, j), None, ALU.add)
                        link(last)

                conv(xbcp, xbcc, 3, 4, 6, "conv_w", "conv_b")
                signal("xbcc_raw")
                dve.wait_ge(S["scc_ready"], l + 1)
                link(V.memset(chp[:, :, 0:2], 0.0))
                for j in range(4):
                    V.tensor_copy(chp[:, j, 2 + TP:].rearrange("p (b k) -> p b k", b=NB)[:, :, 0:2],
                                  sc_st[:, j, :].rearrange("p (b k) -> p b k", b=NB))
                    dve.wait_ge(*filled(("in", l, 24 + j)))
                    ps = bank_of(("in", l, 24 + j))
                    V.tensor_tensor(chp[:, j, 2:2 + TP], ps[:, 0:TP], scc[:, j, 0:TP], ALU.mult)
                    V.tensor_tensor(chp[:, j, 2 + TP:].rearrange("p (b k) -> p b k", b=NB)[:, :, 2:],
                                    ps[:, TP:T].rearrange("p (b k) -> p b k", b=NB),
                                    scc[:, j, TP:T].rearrange("p (b k) -> p b k", b=NB), ALU.mult)\
                        .then_inc(free(("in", l, 24 + j)), 1)
                dve.wait_ge(*released(("in", l, 27)))
                signal("cols_ready")
                conv(chp, scc, 2, 3, 4, "sc_w", None)
                dve.wait_ge(S["scb_ready"], l + 1)
                V.tensor_tensor(oC, oC, scc, ALU.mult).then_inc(S["oC_ready"], 1)
                dve.wait_ge(S["oC_ready"], l + 1)
                dve.wait_ge(S["cc_done"], 320 * (l + 1))
                signal("sc_conv")

                for c in range(NCHUNK):
                    t0, n = TILES[c]
                    cc = NCHUNK * l + c
                    w = NH * n
                    d3 = decay[0:n, 0:w].rearrange("p (h t) -> p h t", h=NH)
                    up = C("upto0") if c < 2 else C("upto2", TS)
                    mk = C("decay_mask0") if c < 2 else C("decay_mask2", TS)
                    V.tensor_tensor(d3, bc(up, 1, NH), bc(dta[0:n, c, :], 2, n), ALU.mult).then_inc(S["dD_ready"], 1)
                    dve.wait_ge(*filled(("ac", cc)))
                    ps = bank_of(("ac", cc))
                    V.tensor_copy(acs[0:n, :], ps[0:n, 0:2 * NH]).then_inc(free(("ac", cc)), 1)
                    dve.wait_ge(*released(("ac", cc)))
                    V.tensor_tensor(tail[0:n, :], acs[0:n, NH:], acs[0:n, 0:NH], ALU.subtract).then_inc(S["tl_sub"], 1)
                    for part in range(2 if c < 2 else 1):
                        dve.wait_ge(*filled(("acB", cc, part)))
                        ps = bank_of(("acB", cc, part))
                        w2 = min(512, w)
                        V.tensor_copy(eB[:, part * 512:part * 512 + w2], ps[:, 0:w2]).then_inc(free(("acB", cc, part)), 1)
                    dve.wait_ge(*released(("acB", cc, 1 if c < 2 else 0)))
                    link(V.tensor_tensor(d3, eB[0:n, 0:w].rearrange("p (h t) -> p h t", h=NH), bc(acs[0:n, 0:NH], 2, n), ALU.subtract))
                    V.tensor_tensor(d3, d3, bc(mk, 1, NH), ALU.add).then_inc(S["seg_ready"], 1)
                    dve.wait_ge(*filled(("xtok", cc)))
                    ps = bank_of(("xtok", cc))
                    V.tensor_tensor(xdt[0:n, :].rearrange("p (h d) -> p h d", h=NH), ps[0:n, 0:512].rearrange("p (h d) -> p h d", h=NH),
                                    bc(dt[0:n, c, :], 2, HD), ALU.mult).then_inc(free(("xtok", cc)), 1)
                    dve.wait_ge(*released(("xtok", cc)))
                    dve.wait_ge(S["tl_ready"], cc + 1)
                    V.tensor_tensor(xtl[0:n, :].rearrange("p (h d) -> p h d", h=NH), xdt[0:n, :].rearrange("p (h d) -> p h d", h=NH),
                                    bc(tail[0:n, :], 2, HD), ALU.mult).then_inc(S["xdt_ready"], 1)
                    dve.wait_ge(S["dec_exp"], cc + 1)
                    for g in range(NKV):
                        dve.wait_ge(*filled(("CB", cc, g)))
                        ps = bank_of(("CB", cc, g))
                        V.tensor_tensor(d3[:, 4 * g:4 * g + 4, :], d3[:, 4 * g:4 * g + 4, :],
                                        bc(ps[0:n, 0:n], 1, GRP), ALU.mult).then_inc(free(("CB", cc, g)), 1)
                    dve.wait_ge(*released(("CB", cc, 1)))
                    signal("dec_ready")
                    dve.wait_ge(S["eb_ready"], cc + 1)
                    if c == 2:
                        dve.wait_ge(S["hs_in"], 16 * (l + 1))
                    if c > 0:
                        for g in range(NKV):
                            gd = slice(HD * g, HD * g + HD)
                            last = V.tensor_tensor(cp[gd, 0:GRP * n].rearrange("p (h t) -> p h t", h=GRP),
                                                   bc(xbcc[gd, 5, t0:t0 + n], 1, GRP),
                                                   eB[gd, g * GRP * n:(g + 1) * GRP * n].rearrange("p (h t) -> p h t", h=GRP), ALU.mult)
                        last.then_inc(S["cp_ready"], 1)
                    if c == 2:
                        dve.wait_ge(S["btok_ready"], cc + 1)
                        V.tensor_tensor(bm[0:n, :, :], bc(btok[0:n, :], 1, NB), bc(C("in_batch", TS), 2, P), ALU.mult)\
                            .then_inc(S["bm_ready"], 1)
                    dve.wait_ge(S["xbcc_ready"], l + 1)
                    for g in range(NKV):
                        dve.wait_ge(*filled(("y", cc, g)))
                        ps = bank_of(("y", cc, g))
                        for j in range(2):
                            last = V.scalar_tensor_tensor(oS[:, 2 * g + j, t0:t0 + n], xbcc[:, 2 * g + j, t0:t0 + n],
                                                          PR(l, "ssm_d", 2 * g + j), ps[:, j * n:(j + 1) * n], ALU.mult, ALU.add)
                        last.then_inc(free(("y", cc, g)), 1)
                    if c < 2:
                        dve.wait_ge(*filled(("hd", cc)))
                        ps = bank_of(("hd", cc))
                        for g in range(NKV):
                            gd = slice(HD * g, HD * g + HD)
                            new = ps[gd, 0:256].rearrange("p (h d) -> p h d", h=GRP)
                            if c == 0:
                                last = V.tensor_copy(hT[gd, :, :], new)
                            else:
                                e3 = eB[gd, 0:w].rearrange("p (h t) -> p h t", h=NH)[:, 4 * g:4 * g + 4, n - 1]
                                link(V.tensor_tensor(hT[gd, :, :], hT[gd, :, :], bc(e3, 2, HD), ALU.mult))
                                last = V.tensor_tensor(hT[gd, :, :], hT[gd, :, :], new, ALU.add)
                        last.then_inc(free(("hd", cc)), 1)
                        dve.wait_ge(*released(("hd", cc)))
                        signal("h_ready")
                    else:
                        dve.wait_ge(*filled(("hsd", l, 0)))
                        for g in range(NKV):
                            gd = slice(HD * g, HD * g + HD)
                            e4 = eB[gd, 0:w].rearrange("p (h b t) -> p h b t", h=NH, b=NB)[:, 4 * g:4 * g + 4, :, TD - 1]
                            last = V.tensor_tensor(hs[gd, :, :, :], hs[gd, :, :, :],
                                                   bc(e4.rearrange("p h b -> p b h"), 3, HD), ALU.mult)
                        link(last)
                        for b2 in range(NB // 2):
                            dve.wait_ge(*filled(("hsd", l, b2)))
                            ps = bank_of(("hsd", l, b2))
                            hv = hs[:, 2 * b2:2 * b2 + 2, :, :]
                            V.tensor_tensor(hv, hv, ps[:, 0:512].rearrange("p (b h d) -> p b h d", b=2, h=GRP), ALU.add)\
                                .then_inc(free(("hsd", l, b2)), 1)
                        dve.wait_ge(*released(("hsd", l, 3)))
                V.tensor_tensor(oS, oS, zs, ALU.mult).then_inc(S["y_ready"], 1)
                dve.wait_ge(*released(("yss", l)))
                link(V.reciprocal(std[:, :], std[:, :]))
                for j in range(4):
                    last = V.scalar_tensor_tensor(oS[:, j, :], oS[:, j, :], PR(l, "ssm_norm", j), std[:, :], ALU.mult, ALU.mult)
                last.then_inc(S["oS_ready"], 1)
                signal("mix_done")

                for m in range(KD):
                    for k3 in range(3):
                        g_u = use_of[("gate", l, m, k3)]
                        dve.wait_ge(bank_free[g_u % 8], g_u // 8 + 1)
                        gate = gs_[:, (m % 2) * 3 + k3, :]
                        dve.wait_ge(*filled(("proj", l, m, k3)))
                        ps = bank_of(("proj", l, m, k3))
                        dst = tmp[:, m, :] if k3 == 0 else gate
                        V.tensor_tensor(dst, ps[:, 0:T], gate, ALU.mult).then_inc(free(("proj", l, m, k3)), 1)
                        if k3:
                            dve.wait_ge(*released(("proj", l, m, k3)))
                            ins = V.tensor_tensor(tmp[:, m, :], tmp[:, m, :], gate, ALU.add)
                            if k3 == 2:
                                ins.then_inc(S["gate_sig"], 1)
                            else:
                                link(ins)
                signal("merged_ready")
                for m in range(KD):
                    dve.wait_ge(*filled(("o", l, m)))
                    ps = bank_of(("o", l, m))
                    V.tensor_tensor(xT[:, m, :], xT[:, m, :], ps[:, 0:T], ALU.add).then_inc(free(("o", l, m)), 1)
                signal("x_ready")
                rms(l, 1, "norm_ffn")
                if l == 0:
                    for f in range(NFD):
                        g_u = use_of[("fg", f)]
                        dve.wait_ge(bank_free[g_u % 8], g_u // 8 + 1)
                        dve.wait_ge(*filled(("fu", f)))
                        ps = bank_of(("fu", f))
                        V.tensor_tensor(h[:, f, :], gs_[:, f % 2, :], ps[:, 0:T], ALU.mult).then_inc(free(("fu", f)), 1)
                    for m in range(KD):
                        dve.wait_ge(*filled(("fd", m)))
                        ps = bank_of(("fd", m))
                        V.tensor_tensor(xT[:, m, :], xT[:, m, :], ps[:, 0:T], ALU.add).then_inc(free(("fd", m)), 1)
                    signal("x_ready")
                    dve.wait_ge(*released(("fd", 7)))

            link(V.memset(rl, 0.0))
            dve.wait_ge(*filled(("router",)))
            ps = bank_of(("router",))
            V.tensor_copy(rl[0:TS, 2, :], ps[0:TS, 16:24])
            V.tensor_copy(rl[:, 0:2, :], ps[:, 0:16].rearrange("p (a b) -> p a b", a=2)).then_inc(free(("router",)), 1)
            dve.wait_ge(*released(("router",)))
            prefer = bc(C("exp_rank"), 1, 3)

            def best(src, sel, m):
                link(V.tensor_reduce(m, src, AX.X, ALU.max))
                link(V.tensor_tensor(sel, src, m.to_broadcast([P, 3, NE]), ALU.is_equal))
                link(V.tensor_tensor(sel, sel, prefer, ALU.mult))
                link(V.tensor_reduce(rg1, sel, AX.X, ALU.max))
                link(V.tensor_tensor(sel, prefer, rg1.to_broadcast([P, 3, NE]), ALU.is_equal))

            best(rl, rs1, rm1)
            link(V.scalar_tensor_tensor(rl2, rs1, NEG, rl, ALU.mult, ALU.add))
            best(rl2, rs2, rm2)
            V.tensor_tensor(mask, rs1, rs2, ALU.add).then_inc(S["cnt_ready"], 1)
            V.tensor_tensor(re, rm2, rm1, ALU.subtract).then_inc(S["re_sub"], 1)
            dve.wait_ge(S["re_exp"], 1)
            link(V.tensor_scalar(rg1, re, 1.0, None, ALU.add))
            link(V.reciprocal(rg1, rg1))
            link(V.tensor_tensor(rg2, re, rg1, ALU.mult))
            link(V.tensor_tensor(rt, rs1, rg1.to_broadcast([P, 3, NE]), ALU.mult))
            link(V.tensor_tensor(rs2, rs2, rg2.to_broadcast([P, 3, NE]), ALU.mult))
            link(V.tensor_tensor(rt, rt, rs2, ALU.add))
            dve.wait_ge(*filled(("cnt",)))
            ps = bank_of(("cnt",))
            link(V.tensor_copy(cnt, ps[:, 0:NE]))
            V.tensor_copy(rank[0:TS, 2, :], ps[0:TS, 3 * NE:4 * NE])
            V.tensor_copy(rank[:, 0:2, :], ps[:, NE:3 * NE].rearrange("p (a b) -> p a b", a=2)).then_inc(free(("cnt",)), 1)
            dve.wait_ge(*released(("cnt",)))
            link(V.scalar_tensor_tensor(rank, rank, 1000.0, mask, ALU.add, ALU.mult))
            link(V.tensor_scalar(rank, rank, -1000.0, None, ALU.add))
            link(V.tensor_scalar(runs, cnt, float(CAP), 1.0, ALU.is_gt, ALU.add))
            link(V.tensor_scalar(en1, cnt, 2.0 * CAP, None, ALU.is_gt))
            link(V.tensor_tensor(runs, runs, en1, ALU.add))
            src = runs
            for step, dst in ((1, en1), (2, en2), (4, en3)):
                V.tensor_copy(dst[:, 0:step], src[:, 0:step])
                link(V.tensor_tensor(dst[:, step:NE], src[:, step:NE], src[:, 0:NE - step], ALU.add))
                src = dst
            link(V.tensor_tensor(le, bc(en3, 1, 16), bc(C("iota")[:, 0:16], 2, NE), ALU.is_le))
            link(V.tensor_reduce(tabf[:, 0:16], le, AX.X, ALU.add))
            link(V.tensor_scalar(tabf[:, 0:16], tabf[:, 0:16], NE - 1.0, None, ALU.min))
            link(V.tensor_tensor(lei, le, bc(runs, 1, 16), ALU.mult))
            link(V.tensor_reduce(tabf[:, 16:32], lei, AX.X, ALU.add))
            link(V.tensor_tensor(tabf[:, 16:32], C("iota")[:, 0:16], tabf[:, 16:32], ALU.subtract))
            link(V.tensor_scalar(tabf[:, 16:32], tabf[:, 16:32], float(CAP), 2.0 * CAP, ALU.mult, ALU.min))
            V.tensor_copy(tabf[:, 32:33], en3[:, NE - 1:NE])
            link(V.memset(tabf[:, 33:48], 0.0))
            V.tensor_copy(passes[0:1, :], tabf[0:1, :]).then_inc(S["table_ready"], 1)
            dve.wait_ge(S["table_ready"], 1)

            def make_pick(i):
                ex = dve.value_load(passes[0:1, bass.ds(i, 1)], min_val=0, max_val=NE - 1)
                slot = dve.value_load(passes[0:1, bass.ds(i + 16, 1)], min_val=0, max_val=2 * CAP)
                for tt, (t0, n) in enumerate(TILES):
                    mine = rank[0:n, tt, bass.ds(ex, 1)]
                    slots = C("iota", n)[:, bass.ds(slot, CAP)]
                    V.tensor_scalar(pickw[0:n, tt, :], slots, mine, rt[0:n, tt, bass.ds(ex, 1)], ALU.is_equal, ALU.mult)
                    last = V.tensor_scalar(pick[0:n, tt, :], slots, mine, None, ALU.is_equal)
                last.then_inc(S["pick_ready"], 1)

            V.memset(yT, 0.0)
            link(V.memset(pickw, 0.0))
            V.memset(spread, 0.0).then_inc(S["zero_ready"], 1)
            make_pick(0)
            n_pass = dve.value_load(passes[0:1, 32:33], min_val=NE, max_val=MAX_PASSES)

            def add_scatter(key, it):
                for m in range(KD):
                    dve.wait_ge(*filled((key, m), it))
                    ps = bank_of((key, m))
                    last = V.tensor_tensor(xT[:, m, :], xT[:, m, :], ps[:, 0:T], ALU.add)
                    last.then_inc(free((key, m)), 1)

            with dve.Fori(0, n_pass) as i:
                def up(q):
                    dve.wait_ge(S["silu_ready"], i * (NFE // 2) + q + 1)
                    dve.wait_ge(*filled(("gu", q), i))
                    ps = bank_of(("gu", q))
                    V.tensor_tensor(he[:, 2 * q:2 * q + 2, :], sg[:, q % 2, :].rearrange("p (a b) -> p a b", a=2),
                                    ps[:, 2 * CAP:4 * CAP].rearrange("p (a b) -> p a b", a=2), ALU.mult)\
                        .then_inc(free(("gu", q)), 1)

                for q in range(4):
                    up(q)
                add_scatter("sc", i)
                dve.wait_ge(*filled(("sp", 2), i))
                make_pick(i + 1)
                for q in range(4, NFE // 2):
                    up(q)
            add_scatter("sc_last", n_pass - 1)
            signal("x_ready")


def blocks(w):
    K, N = w.shape
    return w.reshape(K // P, P, N // P, P).transpose(2, 0, 1, 3)


def head_tiles(cols):
    return cols.reshape(NKV, GRP, HD).transpose(1, 0, 2).reshape(-1)


def weight_stream(a):
    out = np.empty((N_SLOTS * BPS, P, P), np.float32)
    at = 0

    def put(b):
        nonlocal at
        b = b.reshape(-1, P, P)
        out[at:at + len(b)] = b
        at += len(b)

    for l in range(DEPTH):
        w = a["w_in"][l]
        q = w[:, 0:512][:, head_tiles(np.arange(512))]
        kv = w[:, 512:1280].reshape(D, 3, 2, P)
        put(blocks(q))
        put(blocks(kv[:, :, 0].reshape(D, 3 * P)))
        put(blocks(kv[:, :, 1].reshape(D, 3 * P)))
        cm = np.zeros((2, 32, P, P), np.float32)
        for g in range(NKV):
            cm[:, :, g * HD:(g + 1) * HD, g * HD:(g + 1) * HD] = a["w_cmp"][l]
        put(cm)
        put(cm)
        put(blocks(w[:, 1816:2584]))
        put(blocks(w[:, 1304:1816]))
        put(blocks(w[:, 3104:3616]))
        put(blocks(w[:, 3616:4128]))
        put(blocks(w[:, 2592:3104]))
        mg = blocks(w[:, 4128:]).reshape(3, KD, KD, P, P)
        wb = a["w_branch"][l]
        br = np.stack([blocks(wb[0][head_tiles(np.arange(512))]), blocks(wb[1]), blocks(wb[2])])
        for m in range(KD):
            put(mg[:, m])
            put(br[:, m])
        put(blocks(a["w_out"][l]))
        if l == 0:
            put(np.stack([blocks(a["ffn_w_gate"][0]), blocks(a["ffn_w_up"][0])], 1))
            put(blocks(a["ffn_w_down"][0]))
    for e in range(NE):
        put(np.stack([blocks(a["moe_w_gate"][0, e]), blocks(a["moe_w_up"][0, e])], 1))
        put(blocks(a["moe_w_down"][0, e]))
    assert at == len(out)
    return np.ascontiguousarray(out.reshape(N_SLOTS, BPS, P, P).transpose(0, 2, 1, 3)).reshape(N_SLOTS, P, SLOTF)


def feature_cols(v, n):
    return v.reshape(-1, P).T.reshape(P, -1)


def layer_params(a):
    out = np.zeros((P, DEPTH, N_PAR), np.float32)

    def put(l, name, v):
        at, n = PAR_AT[name]
        out[:, l, at:at + n] = v.reshape(P, n)

    for l in range(DEPTH):
        put(l, "norm_mix", feature_cols(a["norm_mix"][l], KD))
        put(l, "norm_ffn", feature_cols(a["norm_ffn"][l], KD))
        qk = np.concatenate([np.tile(a["q_norm"][l], (4, 2)), np.tile(a["k_norm"][l], (1, 2))])
        put(l, "qk_norm", np.ascontiguousarray(qk.T))
        put(l, "conv_w", feature_cols(a["ssm_conv_w"][l], 6))
        put(l, "conv_b", feature_cols(a["ssm_conv_b"][l], 6))
        put(l, "ssm_d", feature_cols(np.repeat(a["ssm_d"][l], HD), 4))
        put(l, "ssm_norm", feature_cols(a["ssm_norm"][l], 4))
        put(l, "sc_w", feature_cols(a["sc_conv_w"][l], 4))
        put(l, "dt_bias", np.tile(a["ssm_dt_bias"][l], (P, 1)))
        put(l, "a_log", np.tile(a["ssm_a_log"][l], (P, 1)))
        w = a["w_in"][l]
        sm = np.concatenate([w[:, 1280:1304], w[:, 2584:2592]], 1)
        put(l, "w_small", np.ascontiguousarray(sm.reshape(KD, P, 32).transpose(1, 0, 2)))
        if l == 1:
            put(l, "router", np.ascontiguousarray(a["moe_router"][0].reshape(KD, P, NE).transpose(1, 0, 2)))
    return out.reshape(P, -1)


def kernel(**inputs):
    import concourse.bacc as bacc
    from concourse.bass_utils import run_bass_kernel_spmd

    a = {k: np.asarray(v) for k, v in inputs.items()}
    nc = bacc.Bacc("TRN2", target_bir_lowering=False, num_devices=1)
    arrays, args = {}, []

    def ext(name, arr):
        arr = np.ascontiguousarray(arr)
        arrays["in_" + name] = arr
        args.append(nc.dram_tensor("in_" + name, arr.shape, mybir.dt.from_np(arr.dtype), kind="ExternalInput").ap())

    def out(name, shape):
        args.append(nc.dram_tensor("out_" + name, shape, mybir.dt.float32, kind="ExternalOutput").ap())

    x = np.concatenate([a["x_prompt"].reshape(TP, D), a["x_sample"].reshape(TS, D)])
    ext("xT", x.reshape(T, KD, P).transpose(2, 1, 0).reshape(P, -1))
    ext("consts", np.concatenate([np.ascontiguousarray(v) for v in CONST.values()], 1))
    ext("params", layer_params(a))
    ext("wstream", weight_stream(a))
    ext("page_table", a["page_table"].reshape(1, -1))
    pg = a["cache_nsa_pages"]
    n_pool = pg.shape[1]
    pg = pg.reshape(DEPTH * n_pool, PAGE, 4, P)
    ext("kc_pages", pg[:, :, 0].transpose(0, 2, 1))
    ext("vc_pages", pg[:, :, 1].transpose(0, 2, 1))
    ext("slc_pages", np.stack([pg[:, :, 2].transpose(0, 2, 1), pg[:, :, 3]], 2).reshape(DEPTH * n_pool, P, 2 * P))
    win = a["cache_nsa_window"].reshape(DEPTH, NB, WIN, 2, P)
    ext("win_kT", win[:, :, :, 0].transpose(0, 3, 1, 2))
    ext("win_v", win[:, :, :, 1].reshape(DEPTH, NB, 4, P, P).transpose(0, 1, 3, 2, 4))
    ext("win_rows", win.reshape(DEPTH, NB, WIN, 2 * P))
    st = a["state_ssm"].reshape(DEPTH, NB, NKV, GRP, HD, SSMN).transpose(0, 2, 5, 1, 3, 4)
    ext("ssm_in", st.reshape(DEPTH, P, NB, GRP, HD))
    ext("conv_in", a["state_ssm_conv"].reshape(DEPTH, NB, 3, 6, P).transpose(0, 4, 3, 1, 2).reshape(DEPTH, P, 6, NB * 3))
    ext("sc_in", a["state_shortconv"].reshape(DEPTH, NB, 2, 4, P).transpose(0, 4, 3, 1, 2).reshape(DEPTH, P, 4, NB * 2))
    out("y", (P, KD * T))
    out("kv", (DEPTH, P, 6, T))
    out("win_keep", (DEPTH, NB, WIN - TD, 2 * P))
    out("ssm_p", (DEPTH, P, GRP, HD))
    out("ssm_s", (DEPTH, P, NB, GRP, HD))
    out("conv_last", (DEPTH, P, 6, 3 + NB * 3))
    out("sc_last", (DEPTH, P, 4, 2 + NB * 2))
    build(nc, *args)
    res = run_bass_kernel_spmd(nc, [arrays], core_ids=[0]).results[0]
    r = {k[4:]: res[k] for k in res if k.startswith("out_")}

    y = r["y"].reshape(P, KD, T).transpose(2, 1, 0).reshape(T, D)
    kv = r["kv"].reshape(DEPTH, NKV, HD, 2, 3, T).transpose(0, 5, 4, 3, 1, 2)
    rows = kv[:, :, 0:2].reshape(DEPTH, T, 4, NKV, HD)
    wkv = kv[:, :, 2]
    nsa_p = np.ascontiguousarray(rows[:, :TP]).reshape(DEPTH, 1, TP, 4, NKV, HD)
    nsa_s = np.ascontiguousarray(rows[:, TP:]).reshape(DEPTH, NB, TD, 4, NKV, HD)
    win_p = np.ascontiguousarray(wkv[:, :TP]).reshape(DEPTH, 1, TP, 2, NKV, HD)
    win_s = np.concatenate([r["win_keep"].reshape(DEPTH, NB, WIN - TD, 2, NKV, HD),
                            wkv[:, TP:].reshape(DEPTH, NB, TD, 2, NKV, HD)], 2)
    ssm_p = r["ssm_p"].reshape(DEPTH, NKV, SSMN, GRP, HD).transpose(0, 1, 3, 4, 2).reshape(DEPTH, 1, NH, HD, SSMN)
    ssm_s = r["ssm_s"].reshape(DEPTH, NKV, SSMN, NB, GRP, HD).transpose(0, 3, 1, 4, 5, 2).reshape(DEPTH, NB, NH, HD, SSMN)
    cl = r["conv_last"]
    conv_p = cl[:, :, :, 0:3].transpose(0, 3, 2, 1).reshape(DEPTH, 1, 3, XBC)
    conv_s = cl[:, :, :, 3:].reshape(DEPTH, P, 6, NB, 3).transpose(0, 3, 4, 2, 1).reshape(DEPTH, NB, 3, XBC)
    sl = r["sc_last"]
    sc_p = sl[:, :, :, 0:2].transpose(0, 3, 2, 1).reshape(DEPTH, 1, 2, SC)
    sc_s = sl[:, :, :, 2:].reshape(DEPTH, P, 4, NB, 2).transpose(0, 3, 4, 2, 1).reshape(DEPTH, NB, 2, SC)
    return tuple(np.ascontiguousarray(v) for v in (
        y[:TP].reshape(1, TP, D), y[TP:].reshape(NB, TD, D), nsa_p, nsa_s, win_p, win_s, ssm_p, ssm_s,
        conv_p, conv_s, sc_p, sc_s))
```

```python
import math
from contextlib import ExitStack

import numpy as np
import concourse.bass as bass
from concourse import mybir

D, DEPTH = 1024, 2
TP, NB, TD = 256, 8, 4
TS = NB * TD
T = TP + TS
PAST, PAGE, WIN = 1024, 128, 512
NPG = PAST // PAGE
NH, NKV, HD, GRP = 8, 2, 64, 4
STRIDE, NCS, NCP = 16, 63, 15
SEL, NMID = 64, 14
SSMI, SSMN, XBC, SC = 512, 64, 768, 512
FF, FE, NE = 2816, 3584, 8
EPS, NEG = 1e-6, -1e30
P = 128
KD = D // P
HALF = NB // 2

BPS = 16
RING = 6
MARKS = 32
CAP = 96
MAX_PASSES = NE + 2 * (TP + NB * TD) // (CAP + 1)
SLOTF = BPS * P
NQKV = 10
REST = ([("x", j) for j in range(6)] + [("z", j) for j in range(4)] + [(k, j) for j in range(4) for k in "ch"]
        + [("b", j) for j in range(4)])
NREST = len(REST)
EARLY = 3
UNIT_REST = [None if n in (3, 6, 9) else EARLY + n - n // 3 for n in range(12)]
CMP1_UNIT = 3
MERGE = [(br, m) for br in (0, 2, 1) for m in range(KD)]
GROUPS = [range(u, u + 2) for u in range(0, 2 * KD, 2)] + [range(u, u + 4) for u in range(2 * KD, 3 * KD, 4)]
NCMPB = 64
MIX_BLOCKS = NQKV * KD + 2 * NCMPB + NREST * KD + 3 * KD * KD + 12 * KD + KD * KD
NFD, NFE = FF // P, FE // P
FFN_BLOCKS = NFD * 3 * KD
EXP_BLOCKS = NFE * 3 * KD
LAYER_SLOT = [0, (MIX_BLOCKS + FFN_BLOCKS) // BPS]
PRE_SLOTS = (2 * MIX_BLOCKS + FFN_BLOCKS) // BPS
EXP_SLOTS = EXP_BLOCKS // BPS
N_SLOTS = PRE_SLOTS + NE * EXP_SLOTS
assert (MIX_BLOCKS % BPS, FFN_BLOCKS % BPS, EXP_BLOCKS % BPS, EXP_SLOTS % RING) == (0, 0, 0, 0)

TILES = [(0, 128), (128, 128), (256, 32)]
NCHUNK = 3


def constants():
    c = {}
    eye = np.eye(P, dtype=np.float32)
    i = np.arange(P)
    c["eps"] = np.full((P, 1), EPS, np.float32)
    c["ident"] = eye
    c["ones"] = np.ones((P, P), np.float32)
    c["head_ones"] = (i[:, None] // HD == i[None, :] // HD).astype(np.float32)
    rot = np.zeros((P, P), np.float32)
    for m in range(P):
        if m % HD < HD // 2:
            rot[m + HD // 2, m] = -1.0
        else:
            rot[m - HD // 2, m] = 1.0
    c["rot"] = rot
    row_b, row_g, row_r, row_t = i // 32, i // 16 % 2, i // 4 % 4, i % 4
    grp = row_b * 8 + row_g * 4 + row_t
    c["group_sum"] = (grp[:, None] == grp[None, :]).astype(np.float32)
    half = HD // 2
    inv = np.exp(np.float32(-math.log(10000.0)) * np.arange(half, dtype=np.float32) / np.float32(half)).astype(np.float32)
    pos = np.concatenate([np.arange(TP), PAST + np.tile(np.arange(TD), NB)]).astype(np.float32)
    ang = (pos[None, :] * inv[i % half][:, None]).astype(np.float32)
    c["cos"], c["sin"] = np.cos(ang).astype(np.float32), np.sin(ang).astype(np.float32)
    c["causal0"] = np.where(i[None, :] <= i[:, None], 0, NEG).astype(np.float32)
    c["causal1"] = np.where(np.arange(TP)[None, :] <= i[:, None] + P, 0, NEG).astype(np.float32)
    end = np.arange(NCP) * STRIDE + 31
    qp = i[:, None] + P * np.arange(2)[None, :]
    vis = end[None, None, :] <= qp[:, :, None]
    c["cmp_mask"] = np.where(vis, 0, NEG).astype(np.float32).reshape(P, -1)
    c["cmp_any"] = vis.any(-1).astype(np.float32)
    tb, tt = np.arange(TS) // TD, np.arange(TS) % TD
    new = [np.where((tb[None, :] == (row_b + HALF * h)[:, None]) & (tt[None, :] <= row_t[:, None]), 0, NEG) for h in range(2)]
    c["new_mask"] = np.concatenate(new, 1).astype(np.float32)
    c["win_mask"] = np.where(np.arange(TD)[None, :] > row_t[:, None], 0, NEG).astype(np.float32)
    c["blk_idx"] = np.broadcast_to(np.arange(1, NMID + 1, dtype=np.float32), (P, NMID))
    c["upto0"] = (i[:, None] <= i[None, :]).astype(np.float32)
    c["decay_mask0"] = ((1 - c["upto0"]) * NEG).astype(np.float32)
    same = tb[:, None] == tb[None, :]
    up = np.zeros((P, TS), np.float32)
    up[:TS] = same & (tt[:, None] <= tt[None, :])
    c["upto2"] = up
    c["decay_mask2"] = ((1 - up) * NEG).astype(np.float32)
    sb = np.zeros((P, TS), np.float32)
    sb[:TS] = same
    c["same2"] = sb
    bc = np.zeros((P, NB), np.float32)
    bc[:TS] = tb[:, None] == np.arange(NB)[None, :]
    c["in_batch"] = bc
    c["iota"] = np.broadcast_to(np.arange(3 * CAP, dtype=np.float32), (P, 3 * CAP))
    c["before"] = (i[:, None] < i[None, :]).astype(np.float32)
    c["exp_rank"] = np.broadcast_to(NE - np.arange(NE, dtype=np.float32), (P, NE))
    sel = np.zeros((P, 12, P), np.float32)
    for br in range(3):
        for r in range(GRP):
            for g in range(NKV):
                sel[(g * GRP + r) * 3 + br, br * GRP + r, g * HD:(g + 1) * HD] = 1
    c["gate_sel"] = sel.reshape(P, -1)
    return c


CONST = constants()
CONST_AT, _n = {}, 0
for _k, _v in CONST.items():
    CONST_AT[_k] = (_n, _v.shape[1])
    _n += _v.shape[1]
N_CONST = _n
FIRST_CONST = CONST_AT["ones"][0] + CONST_AT["ones"][1]

PAR = {"norm_mix": KD, "norm_ffn": KD, "qk_norm": 7, "conv_w": 4 * 6, "conv_b": 6, "ssm_d": 4, "ssm_norm": 4,
       "sc_w": 3 * 4, "dt_bias": NH, "a_log": NH, "w_small": KD * 32, "router": KD * NE}
PAR_AT, _n = {}, 0
for _k, _v in PAR.items():
    PAR_AT[_k] = (_n, _v)
    _n += _v
N_PAR = _n

XBCW = 3 + TP + NB * (3 + TD)
SCW = 2 + TP + NB * (2 + TD)


def build(nc, xT_in, consts, params, wstream, page_table, cmp_pages, slc_pages, win_kT, win_v, win_rows,
          ssm_in, conv_in, sc_in, y_out, kv_out, win_out, ssm_p_out, ssm_s_out, conv_out, sc_out):
    f32, i32 = mybir.dt.float32, mybir.dt.int32
    ALU, ACT, AX = mybir.AluOpType, mybir.ActivationFunctionType, mybir.AxisListType
    V, A = nc.vector, nc.scalar

    with ExitStack() as ctx:
        def sb(name, cols, dt=f32):
            return ctx.enter_context(nc.sbuf_tensor(name, [P, cols], dt))

        def sem(name):
            return ctx.enter_context(nc.semaphore(name))

        xT_ = sb("xT", KD * T)
        xn_ = sb("xn", KD * T)
        tmp_ = sb("tmp", KD * T)
        oN_ = sb("o_nsa", 4 * T)
        oS_ = sb("o_ssm", 4 * T)
        oC_ = sb("o_sc", 4 * T)
        wring = sb("wring", RING * SLOTF)
        pages = sb("pages", 3 * 4096)
        cst = sb("cst", N_CONST)
        par = sb("par", DEPTH * N_PAR)
        std = sb("std", T)
        mark = sb("mark", 2 * MARKS)
        REG = 12100
        reg = sb("phase_region", REG)
        ptab = sb("ptab", NB * NPG, i32)
        passes = sb("passes", 3 * 16, i32)

        def view(t, off, *dims):
            n = int(np.prod(dims))
            ap = t[:, off:off + n]
            if len(dims) == 2:
                ap = ap.rearrange("p (a b) -> p a b", b=dims[1])
            elif len(dims) == 3:
                ap = ap.rearrange("p (a b c) -> p a b c", b=dims[1], c=dims[2])
            elif len(dims) == 4:
                ap = ap.rearrange("p (a b c d) -> p a b c d", b=dims[1], c=dims[2], d=dims[3])
            return ap

        xT, xn, tmp = (view(t, 0, KD, T) for t in (xT_, xn_, tmp_))
        oN, oS, oC = (view(t, 0, 4, T) for t in (oN_, oS_, oC_))

        class Region:
            def __init__(self, at):
                self.at = at

            def __call__(self, *dims):
                ap = view(reg, self.at, *dims)
                self.at += int(np.prod(dims))
                assert self.at <= REG, self.at
                return ap

        ra = Region(0)
        qkv = ra(NQKV, T)
        vtok = ra(3, 3, P)
        otok = ra(2, GRP, NKV, HD)
        gates = ra(3, 24)
        small = ra(3, 32)
        gT = ra(TS)
        gB = ra(3, GRP, TS)
        kvT = [(ra(HALF, NCS), ra(HALF, NCS)), (view(oC_, 0, HALF, NCS), view(oC_, HALF * NCS, HALF, NCS))]
        kcTp, vcTp = ra(NCP + 1), ra(NCP + 1)
        vcp = ra(P)
        mx, ssum, rsum, coef = ra(2, GRP), ra(2, GRP), ra(GRP), ra(GRP)
        scratch = ra.at
        rq = view(reg, scratch, 7, T)
        rp = Region(scratch)
        S_p = [rp(1024), rp(1024)]
        PT_p = rp(2, 4 * P)
        otmp = rp(GRP, HD)
        rs_ = Region(scratch)
        qbd = rs_(NB, 32)
        vc = rs_(HALF, P)
        S_s = rs_(PAST + TS)
        PT_s = rs_(9, P)
        S_c = rs_(64)
        PT_c = rs_(P)
        imp, drop, tie, m1 = rs_(NMID), rs_(NMID), rs_(NMID), rs_(4)
        orow = rs_(3, P)
        smx, ssm, srs = rs_(4), rs_(4), rs_(4)
        osam = rs_(2, HALF * 16)
        rt_ = Region(REG - 2 * T - 4 * SCW - 4 * NB * 2 - 6 * NB * 3)
        assert rt_.at >= max(rp.at, rs_.at)
        scc = rt_(2, T)
        chp = rt_(4, SCW)
        sc_st = rt_(4, NB * 2)
        cv_st = rt_(6, NB * 3)
        xbcp = view(tmp_, 0, 6, XBCW)
        rb = Region(0)
        dt = rb(3, NH)
        dta = rb(3, NH)
        sp_v, sp_e, sp_z, sp_q, sp_p = (rb(3, NH) for _ in range(5))
        ea = rb(NH)
        xbcc = rb(6, T)
        b_scratch = rb.at
        rc = Region(b_scratch)
        sconv = rc(4, T)
        rd = Region(b_scratch)
        decay = rd(1024)
        eB = rd(1024)
        cp = rd(GRP * P)
        xdt = rd(SSMI)
        xtl = rd(SSMI)
        btok = rd(P)
        hT = rd(GRP, HD)
        acs = rd(2 * NH)
        tail = rd(NH)
        hs_at = rd.at
        hs = rd(NB, GRP, HD)
        bm = rd(NB, P)
        merged = rd(KD, T)
        assert max(rc.at, rd.at - KD * T) <= REG - 2 * T - 4 * SCW - 4 * NB * 2 - 6 * NB * 3
        early_gates = view(reg, hs_at, 4, T)

        def gate_buffer(u):
            return early_gates[:, u, :] if u < 4 else tmp[:, 4 + u % 4, :]

        rf = Region(0)
        h = rf(NFD, T)
        gs_ = rf(2, T)
        rm = Region(0)
        xtok = rm(3, D)
        he = rm(NFE, CAP)
        xe = rm(KD, CAP)
        pick, pickw = rm(3, CAP), rm(3, CAP)
        spread = rm(T)
        yT, yS = rm(KD, CAP), rm(KD, P)
        sg = rm(2, 2 * CAP)
        rl, rl2, rs1, rs2, rt, rank, mask = (rm(3, NE) for k in range(7))
        rm1, rm2, re, rg1, rg2 = (rm(3, 1) for k in range(5))
        cnt, runs, en1, en2, en3 = (rm(NE) for k in range(5))
        le, lei = rm(16, NE), rm(16, NE)
        tabf = rm(3 * 16)

        def C(name, rows=P):
            a, n = CONST_AT[name]
            return cst[0:rows, a:a + n]

        def PR(l, name, i=0, n=1):
            a, _ = PAR_AT[name]
            a += l * N_PAR + i
            return par[:, a:a + n]

        def bc(ap, axis, n):
            a = ap.unsqueeze(axis)
            shape = list(a.shape)
            shape[axis] = n
            return a.to_broadcast(shape)

        psum = [ctx.enter_context(nc.psum_tensor(f"bank{i}", [P, 512], f32)) for i in range(8)]
        bank_full = [sem(f"bank_full{i}") for i in range(8)]
        bank_free = [sem(f"bank_free{i}") for i in range(8)]
        w_full = [sem(f"w_full{i}") for i in range(RING)]
        w_free = [sem(f"w_free{i}") for i in range(RING)]
        pg_full = [sem(f"pg_full{i}") for i in range(3)]
        names = ("const_in tables_in x_in ptab_in sq_ready xn_ready x_ready small_ready gates_ready qkv_ready qksq_ready "
                 "qk_normed qk_ready vtok_ready vcT_ready vc_ready smax exp_ready pt_ready otok_ready "
                 "qbd_ready scmax sc_exp pc_ready ptc_ready ssmax ss_exp pts_ready orow_ready gT_ready attn_done "
                 "st_in xbcc_raw xbcc_ready cols_ready spa sp_exp ea_ready dD_ready eb_ready seg_ready dec_exp "
                 "dec_ready tl_sub tl_ready cp_ready xdt_ready btok_ready h_ready bm_ready y_ready ysq_ready "
                 "oS_ready part_sum merged_ready silu_ready cnt_ready pick_ready table_ready zero_ready "
                 "re_sub re_exp kv_done hp_done hs_done cc_done win_done dve_chain act_chain zeroed y_done "
                 "oC_ready hs_in").split()
        S = {n: sem(n) for n in names}

        use_of = {}
        moe_base = [0]
        MOE_USES = 32
        assert MOE_USES % 8 == 0

        def filled(key, it=None):
            u = use_of[key]
            n = u // 8 + 1
            return bank_full[u % 8], n if it is None else it * (MOE_USES // 8) + n

        def released(key, it=None, back=0):
            u = use_of[key]
            n = u // 8 + 1 - back * (MOE_USES // 8)
            return bank_free[u % 8], n if it is None else it * (MOE_USES // 8) + n

        def bank_of(key):
            return psum[use_of[key] % 8]

        def free(key):
            return bank_free[use_of[key] % 8]

        DOWN = ((0, 3), (3, 3), (6, 2))

        FILLS = [(l, hf, what) for l in range(DEPTH) for hf, what in (
            (0, "cmp0"), (0, "cmp1"), (1, "cmp0"), (1, "cmp1"),
            (0, "win"), (0, "slc0"), (0, "slc1"), (1, "slc0"), (1, "win"), (1, "slc1"))]
        fill_dmas = {"cmp0": 2 * NPG, "cmp1": 2 * NPG, "slc0": 2 * NPG, "slc1": 2 * NPG, "win": 1 + HALF}
        fill_at, fill_sum = {}, [0, 0, 0]
        for n, f in enumerate(FILLS):
            fill_sum[n % 3] += 16 * fill_dmas[f[2]]
            fill_at[f] = (n % 3, fill_sum[n % 3])

        def page_slot(f):
            return 4096 * fill_at[f][0]

        UNITS = [(g, qt, br) for g in range(NKV) for qt in range(2) for br in range(3)]

        block = ctx.enter_context(nc.Block())

        @block.tensor
        def _(pe):
            uses = [0]
            blk = [0]
            last_slot = [-1]

            def bank(key):
                u = uses[0]
                uses[0] += 1
                use_of[key] = u
                if u >= 8:
                    pe.wait_ge(bank_free[u % 8], u // 8)
                return psum[u % 8], bank_full[u % 8]

            def wblock():
                n = blk[0]
                blk[0] += 1
                s, o = divmod(n, BPS)
                release = None
                if s != last_slot[0]:
                    pe.wait_ge(w_full[s % RING], 16 * (s // RING + 1))
                    if s > 0:
                        release = w_free[(s - 1) % RING]
                    last_slot[0] = s
                a = (s % RING) * SLOTF + o * P
                return wring[:, a:a + P], release

            def product(key, n, rhs, width=T, w=wblock):
                ps, done = bank(key)
                for k in range(n):
                    wb, release = w()
                    mm = nc.tensor.matmul(ps[:, 0:width], wb, rhs(k), start=(k == 0), stop=(k == n - 1))
                    if release is not None:
                        mm.then_inc(release, 1)
                mm.then_inc(done, 1)

            def column_sum(key, n, lhs, rhs):
                ps, done = bank(key)
                for k in range(n):
                    mm = nc.tensor.matmul(ps[:, 0:T], lhs, rhs(k), start=(k == 0), stop=(k == n - 1))
                mm.then_inc(done, 1)

            def rms_sum(l, which):
                ps, done = bank(("ss", l, which))
                for k in range(KD):
                    pe.wait_ge(S["sq_ready"], KD * (2 * l + which) + k + 1)
                    mm = nc.tensor.matmul(ps[:, 0:T], C("ones"), tmp[:, k, :], start=(k == 0), stop=(k == KD - 1))
                mm.then_inc(done, 1)

            def normed_tile(k):
                pe.wait_ge(S["xn_ready"], KD + k + 1)
                return xn[:, k, :]

            ident = C("ident")
            pe.wait_ge(S["const_in"], 32)
            for l in range(DEPTH):
                rms_sum(l, 0)
                pe.wait_ge(S["xn_ready"], KD * (2 * l + 1))
                ps, done = bank(("small", l))
                for tt, (t0, n) in enumerate(TILES):
                    for k in range(KD):
                        mm = nc.tensor.matmul(ps[0:n, 32 * tt:32 * tt + 32], xn[:, k, t0:t0 + n],
                                              PR(l, "w_small", 32 * k, 32), start=(k == 0), stop=(k == KD - 1))
                mm.then_inc(done, 1)
                for i in range(NQKV):
                    product(("in", l, i), KD, lambda k: xn[:, k, :])
                if l == 0:
                    pe.wait_ge(S["tables_in"], 16)
                for i in range(7):
                    pe.wait_ge(S["qksq_ready"], 7 * l + i + 1)
                    column_sum(("qkss", l, i), 1, C("head_ones"), lambda k: tmp[:, i, :])
                pe.wait_ge(S["qkv_ready"], l + 1)
                for tt, (t0, n) in enumerate(TILES):
                    ps, done = bank(("vt", l, tt))
                    for br in range(3):
                        mm = nc.tensor.transpose(ps[0:n, br * P:(br + 1) * P], qkv[:, 7 + br, t0:t0 + n], ident)
                    mm.then_inc(done, 1)
                pe.wait_ge(S["gates_ready"], l + 1)
                ps, done = bank(("gT", l))
                nc.tensor.transpose(ps[0:24, 0:TS], gates[0:TS, 2, :], C("ident", TS)[:, 0:TS]).then_inc(done, 1)
                pe.wait_ge(S["gT_ready"], l + 1)
                ps, done = bank(("gB", l))
                for j in range(12):
                    mm = nc.tensor.matmul(ps[:, j * TS:(j + 1) * TS], C("gate_sel", 24)[:, j * P:(j + 1) * P],
                                          gT[0:24, :], start=True, stop=True)
                mm.then_inc(done, 1)
                def rest(i):
                    product(("rest", l, i), KD, lambda k: xn[:, k, :])

                rest(0)
                for i in range(7):
                    pe.wait_ge(S["qk_normed"], 7 * l + i + 1)
                    column_sum(("rot", l, i), 1, C("rot"), lambda k: qkv[:, i, :])

                def compress(hf):
                    fills = [(l, hf, "cmp0"), (l, hf, "cmp1")]
                    for f in fills:
                        pe.wait_ge(pg_full[fill_at[f][0]], fill_at[f][1])
                    for kind in range(2):
                        src = [view(pages, page_slot(f) + 2048 * kind, 2, PAST // STRIDE, STRIDE) for f in fills]
                        out = [bank(("cmp", l, hf, kind, k)) for k in range(2)]
                        if hf == 0:
                            if kind == 0:
                                pe.wait_ge(S["qk_ready"], l + 1)
                            ps2, done2 = bank(("cmpp", l, kind))
                            prm = qkv[:, (4, 7)[kind], 0:TP].rearrange("p (c j) -> p c j", j=STRIDE)
                        for j in range(32):
                            wb, release = wblock()
                            a, jj = divmod(j, STRIDE)
                            for k, (ps, done) in enumerate(out):
                                mm = nc.tensor.matmul(ps[:, 0:2 * NCS].rearrange("p (b c) -> p b c", b=2), wb,
                                                      src[k][:, :, a:a + NCS, jj], start=(j == 0), stop=(j == 31))
                                if j == 31:
                                    mm.then_inc(done, 1)
                                elif k == 1 and release is not None:
                                    mm.then_inc(release, 1)
                            if hf == 0:
                                mm = nc.tensor.matmul(ps2[:, 0:NCP], wb, prm[:, a:a + NCP, jj], start=(j == 0), stop=(j == 31))
                        if hf == 0:
                            mm.then_inc(done2, 1)

                for i in range(1, EARLY):
                    rest(i)
                compress(0)
                pe.wait_ge(S["vcT_ready"], 3 * l + 2)
                ps, done = bank(("vcp", l))
                nc.tensor.transpose(ps[0:NCP, 0:P], vcTp[:, 0:NCP], ident).then_inc(done, 1)
                pe.wait_ge(S["vtok_ready"], l + 1)

                def unit_scores(n):
                    g, qt, br = UNITS[n]
                    gd = slice(HD * g, HD * g + HD)
                    q = lambda r: qkv[gd, r, qt * P:qt * P + P]
                    if br == 0:
                        ps, done = bank(("S", l, n, 0))
                        for r in range(GRP):
                            mm = nc.tensor.matmul(ps[:, r * NCP:(r + 1) * NCP], q(r), kcTp[gd, 0:NCP], start=True, stop=True)
                        mm.then_inc(done, 1)
                        return
                    nk = P * (qt + 1)
                    for part in range(qt + 1):
                        ps, done = bank(("S", l, n, part))
                        for i in range(512 // nk):
                            r = part * 2 + i
                            mm = nc.tensor.matmul(ps[:, i * nk:(i + 1) * nk], q(r), qkv[gd, 4 + br, 0:nk], start=True, stop=True)
                        mm.then_inc(done, 1)

                def unit_transposes(n):
                    g, qt, br = UNITS[n]
                    w = NCP if br == 0 else P
                    nkc = 1 if br == 0 else qt + 1
                    s = S_p[n % 2][:, 0:GRP * w * nkc].rearrange("p (r k) -> p r k", r=GRP)
                    pe.wait_ge(S["exp_ready"], 12 * l + n + 1)
                    for kc in range(nkc):
                        ps, done = bank(("T", l, n, kc))
                        for r in range(GRP):
                            mm = nc.tensor.transpose(ps[0:w, r * P:(r + 1) * P], s[:, r, kc * w:(kc + 1) * w], ident)
                        mm.then_inc(done, 1)

                def unit_out(n):
                    g, qt, br = UNITS[n]
                    w = NCP if br == 0 else P
                    nkc = 1 if br == 0 else qt + 1
                    pe.wait_ge(S["pt_ready"], 12 * l + n + 1)
                    ps, done = bank(("O", l, n))
                    for r in range(GRP):
                        for kc in range(nkc):
                            v = vcp[0:w, g * HD:(g + 1) * HD] if br == 0 else vtok[:, kc, br, g * HD:(g + 1) * HD]
                            mm = nc.tensor.matmul(ps[:, r * HD:(r + 1) * HD], PT_p[0:w, kc, r * P:(r + 1) * P], v,
                                                  start=(kc == 0), stop=(kc == nkc - 1))
                    mm.then_inc(done, 1)

                pe.wait_ge(S["vc_ready"], 3 * l + 1)
                for n in range(13):
                    if n == CMP1_UNIT:
                        compress(1)
                    if n < 12:
                        unit_scores(n)
                    if n > 0:
                        unit_transposes(n - 1)
                    if n < 12:
                        if UNIT_REST[n] is not None:
                            rest(UNIT_REST[n])
                    if n > 0:
                        unit_out(n - 1)
                pe.wait_ge(S["otok_ready"], l + 1)
                for qt in range(2):
                    ps, done = bank(("ot", l, qt))
                    for r in range(GRP):
                        mm = nc.tensor.transpose(ps[:, r * P:(r + 1) * P], otok[:, qt, r, :, :], ident)
                    mm.then_inc(done, 1)

                pe.wait_ge(S["qbd_ready"], l + 1)
                for hf in range(2):
                    it = 2 * l + hf
                    kcT, vcT = kvT[hf]
                    pe.wait_ge(S["vcT_ready"], 3 * l + 2 + hf)
                    ps, done = bank(("vct", l, hf))
                    for bi in range(HALF):
                        mm = nc.tensor.transpose(ps[0:NCS, bi * P:(bi + 1) * P], vcT[:, bi, :], ident)
                    mm.then_inc(done, 1)
                    ps, done = bank(("Sc", l, hf))
                    for bi in range(HALF):
                        mm = nc.tensor.matmul(ps[32 * bi:32 * bi + 32, 0:NCS], qbd[:, hf * HALF + bi, :], kcT[:, bi, :],
                                              start=True, stop=True)
                    mm.then_inc(done, 1)
                    rest(12 + 5 * hf)
                    pe.wait_ge(S["pc_ready"], it + 1)
                    ps, done = bank(("imp", l, hf))
                    nc.tensor.matmul(ps[:, 0:NCS], C("group_sum"), S_c[:, 0:NCS], start=True, stop=True).then_inc(done, 1)
                    ps, done = bank(("Tc", l, hf))
                    nc.tensor.transpose(ps[0:NCS, 0:P], S_c[:, 0:NCS], ident).then_inc(done, 1)
                    pe.wait_ge(S["ptc_ready"], it + 1)
                    pe.wait_ge(S["vc_ready"], 3 * l + 2 + hf)
                    ps, done = bank(("Oc", l, hf))
                    for bi in range(HALF):
                        mm = nc.tensor.matmul(ps[32 * bi:32 * bi + 32, 0:P], PT_c[0:NCS, 32 * bi:32 * bi + 32],
                                              vc[0:NCS, bi, :], start=True, stop=True)
                    mm.then_inc(done, 1)
                    for o, br, ncol in ((1, 2, WIN), (2, 1, PAST)):
                        nk = ncol // 512
                        keys = []
                        for bi in range(HALF):
                            if br == 1:
                                f = (l, hf, ("slc0", "slc1")[bi // 2])
                                s = view(pages, page_slot(f), 2, NPG, 2, P)[:, bi % 2]
                                keys.append((f, s[:, :, 0, :], s[:, :, 1, :]))
                            else:
                                f = (l, hf, "win")
                                s = view(pages, page_slot(f), 2, HALF, 4, P)
                                keys.append((f, s[:, 0, bi], s[:, 1, bi]))
                        for c in range(nk):
                            ps, done = bank(("Ss", l, hf, br, c))
                            for bi in range(HALF):
                                f, kT, _ = keys[bi]
                                pe.wait_ge(pg_full[fill_at[f][0]], fill_at[f][1])
                                mm = nc.tensor.matmul(ps[32 * bi:32 * bi + 32, 0:512].rearrange("p (a b) -> p a b", a=4),
                                                      qbd[:, hf * HALF + bi, :], kT[:, 4 * c:4 * c + 4, :], start=True, stop=True)
                            mm.then_inc(done, 1)
                        ps, done = bank(("Sn", l, hf, br))
                        for bi in range(HALF):
                            mm = nc.tensor.matmul(ps[32 * bi:32 * bi + 32, 0:TS], qbd[:, hf * HALF + bi, :],
                                                  qkv[:, 4 + br, TP:T], start=True, stop=True)
                        mm.then_inc(done, 1)
                        rest(12 + 5 * hf + 2 * o - 1)
                        pe.wait_ge(S["ss_exp"], 2 * it + o)
                        for c in range(nk):
                            ps, done = bank(("Ts", l, hf, br, c))
                            for i in range(4):
                                mm = nc.tensor.transpose(ps[:, i * P:(i + 1) * P], S_s[:, 512 * c + i * P:512 * c + (i + 1) * P], ident)
                            mm.then_inc(done, 1)
                        ps, done = bank(("Tn", l, hf, br))
                        nc.tensor.transpose(ps[0:TS, 0:P], S_s[:, ncol:ncol + TS], ident).then_inc(done, 1)
                        rest(12 + 5 * hf + 2 * o)
                        pe.wait_ge(S["pts_ready"], 2 * it + o)
                        ps, done = bank(("Os", l, hf, br))
                        for bi in range(HALF):
                            for c in range(4 * nk):
                                nc.tensor.matmul(ps[32 * bi:32 * bi + 32, 0:P], PT_s[:, c, 32 * bi:32 * bi + 32],
                                                 keys[bi][2][:, c, :], start=(c == 0), stop=False)
                            mm = nc.tensor.matmul(ps[32 * bi:32 * bi + 32, 0:P], PT_s[0:TS, 8, 32 * bi:32 * bi + 32],
                                                  vtok[0:TS, 2, br, :], start=False, stop=True)
                        mm.then_inc(done, 1)
                    pe.wait_ge(S["orow_ready"], it + 1)
                    ps, done = bank(("oT", l, hf))
                    for br in range(3):
                        mm = nc.tensor.transpose(ps[:, br * P:(br + 1) * P], orow[:, br, :], ident)
                    mm.then_inc(done, 1)

                o_br = (oN, oS, oC)

                def merge_gates(q):
                    for u in GROUPS[q]:
                        product(("gate", l, u), KD, lambda k: xn[:, k, :])

                def merge_group(q):
                    merge_gates(q)
                    for u in GROUPS[q]:
                        product(("proj", l, u), 4, lambda k: o_br[MERGE[u][0]][:, k, :])

                merge_gates(0)
                pe.wait_ge(S["attn_done"], l + 1)
                for u in GROUPS[0]:
                    product(("proj", l, u), 4, lambda k: oN[:, k, :])
                merge_group(1)
                merge_group(2)
                for c in range(NCHUNK):
                    t0, n = TILES[c]
                    cc = NCHUNK * l + c
                    up = C("upto0") if c < 2 else C("upto2", TS)
                    all_ = C("ones") if c < 2 else C("same2", TS)
                    pe.wait_ge(S["dD_ready"], cc + 1)
                    ps, done = bank(("ac", cc))
                    nc.tensor.matmul(ps[0:n, 0:NH], up, dta[0:n, c, :], start=True, stop=True)
                    nc.tensor.matmul(ps[0:n, NH:2 * NH], all_[:, 0:n], dta[0:n, c, :], start=True, stop=True).then_inc(done, 1)
                    for part in range(2 if c < 2 else 1):
                        ps, done = bank(("acB", cc, part))
                        w = min(512, NH * n)
                        nc.tensor.matmul(ps[:, 0:w], C("ones", n), decay[0:n, part * 512:part * 512 + w],
                                         start=True, stop=True).then_inc(done, 1)
                    pe.wait_ge(S["xbcc_ready"], l + 1)
                    ps, done = bank(("xtok", cc))
                    for j in range(4):
                        mm = nc.tensor.transpose(ps[0:n, j * P:(j + 1) * P], xbcc[:, j, t0:t0 + n], ident)
                    mm.then_inc(done, 1)
                    ps, done = bank(("btok", cc))
                    nc.tensor.transpose(ps[0:n, 0:P], xbcc[:, 4, t0:t0 + n], ident).then_inc(done, 1)
                    for g in range(NKV):
                        ps, done = bank(("CB", cc, g))
                        gd = slice(HD * g, HD * g + HD)
                        nc.tensor.matmul(ps[0:n, 0:n], xbcc[gd, 4, t0:t0 + n], xbcc[gd, 5, t0:t0 + n],
                                         start=True, stop=True).then_inc(done, 1)
                    merge_group((3, 5, 7)[c])
                    pe.wait_ge(S["dec_ready"], cc + 1)
                    pe.wait_ge(S["xdt_ready"], cc + 1)
                    if c > 0:
                        pe.wait_ge(S["cp_ready"], 2 * l + c)
                    for hh in range(NH):
                        j, h2 = divmod(hh % GRP, 2)
                        g, hg = divmod(hh, GRP)
                        if hg == 0:
                            ps, done = bank(("y", cc, g))
                        gd = slice(HD * g, HD * g + HD)
                        o = ps[HD * h2:HD * h2 + HD, j * n:(j + 1) * n]
                        mm = nc.tensor.matmul(o, xdt[0:n, hh * HD:(hh + 1) * HD], decay[0:n, hh * n:(hh + 1) * n],
                                              start=True, stop=(c == 0))
                        if c == 1:
                            mm = nc.tensor.matmul(o, hT[gd, hg, :], cp[gd, hg * n:(hg + 1) * n], start=False, stop=True)
                        if c == 2:
                            for b in range(NB):
                                mm = nc.tensor.matmul(o[:, b * TD:(b + 1) * TD], hs[gd, b, hg, :],
                                                      cp[gd, hg * n + b * TD:hg * n + (b + 1) * TD], start=False, stop=(b == NB - 1))
                        if hg == GRP - 1:
                            mm.then_inc(done, 1)
                    pe.wait_ge(S["btok_ready"], cc + 1)
                    if c < 2:
                        ps, done = bank(("hd", cc))
                        for g in range(NKV):
                            mm = nc.tensor.matmul(ps[HD * g:HD * g + HD, 0:256], btok[0:n, g * HD:(g + 1) * HD],
                                                  xtl[0:n, g * 256:(g + 1) * 256], start=True, stop=True)
                        mm.then_inc(done, 1)
                        if c == 0:
                            pe.wait_ge(S["oC_ready"], l + 1)
                        merge_group((4, 6)[c])
                        if c == 0:
                            pe.wait_ge(S["h_ready"], 2 * l + 1)
                    else:
                        pe.wait_ge(S["bm_ready"], l + 1)
                        for b2 in range(NB // 2):
                            ps, done = bank(("hsd", l, b2))
                            for i in range(2):
                                for g in range(NKV):
                                    mm = nc.tensor.matmul(ps[HD * g:HD * g + HD, 256 * i:256 * i + 256],
                                                          bm[0:n, 2 * b2 + i, g * HD:(g + 1) * HD],
                                                          xtl[0:n, g * 256:(g + 1) * 256], start=True, stop=True)
                            mm.then_inc(done, 1)
                merge_gates(8)
                pe.wait_ge(S["ysq_ready"], l + 1)
                column_sum(("yss", l), 4, C("ones"), lambda k: tmp[:, k, :])
                pe.wait_ge(S["oS_ready"], l + 1)
                for u in GROUPS[8]:
                    product(("proj", l, u), 4, lambda k: oS[:, k, :])

                merge_gates(9)
                for u in GROUPS[9]:
                    product(("proj", l, u), 4, lambda k: oS[:, k, :])
                pe.wait_ge(S["merged_ready"], l + 1)
                for m in range(KD):
                    product(("o", l, m), KD, lambda k: merged[:, k, :])
                rms_sum(l, 1)
                if l == 0:
                    for f in range(NFD):
                        product(("fg", f), KD, normed_tile if f == 0 else lambda k: xn[:, k, :])
                        product(("fu", f), KD, lambda k: xn[:, k, :])
                    pe.wait_ge(*released(("fu", NFD - 1)))
                    for m in range(KD):
                        product(("fd", m), NFD, lambda k: h[:, k, :])
            pe.wait_ge(S["xn_ready"], KD * 2 * DEPTH)
            ps, done = bank(("router",))
            for tt, (t0, n) in enumerate(TILES):
                for k in range(KD):
                    mm = nc.tensor.matmul(ps[0:n, NE * tt:NE * tt + NE], xn[:, k, t0:t0 + n],
                                          PR(1, "router", NE * k, NE), start=(k == 0), stop=(k == KD - 1))
            mm.then_inc(done, 1)
            for tt, (t0, n) in enumerate(TILES):
                for hf in range(2):
                    ps, done = bank(("xtk", tt, hf))
                    for k in range(4):
                        mm = nc.tensor.transpose(ps[0:n, k * P:(k + 1) * P], xn[:, 4 * hf + k, t0:t0 + n], ident)
                    mm.then_inc(done, 1)
            pe.wait_ge(S["cnt_ready"], 1)
            ps, done = bank(("cnt",))
            for tt, (t0, n) in enumerate(TILES):
                nc.tensor.matmul(ps[:, 0:NE], C("ones", n), mask[0:n, tt, :], start=(tt == 0), stop=(tt == 2))
            for tt, (t0, n) in enumerate(TILES):
                o = ps[0:n, NE * (tt + 1):NE * (tt + 2)]
                for t2 in range(tt):
                    nc.tensor.matmul(o, C("ones")[:, 0:n], mask[:, t2, :], start=(t2 == 0), stop=False)
                mm = nc.tensor.matmul(o, C("before", n)[:, 0:n], mask[0:n, tt, :], start=(tt == 0), stop=True)
            mm.then_inc(done, 1)
            at = [0]
            inloop = [None]

            def pbank(key):
                u = base + at[0]
                at[0] += 1
                use_of[key] = u
                pe.wait_ge(bank_free[u % 8], inloop[0] * (MOE_USES // 8) + u // 8)
                return psum[u % 8], bank_full[u % 8]

            def gather(bank_, key):
                for hf in range(2):
                    ps, done = bank_((key, hf))
                    for k in range(4):
                        for tt, (t0, n) in enumerate(TILES):
                            c0 = (4 * hf + k) * P
                            mm = nc.tensor.matmul(ps[:, k * CAP:(k + 1) * CAP], xtok[0:n, tt, c0:c0 + P], pick[0:n, tt, :],
                                                  start=(tt == 0), stop=(tt == 2))
                    mm.then_inc(done, 1)

            def to_slots(key):
                for hf in range(2):
                    ps, done = pbank((key, hf))
                    for k in range(4):
                        mm = nc.tensor.transpose(ps[0:CAP, k * P:(k + 1) * P], yT[:, 4 * hf + k, :], ident)
                    mm.then_inc(done, 1)

            def scatter(key):
                for m in range(KD):
                    ps, done = pbank((key, m))
                    nc.tensor.matmul(ps[:, 0:T], yS[0:CAP, m, :], spread[0:CAP, :], start=True, stop=True).then_inc(done, 1)

            pe.wait_ge(S["pick_ready"], 1)
            pe.wait_ge(*released(("xtk", 2, 1)))
            gather(bank, "xe0")
            pe.wait_ge(S["table_ready"], 1)
            n_pass = pe.value_load(passes[0:1, 32:33], min_val=NE, max_val=MAX_PASSES)
            pe.wait_ge(*released(("xe0", 1)))
            base = uses[0]
            assert blk[0] == PRE_SLOTS * BPS
            with pe.Fori(0, n_pass) as i:
                inloop[0] = i
                nb = [0]

                def wmul(out, rhs, start, stop):
                    s, o = divmod(nb[0], BPS)
                    nb[0] += 1
                    s += PRE_SLOTS
                    if o == 0:
                        pe.wait_ge(w_full[s % RING], i * (16 * EXP_SLOTS // RING) + 16 * (s // RING + 1))
                    a = (s % RING) * SLOTF + o * P
                    mm = nc.tensor.matmul(out, wring[:, a:a + P], rhs, start=start, stop=stop)
                    if o == 0:
                        mm.then_inc(w_free[(s - 1) % RING], 1)
                    return mm

                def gate_up(q):
                    ps, done = pbank(("gu", q))
                    for f in range(2):
                        for part in range(2):
                            c0 = (2 * part + f) * CAP
                            for k in range(KD):
                                mm = wmul(ps[:, c0:c0 + CAP], xe[:, k, :], k == 0, k == KD - 1)
                    mm.then_inc(done, 1)

                use_of[("dn", 2)] = base + MOE_USES - 1
                use_of[("xe", 1)] = base + MOE_USES - 4
                use_of[("sp", 2)] = base + 16
                pe.wait_ge(*released(("xe", 1), i, 1))
                gate_up(0)
                gate_up(1)
                pe.wait_ge(*released(("dn", 2), i, 1))
                to_slots("yt")
                gate_up(2)
                gate_up(3)
                pe.wait_ge(*released(("yt", 1), i))
                pe.wait_ge(*released(("sp", 2), i, 1))
                scatter("sc")
                for tt, (t0, n) in enumerate(TILES):
                    ps, done = pbank(("sp", tt))
                    nc.tensor.transpose(ps[0:CAP, 0:P], pickw[:, tt, :], ident).then_inc(done, 1)
                for q in range(4, NFE // 2):
                    gate_up(q)
                pe.wait_ge(S["pick_ready"], i + 2)
                gather(pbank, "xe")
                pe.wait_ge(*released(("gu", NFE // 2 - 1), i))
                for d, (m0, nm) in enumerate(DOWN):
                    ps, done = pbank(("dn", d))
                    for m in range(nm):
                        for k in range(NFE):
                            mm = wmul(ps[:, m * CAP:(m + 1) * CAP], he[:, k, :], k == 0, k == NFE - 1)
                    mm.then_inc(done, 1)
                assert at[0] == MOE_USES and nb[0] == EXP_BLOCKS
                assert (use_of[("dn", 2)], use_of[("xe", 1)], use_of[("sp", 2)]) == (base + 31, base + 28, base + 16)
            inloop[0] = n_pass - 1
            pe.wait_ge(*released(("dn", 2), n_pass - 1))
            to_slots("yt_last")
            pe.wait_ge(*released(("yt_last", 1), n_pass - 1))
            pe.wait_ge(*released(("sp", 2), n_pass - 1))
            scatter("sc_last")

        @block.sync
        def _(sp):
            sp.dma_start(xT_[:, :], xT_in).then_inc(S["x_in"], 16)
            sp.dma_start(cst[:, 0:FIRST_CONST], consts[:, 0:FIRST_CONST]).then_inc(S["const_in"], 16)
            sp.dma_start(par[:, :], params).then_inc(S["const_in"], 16)

            def load(pos, index):
                sp.dma_start(wring[:, pos * SLOTF:(pos + 1) * SLOTF],
                             wstream[index, :, :].rearrange("a p n -> (a p) n")).then_inc(w_full[pos], 16)

            for s in range(RING):
                load(s, bass.ds(s, 1))
                if s == 1:
                    sp.dma_start(cst[:, FIRST_CONST:], consts[:, FIRST_CONST:]).then_inc(S["tables_in"], 16)
            known = PRE_SLOTS + RING

            def weights(a, b):
                rounds = (b - a) // RING
                if rounds > 1:
                    with sp.Fori(0, rounds) as i:
                        for j in range(RING):
                            pos = (a + j) % RING
                            sp.wait_ge(w_free[pos], i + (a + j) // RING)
                            load(pos, bass.ds(i * RING + (a + j), 1))
                    a += rounds * RING
                for s in range(a, b):
                    sp.wait_ge(w_free[s % RING], s // RING)
                    load(s % RING, bass.ds(s, 1))

            weights(RING, known)
            sp.wait_ge(S["table_ready"], 1)
            n_pass = sp.value_load(passes[0:1, 32:33], min_val=NE, max_val=MAX_PASSES)

            def pass_slots(i, ex, first, last):
                for s in range(first, last):
                    pos = (PRE_SLOTS + s) % RING
                    sp.wait_ge(w_free[pos], i * (EXP_SLOTS // RING) + (PRE_SLOTS + s) // RING)
                    load(pos, bass.ds(ex * EXP_SLOTS + (PRE_SLOTS + s), 1))

            with sp.Fori(0, n_pass - 1) as i:
                ex = sp.value_load(passes[0:1, bass.ds(i, 1)], min_val=0, max_val=NE - 1)
                pass_slots(i, ex, RING, EXP_SLOTS)
                ex2 = sp.value_load(passes[0:1, bass.ds(i + 1, 1)], min_val=0, max_val=NE - 1)
                pass_slots(i + 1, ex2, 0, RING)
            ex = sp.value_load(passes[0:1, bass.ds(n_pass - 1, 1)], min_val=0, max_val=NE - 1)
            pass_slots(n_pass - 1, ex, RING, EXP_SLOTS)
            sp.wait_ge(S["x_ready"], 1)
            sp.dma_start(y_out, xT_[:, :]).then_inc(S["y_done"], 16)
            sp.wait_ge(S["y_done"], 16)

        @block.gpsimd
        def _(pool):
            pool.dma_start(ptab[0:1, :], page_table).then_inc(S["ptab_in"], 16)
            pool.wait_ge(S["ptab_in"], 16)
            n_pool = cmp_pages.shape[0] // DEPTH

            def fill(f):
                l, hf, what = f
                idx = FILLS.index(f)
                pos = idx % 3
                at = page_slot(f)
                if idx >= 3:
                    pl, phf, pw = FILLS[idx - 3]
                    last = {"cmp0": ("cmp", pl, phf, 1, 0), "cmp1": ("cmp", pl, phf, 1, 1),
                            "slc0": ("Os", pl, phf, 1), "slc1": ("Os", pl, phf, 1), "win": ("Os", pl, phf, 2)}[pw]
                    pool.wait_ge(*filled(last))
                if what == "win":
                    pool.dma_start(view(pages, at, HALF, WIN),
                                 win_kT[l, :, hf * HALF:(hf + 1) * HALF, :]).then_inc(pg_full[pos], 16)
                    for bi in range(HALF):
                        pool.dma_start(view(pages, at + 2048 + bi * 512, 4, P),
                                     win_v[l, hf * HALF + bi]).then_inc(pg_full[pos], 16)
                    return
                first = (hf * HALF + 2 * int(what[3])) * NPG
                with pool.Fori(0, 2 * NPG) as i:
                    page = pool.value_load(ptab[0:1, bass.ds(i + first, 1)], min_val=0, max_val=n_pool - 1)
                    if what[:3] == "cmp":
                        pool.dma_start(view(pages, at, 2, 2048)[:, :, bass.ds(i * P, P)],
                                       cmp_pages[bass.ds(page + l * n_pool, 1), :, :, :].rearrange("a p k n -> (a p) k n")).then_inc(pg_full[pos], 16)
                    else:
                        pool.dma_start(pages[:, bass.ds(i * 2 * P + at, 2 * P)],
                                       slc_pages[bass.ds(page + l * n_pool, 1), :, :].rearrange("a p n -> (a p) n")).then_inc(pg_full[pos], 16)

            pool.wait_ge(w_full[2], 16)
            for f in FILLS[0:3]:
                fill(f)
            for l in range(DEPTH):
                pool.dma_start(sc_st, sc_in[l]).then_inc(S["st_in"], 16)
                pool.dma_start(cv_st, conv_in[l]).then_inc(S["st_in"], 16)
                pool.dma_start(win_out[l], win_rows[l, :, TD:, :]).then_inc(S["win_done"], 16)
                pool.wait_ge(S["qk_ready"], l + 1)
                pool.dma_start(kv_out[l], qkv[:, 4:10, :]).then_inc(S["kv_done"], 16)
                for f in FILLS[3:10] if l == 0 else FILLS[13:20]:
                    fill(f)
                pool.wait_ge(S["cols_ready"], l + 1)
                for t in range(6):
                    pool.dma_start(conv_out[l, :, t, 0:3], xbcp[:, t, TP:TP + 3]).then_inc(S["cc_done"], 16)
                    pool.dma_start(conv_out[l, :, t, 3:27].rearrange("p (b k) -> p b k", b=NB),
                                   xbcp[:, t, 3 + TP:].rearrange("p (b k) -> p b k", b=NB)[:, :, TD:TD + 3]).then_inc(S["cc_done"], 16)
                for t in range(4):
                    pool.dma_start(sc_out[l, :, t, 0:2], chp[:, t, TP:TP + 2]).then_inc(S["cc_done"], 16)
                    pool.dma_start(sc_out[l, :, t, 2:18].rearrange("p (b k) -> p b k", b=NB),
                                   chp[:, t, 2 + TP:].rearrange("p (b k) -> p b k", b=NB)[:, :, TD:TD + 2]).then_inc(S["cc_done"], 16)
                pool.wait_ge(S["cc_done"], 320 * (l + 1))
                pool.wait_ge(S["oC_ready"], l + 1)
                pool.wait_ge(*released(("proj", l, 3)))
                pool.dma_start(hs, ssm_in[l]).then_inc(S["hs_in"], 16)
                if l == 0:
                    for f in FILLS[10:13]:
                        fill(f)
                pool.wait_ge(S["h_ready"], 2 * l + 2)
                pool.dma_start(ssm_p_out[l], hT).then_inc(S["hp_done"], 16)
                pool.wait_ge(S["y_ready"], l + 1)
                pool.dma_start(ssm_s_out[l], hs).then_inc(S["hs_done"], 16)
                pool.wait_ge(S["hp_done"], 16 * (l + 1))
                pool.wait_ge(S["hs_done"], 16 * (l + 1))
            pool.wait_ge(S["win_done"], 32)

        @block.scalar
        def _(act):
            chain, marks = [0], [0]

            def link(ins):
                chain[0] += 1
                ins.then_inc(S["act_chain"], 1)
                act.wait_ge(S["act_chain"], chain[0])

            def copy(out, in_):
                return A.activation(out, in_, ACT.Copy)

            def evac(key, out, cols, rows=P, name=None):
                act.wait_ge(*filled(key))
                ps = bank_of(key)
                src = ps[0:rows, 0:cols]
                if len(out.shape) == 3:
                    src = src.rearrange("p (a b) -> p a b", b=out.shape[2])
                copy(out, src).then_inc(free(key), 1)

            def signal(name):
                marks[0] += 1
                k = marks[0] % MARKS
                A.activation(mark[0:1, k:k + 1], eps[0:1, :], ACT.Copy).then_inc(S[name], 1)

            eps = C("eps")
            act.wait_ge(S["const_in"], 32)
            act.wait_ge(S["x_in"], 16)
            act.wait_ge(S["zeroed"], 1)

            def rms(l, which):
                for k in range(KD):
                    if which:
                        act.wait_ge(*released(("o", l, k)))
                    elif l:
                        act.wait_ge(*released(("fd", k)))
                    A.activation(tmp[:, k, :], xT[:, k, :], ACT.Square).then_inc(S["sq_ready"], 1)
                act.wait_ge(*filled(("ss", l, which)))
                ps = bank_of(("ss", l, which))
                A.activation(std[:, :], ps[:, 0:T], ACT.Sqrt, bias=eps, scale=1.0 / D).then_inc(free(("ss", l, which)), 1)

            for l in range(DEPTH):
                rms(l, 0)
                act.wait_ge(*filled(("small", l)))
                ps = bank_of(("small", l))
                if l:
                    act.wait_ge(S["kv_done"], 16 * l)
                copy(small[0:TS, 2, :], ps[0:TS, 64:96]).then_inc(S["small_ready"], 1)
                copy(small[:, 0:2, :], ps[:, 0:64].rearrange("p (a b) -> p a b", a=2)).then_inc(free(("small", l)), 1)
                act.wait_ge(*released(("small", l)))
                A.activation(gates[0:TS, 2, :], small[0:TS, 2, 0:24], ACT.Sigmoid)
                A.activation(gates[:, 0:2, :], small[:, 0:2, 0:24], ACT.Sigmoid).then_inc(S["gates_ready"], 1)
                for i in range(NQKV):
                    evac(("in", l, i), qkv[:, i, :], T)
                    if 1 <= i <= 7:
                        act.wait_ge(*released(("in", l, i - 1)))
                        A.activation(tmp[:, i - 1, :], qkv[:, i - 1, :], ACT.Square).then_inc(S["qksq_ready"], 1)
                signal("qkv_ready")
                for i in range(7):
                    act.wait_ge(*filled(("qkss", l, i)))
                    ps = bank_of(("qkss", l, i))
                    A.activation(rq[:, i, :], ps[:, 0:T], ACT.Sqrt, bias=eps, scale=1.0 / HD).then_inc(free(("qkss", l, i)), 1)
                for tt, (t0, n) in enumerate(TILES):
                    evac(("vt", l, tt), vtok[0:n, tt, :, :], 3 * P, n)
                signal("vtok_ready")
                act.wait_ge(*filled(("gT", l)))
                ps = bank_of(("gT", l))
                copy(gT[0:24, :], ps[0:24, 0:TS]).then_inc(free(("gT", l)), 1)
                signal("gT_ready")
                act.wait_ge(*filled(("gB", l)))
                ps = bank_of(("gB", l))
                copy(gB.rearrange("p a b c -> p (a b c)"), ps[:, 0:384]).then_inc(free(("gB", l)), 1)
                def rest(i):
                    kind, j = REST[i]
                    if kind == "h":
                        return
                    key = ("rest", l, i)
                    act.wait_ge(*filled(key))
                    ps = bank_of(key)
                    if kind == "x":
                        copy(xbcp[:, j, 3:3 + TP], ps[:, 0:TP])
                        copy(xbcp[:, j, 3 + TP:].rearrange("p (b k) -> p b k", b=NB)[:, :, 3:],
                             ps[:, TP:T].rearrange("p (b k) -> p b k", b=NB)).then_inc(free(key), 1)
                    elif kind == "z":
                        A.activation(oS[:, j, :], ps[:, 0:T], ACT.Silu).then_inc(free(key), 1)
                    elif kind == "c":
                        if j >= 2:
                            act.wait_ge(*released(("rest", l, REST.index(("h", j - 2)))))
                        copy(scc[:, j % 2, :], ps[:, 0:T]).then_inc(free(key), 1)
                    else:
                        copy(oC[:, j, :], ps[:, 0:T]).then_inc(free(key), 1)

                for i in range(EARLY):
                    rest(i)
                for kind, (o, op) in enumerate(((kvT[0][0], kcTp), (kvT[0][1], vcTp))):
                    for k in range(2):
                        evac(("cmp", l, 0, kind, k), o[:, 2 * k:2 * k + 2, :], 2 * NCS)
                    evac(("cmpp", l, kind), op[:, 0:NCP], NCP)
                    signal("vcT_ready")
                evac(("vcp", l), vcp[0:NCP, :], P, NCP)
                signal("vc_ready")
                rest(UNIT_REST[0])
                for n, (g, qt, br) in enumerate(UNITS):
                    w = NCP if br == 0 else P * (qt + 1)
                    s = S_p[n % 2][:, 0:GRP * w].rearrange("p (r k) -> p r k", r=GRP)
                    act.wait_ge(S["smax"], 12 * l + n + 1)
                    for r in range(GRP):
                        e = A.activation(s[:, r, :], s[:, r, :], ACT.Exp, bias=mx[:, n % 2, r:r + 1],
                                         accum_out=ssum[:, n % 2, r:r + 1])
                    e.then_inc(S["exp_ready"], 1)
                    if n == CMP1_UNIT - 1:
                        for kind, k in ((0, 0), (0, 1), (1, 0), (1, 1)):
                            evac(("cmp", l, 1, kind, k), kvT[1][kind][:, 2 * k:2 * k + 2, :], 2 * NCS)
                        signal("vcT_ready")
                    rows = min(w, P)
                    for kc in range(1 if br == 0 else qt + 1):
                        evac(("T", l, n, kc), PT_p[0:rows, kc, :], 512, rows)
                    signal("pt_ready")
                    if n < 11 and UNIT_REST[n + 1] is not None:
                        rest(UNIT_REST[n + 1])
                for qt in range(2):
                    evac(("ot", l, qt), oN[:, :, qt * P:(qt + 1) * P], 512)
                for hf in range(2):
                    it = 2 * l + hf
                    if hf == 1:
                        act.wait_ge(S["orow_ready"], it)
                    evac(("vct", l, hf), vc[0:NCS, :, :], 512, NCS)
                    signal("vc_ready")
                    act.wait_ge(S["scmax"], it + 1)
                    A.activation(S_c[:, 0:NCS], S_c[:, 0:NCS], ACT.Exp, bias=smx[:, 0:1], accum_out=ssm[:, 0:1]).then_inc(S["sc_exp"], 1)
                    rest(12 + 5 * hf)
                    evac(("Tc", l, hf), PT_c[0:NCS, :], P, NCS)
                    signal("ptc_ready")
                    for o, br, ncol in ((1, 2, WIN), (2, 1, PAST)):
                        act.wait_ge(S["ssmax"], 2 * it + o)
                        A.activation(S_s[:, 0:ncol + TS], S_s[:, 0:ncol + TS], ACT.Exp, bias=smx[:, br:br + 1],
                                     accum_out=ssm[:, br:br + 1]).then_inc(S["ss_exp"], 1)
                        rest(12 + 5 * hf + 2 * o - 1)
                        for c in range(ncol // 512):
                            evac(("Ts", l, hf, br, c), PT_s[:, 4 * c:4 * c + 4, :], 512)
                        evac(("Tn", l, hf, br), PT_s[0:TS, 8, :], P, TS)
                        signal("pts_ready")
                        rest(12 + 5 * hf + 2 * o)
                act.wait_ge(S["attn_done"], l + 1)
                act.wait_ge(S["kv_done"], 16 * (l + 1))
                A.activation(ea, PR(l, "a_log", 0, NH), ACT.Exp).then_inc(S["ea_ready"], 1)
                act.wait_ge(S["spa"], l + 1)
                A.activation(sp_e, sp_e, ACT.Exp, scale=-1.0).then_inc(S["sp_exp"], 1)
                def sigmoid(q):
                    for u in GROUPS[q]:
                        key = ("gate", l, u)
                        act.wait_ge(*filled(key))
                        v = u - 4
                        if 4 <= v < KD:
                            act.wait_ge(*released(("proj", l, v)))
                        elif v >= KD:
                            act.wait_ge(S["part_sum"], 2 * KD * l + v - KD + 1)
                        A.activation(gate_buffer(u), bank_of(key)[:, 0:T], ACT.Sigmoid).then_inc(free(key), 1)

                sigmoid(0)
                sigmoid(1)
                act.wait_ge(S["xbcc_raw"], l + 1)
                A.activation(xbcc, xbcc, ACT.Silu).then_inc(S["xbcc_ready"], 1)
                act.wait_ge(S["cc_done"], 320 * (l + 1))
                sigmoid(2)
                for c in range(NCHUNK):
                    n = TILES[c][1]
                    cc = NCHUNK * l + c
                    w = NH * n
                    if c > 0:
                        sigmoid(2 * c + 2)
                    act.wait_ge(S["tl_sub"], cc + 1)
                    A.activation(tail[0:n, :], tail[0:n, :], ACT.Exp).then_inc(S["tl_ready"], 1)
                    act.wait_ge(S["seg_ready"], cc + 1)
                    A.activation(eB[:, 0:w], eB[:, 0:w], ACT.Exp).then_inc(S["eb_ready"], 1)
                    A.activation(decay[0:n, 0:w], decay[0:n, 0:w], ACT.Exp).then_inc(S["dec_exp"], 1)
                    evac(("btok", cc), btok[0:n, :], P, n)
                    signal("btok_ready")
                    sigmoid(2 * c + 3)
                act.wait_ge(S["y_ready"], l + 1)
                A.activation(tmp[:, 0:4, :], oS, ACT.Square).then_inc(S["ysq_ready"], 1)
                act.wait_ge(*filled(("yss", l)))
                ps = bank_of(("yss", l))
                A.activation(std[:, :], ps[:, 0:T], ACT.Sqrt, bias=eps, scale=1.0 / SSMI).then_inc(free(("yss", l)), 1)
                sigmoid(8)
                sigmoid(9)
                act.wait_ge(S["hs_done"], 16 * (l + 1))
                act.wait_ge(S["hp_done"], 16 * (l + 1))
                rms(l, 1)
                if l == 0:
                    for f in range(NFD):
                        act.wait_ge(*filled(("fg", f)))
                        ps = bank_of(("fg", f))
                        if f >= 2:
                            act.wait_ge(*released(("fu", f - 2)))
                        A.activation(gs_[:, f % 2, :], ps[:, 0:T], ACT.Silu).then_inc(free(("fg", f)), 1)
            act.wait_ge(S["re_sub"], 1)
            A.activation(re, re, ACT.Exp).then_inc(S["re_exp"], 1)
            for tt, (t0, n) in enumerate(TILES):
                for hf in range(2):
                    evac(("xtk", tt, hf), xtok[0:n, tt, 512 * hf:512 * hf + 512], 512, n)

            def take(key, out, rows, cols, it):
                act.wait_ge(*filled(key, it))
                ps = bank_of(key)
                src = ps[0:rows, 0:cols]
                if len(out.shape) == 3:
                    src = src.rearrange("p (a b) -> p a b", b=out.shape[2])
                copy(out, src).then_inc(free(key), 1)

            def take_slots(key, it):
                for hf in range(2):
                    take((key, hf), yS[0:CAP, 4 * hf:4 * hf + 4, :], CAP, 512, it)

            def take_gather(key, it):
                for hf in range(2):
                    take((key, hf), xe[:, 4 * hf:4 * hf + 4, :], P, 4 * CAP, it)

            act.wait_ge(S["zero_ready"], 1)
            take_gather("xe0", None)
            act.wait_ge(S["table_ready"], 1)
            n_pass = act.value_load(passes[0:1, 32:33], min_val=NE, max_val=MAX_PASSES)
            with act.Fori(0, n_pass) as i:
                def silu(q):
                    act.wait_ge(*filled(("gu", q), i))
                    ps = bank_of(("gu", q))
                    act.wait_ge(*released(("gu", q - 2 if q >= 2 else NFE // 2 - 2 + q), i, 0 if q >= 2 else 1))
                    A.activation(sg[:, q % 2, :], ps[:, 0:2 * CAP], ACT.Silu).then_inc(S["silu_ready"], 1)

                silu(0)
                silu(1)
                take_slots("yt", i)
                silu(2)
                silu(3)
                for tt, (t0, n) in enumerate(TILES):
                    take(("sp", tt), spread[0:CAP, t0:t0 + n], CAP, n, i)
                for q in range(4, NFE // 2):
                    silu(q)
                take_gather("xe", i)
                for d, (m0, nm) in enumerate(DOWN):
                    take(("dn", d), yT[:, m0:m0 + nm, :], P, nm * CAP, i)
            take_slots("yt_last", n_pass - 1)

        @block.vector
        def _(dve):
            chain, marks = [0], [0]

            def link(ins):
                chain[0] += 1
                ins.then_inc(S["dve_chain"], 1)
                dve.wait_ge(S["dve_chain"], chain[0])

            def signal(name):
                marks[0] += 1
                k = MARKS + marks[0] % MARKS
                V.memset(mark[0:1, k:k + 1], 0.0).then_inc(S[name], 1)

            V.memset(std[:, :], 0.0)
            V.memset(gates, 0.0)
            V.memset(small, 0.0).then_inc(S["zeroed"], 1)
            dve.wait_ge(S["const_in"], 32)
            dve.wait_ge(S["x_in"], 16)

            def rms(l, which, w):
                dve.wait_ge(*released(("ss", l, which)))
                link(V.reciprocal(std[:, :], std[:, :]))
                for k in range(KD):
                    V.scalar_tensor_tensor(xn[:, k, :], xT[:, k, :], PR(l, w, k), std[:, :], ALU.mult, ALU.mult)\
                        .then_inc(S["xn_ready"], 1)
                dve.wait_ge(S["xn_ready"], KD * (2 * l + which + 1))

            for l in range(DEPTH):
                rms(l, 0, "norm_mix")
                if l == 0:
                    dve.wait_ge(S["tables_in"], 16)
                for i in range(7):
                    dve.wait_ge(*released(("qkss", l, i)))
                    link(V.reciprocal(rq[:, i, :], rq[:, i, :]))
                    V.scalar_tensor_tensor(qkv[:, i, :], qkv[:, i, :], PR(l, "qk_norm", i), rq[:, i, :], ALU.mult, ALU.mult)\
                        .then_inc(S["qk_normed"], 1)
                for i in range(7):
                    dve.wait_ge(*filled(("rot", l, i)))
                    ps = bank_of(("rot", l, i))
                    V.tensor_tensor(rq[:, i, :], ps[:, 0:T], C("sin"), ALU.mult).then_inc(free(("rot", l, i)), 1)
                    link(V.tensor_tensor(qkv[:, i, :], qkv[:, i, :], C("cos"), ALU.mult))
                    last = V.tensor_tensor(qkv[:, i, :], qkv[:, i, :], rq[:, i, :], ALU.add)
                last.then_inc(S["qk_ready"], 1)
                dve.wait_ge(S["qk_ready"], l + 1)

                def unit_softmax(n):
                    g, qt, br = UNITS[n]
                    w = NCP if br == 0 else P * (qt + 1)
                    s = S_p[n % 2][:, 0:GRP * w].rearrange("p (r k) -> p r k", r=GRP)
                    if br == 0:
                        mask = C("cmp_mask")[:, qt * NCP:(qt + 1) * NCP]
                    else:
                        mask = C(("causal0", "causal1")[qt])
                    parts = 2 if (br and qt) else 1
                    nr = GRP // parts
                    for part in range(parts):
                        dve.wait_ge(*filled(("S", l, n, part)))
                        ps = bank_of(("S", l, n, part))
                        V.scalar_tensor_tensor(s[:, part * nr:(part + 1) * nr, :],
                                               ps[:, 0:nr * w].rearrange("p (r k) -> p r k", r=nr), HD ** -0.5,
                                               bc(mask, 1, nr), ALU.mult, ALU.add).then_inc(free(("S", l, n, part)), 1)
                    dve.wait_ge(*released(("S", l, n, parts - 1)))
                    V.tensor_reduce(mx[:, n % 2, :], s, AX.X, ALU.max, negate=True).then_inc(S["smax"], 1)

                def unit_out(n):
                    g, qt, br = UNITS[n]
                    dve.wait_ge(S["exp_ready"], 12 * l + n + 1)
                    dve.wait_ge(S["gates_ready"], l + 1)
                    link(V.reciprocal(rsum, ssum[:, n % 2, :]))
                    gate = gates[:, qt, g * 12:(g + 1) * 12].rearrange("p (r k) -> p r k", k=3)[:, :, br]
                    link(V.tensor_tensor(coef, rsum, gate, ALU.mult))
                    if br == 0:
                        link(V.tensor_scalar(coef, coef, C("cmp_any")[:, qt:qt + 1], None, ALU.mult))
                    dve.wait_ge(*filled(("O", l, n)))
                    ps = bank_of(("O", l, n))
                    src = ps[:, 0:256].rearrange("p (r d) -> p r d", r=GRP)
                    dst = otok[:, qt, :, g, :]
                    out = dst if br == 0 else otmp
                    V.tensor_tensor(out, src, bc(coef, 2, HD), ALU.mult).then_inc(free(("O", l, n)), 1)
                    if br:
                        dve.wait_ge(*released(("O", l, n)))
                        link(V.tensor_tensor(dst, dst, otmp, ALU.add))

                def rest(i):
                    kind, j = REST[i]
                    if kind != "h":
                        return
                    key = ("rest", l, i)
                    dve.wait_ge(*released(("rest", l, i - 1)))
                    dve.wait_ge(*filled(key))
                    ps = bank_of(key)
                    V.tensor_tensor(chp[:, j, 2:2 + TP], ps[:, 0:TP], scc[:, j % 2, 0:TP], ALU.mult)
                    V.tensor_tensor(chp[:, j, 2 + TP:].rearrange("p (b k) -> p b k", b=NB)[:, :, 2:],
                                    ps[:, TP:T].rearrange("p (b k) -> p b k", b=NB),
                                    scc[:, j % 2, TP:T].rearrange("p (b k) -> p b k", b=NB), ALU.mult)\
                        .then_inc(free(key), 1)

                dve.wait_ge(S["st_in"], 32 * (l + 1))
                V.memset(xbcp[:, :, 0:3], 0.0)
                V.memset(chp[:, :, 0:2], 0.0)
                for j in range(6):
                    V.tensor_copy(xbcp[:, j, 3 + TP:].rearrange("p (b k) -> p b k", b=NB)[:, :, 0:3],
                                  cv_st[:, j, :].rearrange("p (b k) -> p b k", b=NB))
                for j in range(4):
                    last = V.tensor_copy(chp[:, j, 2 + TP:].rearrange("p (b k) -> p b k", b=NB)[:, :, 0:2],
                                         sc_st[:, j, :].rearrange("p (b k) -> p b k", b=NB))
                link(last)

                for n in range(13):
                    if n < 12:
                        unit_softmax(n)
                        if UNIT_REST[n] is not None:
                            rest(UNIT_REST[n])
                    if n > 0:
                        unit_out(n - 1)
                signal("otok_ready")
                link(V.memset(qbd, 0.0))
                for g in range(NKV):
                    gd = slice(HD * g, HD * g + HD)
                    last = V.tensor_copy(qbd[gd, :, 16 * g:16 * g + 16].rearrange("p b (r t) -> p b r t", r=GRP),
                                         qkv[gd, 0:GRP, TP:T].rearrange("p r (b t) -> p b r t", b=NB))
                last.then_inc(S["qbd_ready"], 1)
                for hf in range(2):
                    it = 2 * l + hf
                    dve.wait_ge(*filled(("Sc", l, hf)))
                    ps = bank_of(("Sc", l, hf))
                    V.tensor_scalar(S_c[:, 0:NCS], ps[:, 0:NCS], HD ** -0.5, None, ALU.mult).then_inc(free(("Sc", l, hf)), 1)
                    dve.wait_ge(*released(("Sc", l, hf)))
                    V.tensor_reduce(smx[:, 0:1], S_c[:, 0:NCS], AX.X, ALU.max, negate=True).then_inc(S["scmax"], 1)
                    rest(12 + 5 * hf)
                    dve.wait_ge(S["sc_exp"], it + 1)
                    link(V.reciprocal(srs[:, 0:1], ssm[:, 0:1]))
                    V.tensor_scalar(S_c[:, 0:NCS], S_c[:, 0:NCS], srs[:, 0:1], None, ALU.mult).then_inc(S["pc_ready"], 1)
                    dve.wait_ge(*filled(("imp", l, hf)))
                    ps = bank_of(("imp", l, hf))
                    V.tensor_reduce(imp, ps[:, 4:4 + 4 * NMID].rearrange("p (b k) -> p b k", k=4), AX.X, ALU.add)\
                        .then_inc(free(("imp", l, hf)), 1)
                    dve.wait_ge(*released(("imp", l, hf)))
                    link(V.tensor_reduce(m1[:, 0:1], imp, AX.X, ALU.min))
                    link(V.tensor_scalar(tie, imp, m1[:, 0:1], None, ALU.is_equal))
                    link(V.tensor_tensor(tie, tie, C("blk_idx"), ALU.mult))
                    link(V.tensor_reduce(m1[:, 1:2], tie, AX.X, ALU.max))
                    link(V.tensor_scalar(drop, C("blk_idx"), m1[:, 1:2], NEG, ALU.is_equal, ALU.mult))
                    dve.wait_ge(*filled(("Oc", l, hf)))
                    ps = bank_of(("Oc", l, hf))
                    V.tensor_copy(orow[:, 0, :], ps[:, 0:P]).then_inc(free(("Oc", l, hf)), 1)
                    for o, br, ncol in ((1, 2, WIN), (2, 1, PAST)):
                        for c in range(ncol // 512):
                            dve.wait_ge(*filled(("Ss", l, hf, br, c)))
                            ps = bank_of(("Ss", l, hf, br, c))
                            V.tensor_scalar(S_s[:, 512 * c:512 * c + 512], ps[:, 0:512], HD ** -0.5, None, ALU.mult)\
                                .then_inc(free(("Ss", l, hf, br, c)), 1)
                        dve.wait_ge(*filled(("Sn", l, hf, br)))
                        ps = bank_of(("Sn", l, hf, br))
                        V.scalar_tensor_tensor(S_s[:, ncol:ncol + TS], ps[:, 0:TS], HD ** -0.5,
                                               C("new_mask")[:, hf * TS:(hf + 1) * TS], ALU.mult, ALU.add)\
                            .then_inc(free(("Sn", l, hf, br)), 1)
                        dve.wait_ge(*released(("Sn", l, hf, br)))
                        if br == 1:
                            mid = S_s[:, SEL:SEL * (NMID + 1)].rearrange("p (b k) -> p b k", k=SEL)
                            link(V.tensor_tensor(mid, mid, bc(drop, 2, SEL), ALU.add))
                        else:
                            link(V.tensor_tensor(S_s[:, 0:TD], S_s[:, 0:TD], C("win_mask"), ALU.add))
                        V.tensor_reduce(smx[:, br:br + 1], S_s[:, 0:ncol + TS], AX.X, ALU.max, negate=True).then_inc(S["ssmax"], 1)
                        rest(12 + 5 * hf + 2 * o - 1)
                        rest(12 + 5 * hf + 2 * o)
                        dve.wait_ge(S["ss_exp"], 2 * it + o)
                        link(V.reciprocal(srs[:, br:br + 1], ssm[:, br:br + 1]))
                        dve.wait_ge(*filled(("Os", l, hf, br)))
                        ps = bank_of(("Os", l, hf, br))
                        V.tensor_scalar(orow[:, br, :], ps[:, 0:P], srs[:, br:br + 1], None, ALU.mult)\
                            .then_inc(free(("Os", l, hf, br)), 1)
                        dve.wait_ge(*released(("Os", l, hf, br)))
                    signal("orow_ready")
                    dve.wait_ge(*filled(("oT", l, hf)))
                    ps = bank_of(("oT", l, hf))
                    for g in range(NKV):
                        gd = slice(HD * g, HD * g + HD)
                        acc = [osam[gd, k, :].rearrange("p (b r t) -> p b r t", b=HALF, r=GRP) for k in range(2)]
                        for br in range(3):
                            o = ps[gd, br * P:(br + 1) * P].rearrange("p (b q) -> p b q", b=HALF)[:, :, 16 * g:16 * g + 16]\
                                .rearrange("p b (r t) -> p b r t", r=GRP)
                            gt = gB[gd, br, :, 16 * hf:16 * hf + 16].rearrange("p r (b t) -> p b r t", b=HALF)
                            last = V.tensor_tensor(acc[0 if br == 0 else 1], o, gt, ALU.mult)
                            if br == 2 and g == NKV - 1:
                                last.then_inc(free(("oT", l, hf)), 1)
                                dve.wait_ge(*released(("oT", l, hf)))
                            else:
                                link(last)
                            if br == 1:
                                link(V.tensor_tensor(acc[0], acc[0], acc[1], ALU.add))
                            if br == 2:
                                t0 = TP + 16 * hf
                                link(V.tensor_tensor(oN[gd, :, t0:t0 + 16].rearrange("p r (b t) -> p b r t", b=HALF),
                                                     acc[0], acc[1], ALU.add))

                dve.wait_ge(S["kv_done"], 16 * (l + 1))
                V.tensor_tensor(sp_v, small[:, :, 24:32], bc(PR(l, "dt_bias", 0, NH), 1, 3), ALU.add).then_inc(S["attn_done"], 1)
                dve.wait_ge(S["attn_done"], l + 1)
                link(V.tensor_scalar(sp_e, sp_v, -1.0, None, ALU.mult))
                V.tensor_tensor(sp_e, sp_e, sp_v, ALU.max).then_inc(S["spa"], 1)
                dve.wait_ge(S["sp_exp"], l + 1)
                link(V.tensor_scalar(sp_z, sp_e, 2.0, None, ALU.add))
                link(V.reciprocal(sp_z, sp_z))
                link(V.tensor_tensor(sp_z, sp_z, sp_e, ALU.mult))
                link(V.tensor_tensor(sp_q, sp_z, sp_z, ALU.mult))
                link(V.tensor_scalar(sp_p, sp_q, 1.0 / 13, None, ALU.mult))
                for k in (11, 9, 7, 5, 3):
                    link(V.scalar_tensor_tensor(sp_p, sp_p, 1.0 / k, sp_q, ALU.add, ALU.mult))
                link(V.scalar_tensor_tensor(sp_p, sp_p, 1.0, sp_z, ALU.add, ALU.mult))
                link(V.tensor_scalar(sp_v, sp_v, 0.0, None, ALU.max))
                link(V.scalar_tensor_tensor(dt, sp_p, 2.0, sp_v, ALU.mult, ALU.add))
                dve.wait_ge(S["ea_ready"], l + 1)
                link(V.scalar_tensor_tensor(dta, dt, -1.0, bc(ea, 1, 3), ALU.mult, ALU.mult))

                dve.wait_ge(*released(("rest", l, NREST - 1)))
                signal("cols_ready")
                def conv(src, dst, pad, width, tiles, w, bias):
                    for k in range(width):
                        for j in range(tiles):
                            pin, pout = src[:, j, k:k + TP], dst[:, j, 0:TP]
                            sin_ = src[:, j, pad + TP:].rearrange("p (b k) -> p b k", b=NB)[:, :, k:k + TD]
                            sout = dst[:, j, TP:T].rearrange("p (b k) -> p b k", b=NB)
                            wk = PR(l, w, k * tiles + j)
                            for a, o in ((pin, pout), (sin_, sout)):
                                if k == 0:
                                    last = V.tensor_scalar(o, a, wk, None, ALU.mult)
                                else:
                                    last = V.scalar_tensor_tensor(o, a, wk, o, ALU.mult, ALU.add)
                        link(last)
                    if bias:
                        for j in range(tiles):
                            last = V.tensor_scalar(dst[:, j, :], dst[:, j, :], PR(l, bias, j), None, ALU.add)
                        link(last)

                def merge(q):
                    for u in GROUPS[q]:
                        m = MERGE[u][1]
                        gate = gate_buffer(u)
                        dve.wait_ge(*released(("gate", l, u)))
                        dve.wait_ge(*filled(("proj", l, u)))
                        ps = bank_of(("proj", l, u))
                        dst = merged[:, m, :] if u < KD else gate
                        V.tensor_tensor(dst, ps[:, 0:T], gate, ALU.mult).then_inc(free(("proj", l, u)), 1)
                        if u >= KD:
                            dve.wait_ge(*released(("proj", l, u)))
                            if u < 2 * KD:
                                dve.wait_ge(*released(("proj", l, u - KD)))
                            else:
                                dve.wait_ge(S["part_sum"], 2 * KD * l + u - 2 * KD + 1)
                            V.tensor_tensor(merged[:, m, :], merged[:, m, :], gate, ALU.add).then_inc(S["part_sum"], 1)

                conv(xbcp, xbcc, 3, 4, 6, "conv_w", "conv_b")
                signal("xbcc_raw")
                merge(0)
                merge(1)
                conv(chp, sconv, 2, 3, 4, "sc_w", None)
                V.tensor_tensor(oC, oC, sconv, ALU.mult).then_inc(S["oC_ready"], 1)
                dve.wait_ge(S["oC_ready"], l + 1)
                dve.wait_ge(S["cc_done"], 320 * (l + 1))
                merge(2)

                for c in range(NCHUNK):
                    t0, n = TILES[c]
                    cc = NCHUNK * l + c
                    w = NH * n
                    d3 = decay[0:n, 0:w].rearrange("p (h t) -> p h t", h=NH)
                    up = C("upto0") if c < 2 else C("upto2", TS)
                    mk = C("decay_mask0") if c < 2 else C("decay_mask2", TS)
                    V.tensor_tensor(d3, bc(up, 1, NH), bc(dta[0:n, c, :], 2, n), ALU.mult).then_inc(S["dD_ready"], 1)
                    if c > 0:
                        merge(2 * c + 2)
                    dve.wait_ge(*filled(("ac", cc)))
                    ps = bank_of(("ac", cc))
                    V.tensor_copy(acs[0:n, :], ps[0:n, 0:2 * NH]).then_inc(free(("ac", cc)), 1)
                    dve.wait_ge(*released(("ac", cc)))
                    V.tensor_tensor(tail[0:n, :], acs[0:n, NH:], acs[0:n, 0:NH], ALU.subtract).then_inc(S["tl_sub"], 1)
                    for part in range(2 if c < 2 else 1):
                        dve.wait_ge(*filled(("acB", cc, part)))
                        ps = bank_of(("acB", cc, part))
                        w2 = min(512, w)
                        V.tensor_copy(eB[:, part * 512:part * 512 + w2], ps[:, 0:w2]).then_inc(free(("acB", cc, part)), 1)
                    dve.wait_ge(*released(("acB", cc, 1 if c < 2 else 0)))
                    link(V.tensor_tensor(d3, eB[0:n, 0:w].rearrange("p (h t) -> p h t", h=NH), bc(acs[0:n, 0:NH], 2, n), ALU.subtract))
                    V.tensor_tensor(d3, d3, bc(mk, 1, NH), ALU.add).then_inc(S["seg_ready"], 1)
                    dve.wait_ge(*filled(("xtok", cc)))
                    ps = bank_of(("xtok", cc))
                    V.tensor_tensor(xdt[0:n, :].rearrange("p (h d) -> p h d", h=NH), ps[0:n, 0:512].rearrange("p (h d) -> p h d", h=NH),
                                    bc(dt[0:n, c, :], 2, HD), ALU.mult).then_inc(free(("xtok", cc)), 1)
                    dve.wait_ge(*released(("xtok", cc)))
                    dve.wait_ge(S["tl_ready"], cc + 1)
                    V.tensor_tensor(xtl[0:n, :].rearrange("p (h d) -> p h d", h=NH), xdt[0:n, :].rearrange("p (h d) -> p h d", h=NH),
                                    bc(tail[0:n, :], 2, HD), ALU.mult).then_inc(S["xdt_ready"], 1)
                    dve.wait_ge(S["dec_exp"], cc + 1)
                    for g in range(NKV):
                        dve.wait_ge(*filled(("CB", cc, g)))
                        ps = bank_of(("CB", cc, g))
                        V.tensor_tensor(d3[:, 4 * g:4 * g + 4, :], d3[:, 4 * g:4 * g + 4, :],
                                        bc(ps[0:n, 0:n], 1, GRP), ALU.mult).then_inc(free(("CB", cc, g)), 1)
                    dve.wait_ge(*released(("CB", cc, 1)))
                    signal("dec_ready")
                    merge(2 * c + 3)
                    dve.wait_ge(S["eb_ready"], cc + 1)
                    if c == 2:
                        dve.wait_ge(S["hs_in"], 16 * (l + 1))
                    if c > 0:
                        for g in range(NKV):
                            gd = slice(HD * g, HD * g + HD)
                            last = V.tensor_tensor(cp[gd, 0:GRP * n].rearrange("p (h t) -> p h t", h=GRP),
                                                   bc(xbcc[gd, 5, t0:t0 + n], 1, GRP),
                                                   eB[gd, g * GRP * n:(g + 1) * GRP * n].rearrange("p (h t) -> p h t", h=GRP), ALU.mult)
                        last.then_inc(S["cp_ready"], 1)
                    if c == 2:
                        dve.wait_ge(S["btok_ready"], cc + 1)
                        V.tensor_tensor(bm[0:n, :, :], bc(btok[0:n, :], 1, NB), bc(C("in_batch", TS), 2, P), ALU.mult)\
                            .then_inc(S["bm_ready"], 1)
                    dve.wait_ge(S["xbcc_ready"], l + 1)
                    for g in range(NKV):
                        dve.wait_ge(*filled(("y", cc, g)))
                        ps = bank_of(("y", cc, g))
                        for j in range(2):
                            last = V.scalar_tensor_tensor(xbcc[:, 2 * g + j, t0:t0 + n], xbcc[:, 2 * g + j, t0:t0 + n],
                                                          PR(l, "ssm_d", 2 * g + j), ps[:, j * n:(j + 1) * n], ALU.mult, ALU.add)
                        last.then_inc(free(("y", cc, g)), 1)
                        dve.wait_ge(*released(("y", cc, g)))
                    if c < 2:
                        dve.wait_ge(*filled(("hd", cc)))
                        ps = bank_of(("hd", cc))
                        for g in range(NKV):
                            gd = slice(HD * g, HD * g + HD)
                            new = ps[gd, 0:256].rearrange("p (h d) -> p h d", h=GRP)
                            if c == 0:
                                last = V.tensor_copy(hT[gd, :, :], new)
                            else:
                                e3 = eB[gd, 0:w].rearrange("p (h t) -> p h t", h=NH)[:, 4 * g:4 * g + 4, n - 1]
                                link(V.tensor_tensor(hT[gd, :, :], hT[gd, :, :], bc(e3, 2, HD), ALU.mult))
                                last = V.tensor_tensor(hT[gd, :, :], hT[gd, :, :], new, ALU.add)
                        last.then_inc(free(("hd", cc)), 1)
                        dve.wait_ge(*released(("hd", cc)))
                        signal("h_ready")
                    else:
                        dve.wait_ge(*filled(("hsd", l, 0)))
                        for g in range(NKV):
                            gd = slice(HD * g, HD * g + HD)
                            e4 = eB[gd, 0:w].rearrange("p (h b t) -> p h b t", h=NH, b=NB)[:, 4 * g:4 * g + 4, :, TD - 1]
                            last = V.tensor_tensor(hs[gd, :, :, :], hs[gd, :, :, :],
                                                   bc(e4.rearrange("p h b -> p b h"), 3, HD), ALU.mult)
                        link(last)
                        for b2 in range(NB // 2):
                            dve.wait_ge(*filled(("hsd", l, b2)))
                            ps = bank_of(("hsd", l, b2))
                            hv = hs[:, 2 * b2:2 * b2 + 2, :, :]
                            V.tensor_tensor(hv, hv, ps[:, 0:512].rearrange("p (b h d) -> p b h d", b=2, h=GRP), ALU.add)\
                                .then_inc(free(("hsd", l, b2)), 1)
                        dve.wait_ge(*released(("hsd", l, 3)))
                V.tensor_tensor(oS, oS, xbcc[:, 0:4, :], ALU.mult).then_inc(S["y_ready"], 1)
                dve.wait_ge(*released(("yss", l)))
                link(V.reciprocal(std[:, :], std[:, :]))
                for j in range(4):
                    last = V.scalar_tensor_tensor(oS[:, j, :], oS[:, j, :], PR(l, "ssm_norm", j), std[:, :], ALU.mult, ALU.mult)
                last.then_inc(S["oS_ready"], 1)
                merge(8)
                merge(9)
                dve.wait_ge(S["part_sum"], 2 * KD * (l + 1))
                dve.wait_ge(S["hs_done"], 16 * (l + 1))
                dve.wait_ge(S["hp_done"], 16 * (l + 1))
                signal("merged_ready")
                for m in range(KD):
                    dve.wait_ge(*filled(("o", l, m)))
                    ps = bank_of(("o", l, m))
                    V.tensor_tensor(xT[:, m, :], xT[:, m, :], ps[:, 0:T], ALU.add).then_inc(free(("o", l, m)), 1)
                dve.wait_ge(*released(("o", l, KD - 1)))
                rms(l, 1, "norm_ffn")
                if l == 0:
                    for f in range(NFD):
                        g_u = use_of[("fg", f)]
                        dve.wait_ge(bank_free[g_u % 8], g_u // 8 + 1)
                        dve.wait_ge(*filled(("fu", f)))
                        ps = bank_of(("fu", f))
                        V.tensor_tensor(h[:, f, :], gs_[:, f % 2, :], ps[:, 0:T], ALU.mult).then_inc(free(("fu", f)), 1)
                    for m in range(KD):
                        dve.wait_ge(*filled(("fd", m)))
                        ps = bank_of(("fd", m))
                        V.tensor_tensor(xT[:, m, :], xT[:, m, :], ps[:, 0:T], ALU.add).then_inc(free(("fd", m)), 1)
                    dve.wait_ge(*released(("fd", 7)))

            link(V.memset(rl, 0.0))
            dve.wait_ge(*filled(("router",)))
            ps = bank_of(("router",))
            V.tensor_copy(rl[0:TS, 2, :], ps[0:TS, 16:24])
            V.tensor_copy(rl[:, 0:2, :], ps[:, 0:16].rearrange("p (a b) -> p a b", a=2)).then_inc(free(("router",)), 1)
            dve.wait_ge(*released(("router",)))
            prefer = bc(C("exp_rank"), 1, 3)

            def best(src, sel, m):
                link(V.tensor_reduce(m, src, AX.X, ALU.max))
                link(V.tensor_tensor(sel, src, m.to_broadcast([P, 3, NE]), ALU.is_equal))
                link(V.tensor_tensor(sel, sel, prefer, ALU.mult))
                link(V.tensor_reduce(rg1, sel, AX.X, ALU.max))
                link(V.tensor_tensor(sel, prefer, rg1.to_broadcast([P, 3, NE]), ALU.is_equal))

            best(rl, rs1, rm1)
            link(V.scalar_tensor_tensor(rl2, rs1, NEG, rl, ALU.mult, ALU.add))
            best(rl2, rs2, rm2)
            V.tensor_tensor(mask, rs1, rs2, ALU.add).then_inc(S["cnt_ready"], 1)
            V.tensor_tensor(re, rm2, rm1, ALU.subtract).then_inc(S["re_sub"], 1)
            dve.wait_ge(S["re_exp"], 1)
            link(V.tensor_scalar(rg1, re, 1.0, None, ALU.add))
            link(V.reciprocal(rg1, rg1))
            link(V.tensor_tensor(rg2, re, rg1, ALU.mult))
            link(V.tensor_tensor(rt, rs1, rg1.to_broadcast([P, 3, NE]), ALU.mult))
            link(V.tensor_tensor(rs2, rs2, rg2.to_broadcast([P, 3, NE]), ALU.mult))
            link(V.tensor_tensor(rt, rt, rs2, ALU.add))
            dve.wait_ge(*filled(("cnt",)))
            ps = bank_of(("cnt",))
            link(V.tensor_copy(cnt, ps[:, 0:NE]))
            V.tensor_copy(rank[0:TS, 2, :], ps[0:TS, 3 * NE:4 * NE])
            V.tensor_copy(rank[:, 0:2, :], ps[:, NE:3 * NE].rearrange("p (a b) -> p a b", a=2)).then_inc(free(("cnt",)), 1)
            dve.wait_ge(*released(("cnt",)))
            link(V.scalar_tensor_tensor(rank, rank, 1000.0, mask, ALU.add, ALU.mult))
            link(V.tensor_scalar(rank, rank, -1000.0, None, ALU.add))
            link(V.tensor_scalar(runs, cnt, float(CAP), 1.0, ALU.is_gt, ALU.add))
            link(V.tensor_scalar(en1, cnt, 2.0 * CAP, None, ALU.is_gt))
            link(V.tensor_tensor(runs, runs, en1, ALU.add))
            src = runs
            for step, dst in ((1, en1), (2, en2), (4, en3)):
                V.tensor_copy(dst[:, 0:step], src[:, 0:step])
                link(V.tensor_tensor(dst[:, step:NE], src[:, step:NE], src[:, 0:NE - step], ALU.add))
                src = dst
            link(V.tensor_tensor(le, bc(en3, 1, 16), bc(C("iota")[:, 0:16], 2, NE), ALU.is_le))
            link(V.tensor_reduce(tabf[:, 0:16], le, AX.X, ALU.add))
            link(V.tensor_scalar(tabf[:, 0:16], tabf[:, 0:16], NE - 1.0, None, ALU.min))
            link(V.tensor_tensor(lei, le, bc(runs, 1, 16), ALU.mult))
            link(V.tensor_reduce(tabf[:, 16:32], lei, AX.X, ALU.add))
            link(V.tensor_tensor(tabf[:, 16:32], C("iota")[:, 0:16], tabf[:, 16:32], ALU.subtract))
            link(V.tensor_scalar(tabf[:, 16:32], tabf[:, 16:32], float(CAP), 2.0 * CAP, ALU.mult, ALU.min))
            V.tensor_copy(tabf[:, 32:33], en3[:, NE - 1:NE])
            link(V.memset(tabf[:, 33:48], 0.0))
            V.tensor_copy(passes[0:1, :], tabf[0:1, :]).then_inc(S["table_ready"], 1)
            dve.wait_ge(S["table_ready"], 1)

            def make_pick(i):
                ex = dve.value_load(passes[0:1, bass.ds(i, 1)], min_val=0, max_val=NE - 1)
                slot = dve.value_load(passes[0:1, bass.ds(i + 16, 1)], min_val=0, max_val=2 * CAP)
                for tt, (t0, n) in enumerate(TILES):
                    mine = rank[0:n, tt, bass.ds(ex, 1)]
                    slots = C("iota", n)[:, bass.ds(slot, CAP)]
                    V.tensor_scalar(pickw[0:n, tt, :], slots, mine, rt[0:n, tt, bass.ds(ex, 1)], ALU.is_equal, ALU.mult)
                    last = V.tensor_scalar(pick[0:n, tt, :], slots, mine, None, ALU.is_equal)
                last.then_inc(S["pick_ready"], 1)

            V.memset(yT, 0.0)
            link(V.memset(pickw, 0.0))
            V.memset(spread, 0.0).then_inc(S["zero_ready"], 1)
            make_pick(0)
            n_pass = dve.value_load(passes[0:1, 32:33], min_val=NE, max_val=MAX_PASSES)

            def add_scatter(key, it):
                for m in range(KD):
                    dve.wait_ge(*filled((key, m), it))
                    ps = bank_of((key, m))
                    last = V.tensor_tensor(xT[:, m, :], xT[:, m, :], ps[:, 0:T], ALU.add)
                    last.then_inc(free((key, m)), 1)

            with dve.Fori(0, n_pass) as i:
                def up(q):
                    dve.wait_ge(S["silu_ready"], i * (NFE // 2) + q + 1)
                    dve.wait_ge(*filled(("gu", q), i))
                    ps = bank_of(("gu", q))
                    V.tensor_tensor(he[:, 2 * q:2 * q + 2, :], sg[:, q % 2, :].rearrange("p (a b) -> p a b", a=2),
                                    ps[:, 2 * CAP:4 * CAP].rearrange("p (a b) -> p a b", a=2), ALU.mult)\
                        .then_inc(free(("gu", q)), 1)

                for q in range(4):
                    up(q)
                add_scatter("sc", i)
                dve.wait_ge(*filled(("sp", 2), i))
                make_pick(i + 1)
                for q in range(4, NFE // 2):
                    up(q)
            add_scatter("sc_last", n_pass - 1)
            signal("x_ready")


def blocks(w):
    K, N = w.shape
    return w.reshape(K // P, P, N // P, P).transpose(2, 0, 1, 3)


def head_tiles(cols):
    return cols.reshape(NKV, GRP, HD).transpose(1, 0, 2).reshape(-1)


def weight_stream(a):
    out = np.empty((N_SLOTS * BPS, P, P), np.float32)
    at = 0

    def put(b):
        nonlocal at
        b = b.reshape(-1, P, P)
        out[at:at + len(b)] = b
        at += len(b)

    for l in range(DEPTH):
        w = a["w_in"][l]
        q = w[:, 0:512][:, head_tiles(np.arange(512))]
        kv = w[:, 512:1280].reshape(D, 3, 2, P)
        put(blocks(q))
        put(blocks(kv[:, :, 0].reshape(D, 3 * P)))
        put(blocks(kv[:, :, 1].reshape(D, 3 * P)))
        cm = np.zeros((2, 32, P, P), np.float32)
        for g in range(NKV):
            cm[:, :, g * HD:(g + 1) * HD, g * HD:(g + 1) * HD] = a["w_cmp"][l]
        kinds = {"x": w[:, 1816:2584], "z": w[:, 1304:1816], "c": w[:, 3104:3616], "h": w[:, 3616:4128], "b": w[:, 2592:3104]}
        rest = [blocks(kinds[kind][:, j * P:(j + 1) * P]) for kind, j in REST]
        put(np.stack(rest[:EARLY]))
        put(cm)
        put(np.stack(rest[EARLY:EARLY + CMP1_UNIT]))
        put(cm)
        put(np.stack(rest[EARLY + CMP1_UNIT:]))
        mg = blocks(w[:, 4128:]).reshape(3, KD, KD, P, P)
        wb = a["w_branch"][l]
        br = np.stack([blocks(wb[0][head_tiles(np.arange(512))]), blocks(wb[1]), blocks(wb[2])])
        for group in GROUPS:
            for u in group:
                put(mg[MERGE[u][0], MERGE[u][1]])
            for u in group:
                put(br[MERGE[u][0], MERGE[u][1]])
        put(blocks(a["w_out"][l]))
        if l == 0:
            put(np.stack([blocks(a["ffn_w_gate"][0]), blocks(a["ffn_w_up"][0])], 1))
            put(blocks(a["ffn_w_down"][0]))
    for e in range(NE):
        put(np.stack([blocks(a["moe_w_gate"][0, e]), blocks(a["moe_w_up"][0, e])], 1))
        put(blocks(a["moe_w_down"][0, e]))
    assert at == len(out)
    return np.ascontiguousarray(out.reshape(N_SLOTS, BPS, P, P).transpose(0, 2, 1, 3)).reshape(N_SLOTS, P, SLOTF)


def feature_cols(v, n):
    return v.reshape(-1, P).T.reshape(P, -1)


def layer_params(a):
    out = np.zeros((P, DEPTH, N_PAR), np.float32)

    def put(l, name, v):
        at, n = PAR_AT[name]
        out[:, l, at:at + n] = v.reshape(P, n)

    for l in range(DEPTH):
        put(l, "norm_mix", feature_cols(a["norm_mix"][l], KD))
        put(l, "norm_ffn", feature_cols(a["norm_ffn"][l], KD))
        qk = np.concatenate([np.tile(a["q_norm"][l], (4, 2)), np.tile(a["k_norm"][l], (1, 2))])
        put(l, "qk_norm", np.ascontiguousarray(qk.T))
        put(l, "conv_w", feature_cols(a["ssm_conv_w"][l], 6))
        put(l, "conv_b", feature_cols(a["ssm_conv_b"][l], 6))
        put(l, "ssm_d", feature_cols(np.repeat(a["ssm_d"][l], HD), 4))
        put(l, "ssm_norm", feature_cols(a["ssm_norm"][l], 4))
        put(l, "sc_w", feature_cols(a["sc_conv_w"][l], 4))
        put(l, "dt_bias", np.tile(a["ssm_dt_bias"][l], (P, 1)))
        put(l, "a_log", np.tile(a["ssm_a_log"][l], (P, 1)))
        w = a["w_in"][l]
        sm = np.concatenate([w[:, 1280:1304], w[:, 2584:2592]], 1)
        put(l, "w_small", np.ascontiguousarray(sm.reshape(KD, P, 32).transpose(1, 0, 2)))
        if l == 1:
            put(l, "router", np.ascontiguousarray(a["moe_router"][0].reshape(KD, P, NE).transpose(1, 0, 2)))
    return out.reshape(P, -1)


def kernel(**inputs):
    import concourse.bacc as bacc
    from concourse.bass_utils import run_bass_kernel_spmd

    a = {k: np.asarray(v) for k, v in inputs.items()}
    nc = bacc.Bacc("TRN2", target_bir_lowering=False, num_devices=1)
    arrays, args = {}, []

    def ext(name, arr):
        arr = np.ascontiguousarray(arr)
        arrays["in_" + name] = arr
        args.append(nc.dram_tensor("in_" + name, arr.shape, mybir.dt.from_np(arr.dtype), kind="ExternalInput").ap())

    def out(name, shape):
        args.append(nc.dram_tensor("out_" + name, shape, mybir.dt.float32, kind="ExternalOutput").ap())

    x = np.concatenate([a["x_prompt"].reshape(TP, D), a["x_sample"].reshape(TS, D)])
    ext("xT", x.reshape(T, KD, P).transpose(2, 1, 0).reshape(P, -1))
    ext("consts", np.concatenate([np.ascontiguousarray(v) for v in CONST.values()], 1))
    ext("params", layer_params(a))
    ext("wstream", weight_stream(a))
    ext("page_table", a["page_table"].reshape(1, -1))
    pg = a["cache_nsa_pages"]
    n_pool = pg.shape[1]
    pg = pg.reshape(DEPTH * n_pool, PAGE, 4, P)
    ext("cmp_pages", pg[:, :, 0:2].transpose(0, 3, 2, 1))
    ext("slc_pages", np.stack([pg[:, :, 2].transpose(0, 2, 1), pg[:, :, 3]], 2).reshape(DEPTH * n_pool, P, 2 * P))
    win = a["cache_nsa_window"].reshape(DEPTH, NB, WIN, 2, P)
    ext("win_kT", win[:, :, :, 0].transpose(0, 3, 1, 2))
    ext("win_v", win[:, :, :, 1].reshape(DEPTH, NB, 4, P, P).transpose(0, 1, 3, 2, 4))
    ext("win_rows", win.reshape(DEPTH, NB, WIN, 2 * P))
    st = a["state_ssm"].reshape(DEPTH, NB, NKV, GRP, HD, SSMN).transpose(0, 2, 5, 1, 3, 4)
    ext("ssm_in", st.reshape(DEPTH, P, NB, GRP, HD))
    ext("conv_in", a["state_ssm_conv"].reshape(DEPTH, NB, 3, 6, P).transpose(0, 4, 3, 1, 2).reshape(DEPTH, P, 6, NB * 3))
    ext("sc_in", a["state_shortconv"].reshape(DEPTH, NB, 2, 4, P).transpose(0, 4, 3, 1, 2).reshape(DEPTH, P, 4, NB * 2))
    out("y", (P, KD * T))
    out("kv", (DEPTH, P, 6, T))
    out("win_keep", (DEPTH, NB, WIN - TD, 2 * P))
    out("ssm_p", (DEPTH, P, GRP, HD))
    out("ssm_s", (DEPTH, P, NB, GRP, HD))
    out("conv_last", (DEPTH, P, 6, 3 + NB * 3))
    out("sc_last", (DEPTH, P, 4, 2 + NB * 2))
    build(nc, *args)
    res = run_bass_kernel_spmd(nc, [arrays], core_ids=[0]).results[0]
    r = {k[4:]: res[k] for k in res if k.startswith("out_")}

    y = r["y"].reshape(P, KD, T).transpose(2, 1, 0).reshape(T, D)
    kv = r["kv"].reshape(DEPTH, NKV, HD, 2, 3, T).transpose(0, 5, 4, 3, 1, 2)
    rows = kv[:, :, 0:2].reshape(DEPTH, T, 4, NKV, HD)
    wkv = kv[:, :, 2]
    nsa_p = np.ascontiguousarray(rows[:, :TP]).reshape(DEPTH, 1, TP, 4, NKV, HD)
    nsa_s = np.ascontiguousarray(rows[:, TP:]).reshape(DEPTH, NB, TD, 4, NKV, HD)
    win_p = np.ascontiguousarray(wkv[:, :TP]).reshape(DEPTH, 1, TP, 2, NKV, HD)
    win_s = np.concatenate([r["win_keep"].reshape(DEPTH, NB, WIN - TD, 2, NKV, HD),
                            wkv[:, TP:].reshape(DEPTH, NB, TD, 2, NKV, HD)], 2)
    ssm_p = r["ssm_p"].reshape(DEPTH, NKV, SSMN, GRP, HD).transpose(0, 1, 3, 4, 2).reshape(DEPTH, 1, NH, HD, SSMN)
    ssm_s = r["ssm_s"].reshape(DEPTH, NKV, SSMN, NB, GRP, HD).transpose(0, 3, 1, 4, 5, 2).reshape(DEPTH, NB, NH, HD, SSMN)
    cl = r["conv_last"]
    conv_p = cl[:, :, :, 0:3].transpose(0, 3, 2, 1).reshape(DEPTH, 1, 3, XBC)
    conv_s = cl[:, :, :, 3:].reshape(DEPTH, P, 6, NB, 3).transpose(0, 3, 4, 2, 1).reshape(DEPTH, NB, 3, XBC)
    sl = r["sc_last"]
    sc_p = sl[:, :, :, 0:2].transpose(0, 3, 2, 1).reshape(DEPTH, 1, 2, SC)
    sc_s = sl[:, :, :, 2:].reshape(DEPTH, P, 4, NB, 2).transpose(0, 3, 4, 2, 1).reshape(DEPTH, NB, 2, SC)
    return tuple(np.ascontiguousarray(v) for v in (
        y[:TP].reshape(1, TP, D), y[TP:].reshape(NB, TD, D), nsa_p, nsa_s, win_p, win_s, ssm_p, ssm_s,
        conv_p, conv_s, sc_p, sc_s))
```
